# Optimizing a Trainium2 kernel written in Bass

```python
import math
import jax
import jax.numpy as jnp
from jax import lax
import numpy as np
import jax, jax.numpy as jnp

D_MODEL = 1024
BATCH = 1
SEQ = 512
DEPTH = 1

N_MIXERS = 4
MIX_WIDTH = 256
HEAD_DIM = 64
N_HEADS = 4
NORM_EPS = 1e-6
NEG_INF = -1e30

GDN_CONV = 4
GDN_CHUNK = 64

SG_CHUNK = 128
SG_GROUPS = 4
SG_GROUP_DIM = MIX_WIDTH // SG_GROUPS

RWKV_DECAY_RANK = 64
RWKV_A_RANK = 64
RWKV_GN_EPS = 64e-5
RW_WIDTH = 3 * MIX_WIDTH + RWKV_DECAY_RANK + RWKV_A_RANK

NSA_KV_DIM = HEAD_DIM
NSA_CMP_LEN = 32
NSA_CMP_STRIDE = 16
NSA_CMP_RATIO = NSA_CMP_LEN // NSA_CMP_STRIDE
NSA_CMP_HIDDEN = 64
NSA_SEL_BLOCK = 64
NSA_N_SEL = 8
NSA_FORCE_BONUS = 1e4
NSA_WINDOW = 256
NSA_Q_BLOCK = 128
NSA_SEL_Q_BLOCK = 64

IN_SPLITS = (
    3 * MIX_WIDTH,
    N_HEADS,
    N_HEADS,
    MIX_WIDTH,
    MIX_WIDTH,
    MIX_WIDTH,
    MIX_WIDTH,
    RW_WIDTH,
    MIX_WIDTH,
    MIX_WIDTH,
    6 * NSA_KV_DIM,
    3 * N_HEADS,
    MIX_WIDTH,
    N_MIXERS * D_MODEL,
)
IN_OFFSETS = tuple(sum(IN_SPLITS[: i + 1]) for i in range(len(IN_SPLITS) - 1))
D_IN = sum(IN_SPLITS)
ALIBI_SLOPES = tuple(2.0 ** (-8.0 * (h + 1) / N_HEADS) for h in range(N_HEADS))


def rmsnorm(x, gain, eps=NORM_EPS):
    x32 = x.astype(jnp.float32)
    y = x32 * lax.rsqrt(jnp.mean(x32 * x32, axis=-1, keepdims=True) + eps)
    return (y * gain.astype(jnp.float32)).astype(x.dtype)

def layernorm(x, gain, bias, eps):
    x32 = x.astype(jnp.float32)
    xc = x32 - jnp.mean(x32, axis=-1, keepdims=True)
    y = xc * lax.rsqrt(jnp.mean(xc * xc, axis=-1, keepdims=True) + eps)
    return (y * gain.astype(jnp.float32) + bias.astype(jnp.float32)).astype(x.dtype)

def l2norm(x, eps=1e-6):
    x32 = x.astype(jnp.float32)
    return (x32 * lax.rsqrt(jnp.sum(x32 * x32, axis=-1, keepdims=True) + eps)).astype(x.dtype)

def shift_prev(x):
    return jnp.pad(x, ((0, 0), (1, 0), (0, 0)))[:, :-1]

def causal_depthwise_conv(x, w):
    width, ch = w.shape
    return lax.conv_general_dilated(
        x, w[:, None, :].astype(x.dtype), window_strides=(1,),
        padding=((width - 1, 0),), dimension_numbers=('NWC', 'WIO', 'NWC'),
        feature_group_count=ch)

def masked_softmax(s, mask):
    p = jax.nn.softmax(jnp.where(mask, s, NEG_INF), axis=-1)
    return jnp.where(mask, p, 0.0)

def chunked_gated_delta_rule(q, k, v, g, beta):
    B, T, H, E = q.shape
    C = GDN_CHUNK
    N = T // C

    def chunks(t):
        t = t.reshape((B, N, C, H) + t.shape[3:])
        return jnp.moveaxis(t, (1, 3), (0, 2))

    q, k, v, g, beta = (chunks(t) for t in (q, k, v, g, beta))
    gc = jnp.cumsum(g, axis=-1)
    pos = jnp.arange(C)
    causal = pos[:, None] >= pos[None, :]
    strict = pos[:, None] > pos[None, :]
    decay = jnp.where(causal, jnp.exp(jnp.where(causal, gc[..., :, None] - gc[..., None, :], 0.0)), 0.0)
    kb = k * beta[..., None]
    a_mat = jnp.where(strict, jnp.einsum('nbhcd,nbhed->nbhce', kb, k) * decay, 0.0)
    eye = jnp.eye(C, dtype=q.dtype)
    t_inv = lax.linalg.triangular_solve(eye + a_mat, jnp.broadcast_to(eye, a_mat.shape),
                                        left_side=True, lower=True, unit_diagonal=True)
    u = t_inv @ (v * beta[..., None])
    w = t_inv @ (kb * jnp.exp(gc)[..., None])
    attn = jnp.einsum('nbhcd,nbhed->nbhce', q, k) * decay
    g_last = gc[..., -1]
    q_in = q * jnp.exp(gc)[..., None]
    k_out = k * jnp.exp(g_last[..., None] - gc)[..., None]

    def step(state, xs):
        u_n, w_n, attn_n, q_n, k_n, gl_n = xs
        v_new = u_n - w_n @ state
        o_n = q_n @ state + attn_n @ v_new
        state = state * jnp.exp(gl_n)[..., None, None] + jnp.swapaxes(k_n, -1, -2) @ v_new
        return state, o_n

    state0 = jnp.zeros((B, H, E, v.shape[-1]), q.dtype)
    _, o = lax.scan(step, state0, (u, w, attn, q_in, k_out, g_last))
    return jnp.moveaxis(o, (0, 2), (1, 3)).reshape(B, T, H, -1)

def gated_deltanet(qkv, a_logit, b_logit, z, conv_w, a_log, dt_bias, norm_w):
    B, T, _ = qkv.shape
    f32 = jnp.float32
    qkv = jax.nn.silu(causal_depthwise_conv(qkv, conv_w))
    q, k, v = jnp.split(qkv, 3, axis=-1)
    heads = lambda t: t.reshape(B, T, N_HEADS, HEAD_DIM).astype(f32)
    q = l2norm(heads(q)) * (HEAD_DIM ** -0.5)
    k = l2norm(heads(k))
    v = heads(v)
    beta = jax.nn.sigmoid(b_logit.astype(f32))
    g = -jnp.exp(a_log.astype(f32)) * jax.nn.softplus(a_logit.astype(f32) + dt_bias.astype(f32))
    o = chunked_gated_delta_rule(q, k, v, g, beta)
    o = rmsnorm(o, norm_w) * jax.nn.silu(heads(z))
    return o.reshape(B, T, MIX_WIDTH).astype(qkv.dtype)

def spatial_gating(u, v, z, ln_gain, ln_bias, w_s, b_s):
    B, T, _ = u.shape
    u = jax.nn.gelu(u)
    v = jax.nn.gelu(v).reshape(B, T, SG_GROUPS, SG_GROUP_DIM)
    v = layernorm(v, ln_gain.reshape(SG_GROUPS, SG_GROUP_DIM), ln_bias.reshape(SG_GROUPS, SG_GROUP_DIM), 1e-5)
    v = v.reshape(B, T // SG_CHUNK, SG_CHUNK, SG_GROUPS, SG_GROUP_DIM)
    tril = jnp.tril(jnp.ones((SG_CHUNK, SG_CHUNK), dtype=bool))
    w_c = jnp.where(tril, w_s, 0.0).astype(v.dtype)
    mixed = jnp.einsum('gts,bnsgc->bntgc', w_c, v) + b_s.T[:, :, None].astype(v.dtype)
    s = u * mixed.reshape(B, T, MIX_WIDTH)
    return s * jax.nn.silu(z)

def rwkv7_scan(r, w, k, v, kk, a):
    def step(S, xs):
        r_t, w_t, k_t, v_t, kk_t, a_t = xs
        sa = jnp.einsum('bhvk,bhk->bhv', S, -kk_t)
        S = (S * w_t[:, :, None, :] + sa[..., None] * (kk_t * a_t)[:, :, None, :]
             + v_t[..., None] * k_t[:, :, None, :])
        return S, jnp.einsum('bhvk,bhk->bhv', S, r_t)

    B, T, H, E = r.shape
    xs = tuple(jnp.moveaxis(t, 1, 0) for t in (r, w, k, v, kk, a))
    _, o = lax.scan(step, jnp.zeros((B, H, E, E), jnp.float32), xs)
    return jnp.moveaxis(o, 0, 1)

def rwkv7_time_mix(rw, z, mu, w_up, w0, a_up, a0, k_k, k_a, r_k, gn_gain, gn_bias):
    B, T, _ = rw.shape
    f32 = jnp.float32
    rw = (rw + mu * (shift_prev(rw) - rw)).astype(f32)
    r, k, v, wd, ad = jnp.split(
        rw, (MIX_WIDTH, 2 * MIX_WIDTH, 3 * MIX_WIDTH, 3 * MIX_WIDTH + RWKV_DECAY_RANK), axis=-1)
    w_log = -jax.nn.softplus(-(w0.astype(f32) + jnp.tanh(wd) @ w_up.astype(f32))) - 0.5
    decay = jnp.exp(-jnp.exp(w_log))
    a = jax.nn.sigmoid(a0.astype(f32) + ad @ a_up.astype(f32))
    heads = lambda t: t.reshape(B, T, N_HEADS, HEAD_DIM)
    kk = l2norm(heads(k * k_k.astype(f32)))
    k = k * (1.0 + (a - 1.0) * k_a.astype(f32))
    r_h, k_h, v_h = heads(r), heads(k), heads(v)
    o = rwkv7_scan(r_h, heads(decay), k_h, v_h, kk, heads(a))
    o = layernorm(o, gn_gain.reshape(N_HEADS, HEAD_DIM), gn_bias.reshape(N_HEADS, HEAD_DIM), RWKV_GN_EPS)
    o = o + jnp.sum(r_h * k_h * r_k.astype(f32), axis=-1, keepdims=True) * v_h
    return (o.reshape(B, T, MIX_WIDTH) * jax.nn.silu(z.astype(f32))).astype(z.dtype)

def compress_blocks(x, pos_emb, w1, w2):
    B, T, E = x.shape
    ns = T // NSA_CMP_STRIDE
    nc = ns - NSA_CMP_RATIO + 1
    c = x.reshape(B, ns, NSA_CMP_STRIDE, E)
    blocks = jnp.concatenate([c[:, j:j + nc] for j in range(NSA_CMP_RATIO)], axis=2)
    blocks = (blocks + pos_emb.astype(x.dtype)).reshape(B, nc, NSA_CMP_LEN * E)
    return jax.nn.gelu(blocks @ w1) @ w2

def nsa_compressed(q, k, v, pos_emb, w1, w2, slopes):
    B, T, H, E = q.shape
    kc = compress_blocks(k, pos_emb[0], w1[0], w2[0])
    vc = compress_blocks(v, pos_emb[1], w1[1], w2[1])
    nc = kc.shape[1]
    end = jnp.arange(nc) * NSA_CMP_STRIDE + NSA_CMP_LEN - 1
    dist = (jnp.arange(T)[:, None] - end[None, :]).astype(jnp.float32)
    s = (jnp.einsum('bthd,bnd->bhtn', q, kc).astype(jnp.float32) * (E ** -0.5)
         - slopes[:, None, None] * dist)
    p = masked_softmax(s, dist >= 0)
    return jnp.einsum('bhtn,bnd->bthd', p.astype(q.dtype), vc), p

def nsa_selected(q, k, v, p_cmp, slopes):
    B, T, H, E = q.shape
    nc = p_cmp.shape[-1]
    nsb = T // NSA_SEL_BLOCK
    n_sel = min(NSA_N_SEL, nsb)
    cs = np.arange(nc) * NSA_CMP_STRIDE
    bs = np.arange(nsb) * NSA_SEL_BLOCK
    inter = np.clip(np.minimum(cs[:, None] + NSA_CMP_LEN, bs[None, :] + NSA_SEL_BLOCK)
                    - np.maximum(cs[:, None], bs[None, :]), 0, None).astype(np.float32) / NSA_CMP_LEN
    imp = jnp.einsum('bhtn,nj->btj', p_cmp, jnp.asarray(inter))
    cur = jnp.arange(T)[:, None] // NSA_SEL_BLOCK
    blk = jnp.arange(nsb)[None, :]
    forced = (blk == 0) | (blk == cur) | (blk == cur - 1)
    score = jnp.where(blk <= cur, imp + jnp.where(forced, NSA_FORCE_BONUS, 0.0), NEG_INF)
    _, idx = lax.top_k(score, n_sel)

    kb = k.reshape(B, nsb, NSA_SEL_BLOCK, E)
    vb = v.reshape(B, nsb, NSA_SEL_BLOCK, E)
    QB = NSA_SEL_Q_BLOCK
    nqb = T // QB
    qs = jnp.moveaxis(q.reshape(B, nqb, QB, H, E), 1, 0)
    idxs = jnp.moveaxis(idx.reshape(B, nqb, QB, n_sel), 1, 0)
    t0s = jnp.arange(nqb) * QB
    bidx = jnp.arange(B)[:, None, None]

    def one_block(args):
        q_blk, idx_blk, t0 = args
        kg = kb[bidx, idx_blk]
        vg = vb[bidx, idx_blk]
        tq = t0 + jnp.arange(QB)
        pos = idx_blk[..., None] * NSA_SEL_BLOCK + jnp.arange(NSA_SEL_BLOCK)
        dist = (tq[None, :, None, None] - pos).astype(jnp.float32)[:, :, None]
        s = (jnp.einsum('bqhd,bqnsd->bqhns', q_blk, kg).astype(jnp.float32) * (E ** -0.5)
             - slopes[None, None, :, None, None] * dist)
        mask = jnp.broadcast_to(dist >= 0, s.shape)
        p = masked_softmax(s.reshape(B, QB, H, -1), mask.reshape(B, QB, H, -1)).reshape(s.shape)
        return jnp.einsum('bqhns,bqnsd->bqhd', p.astype(q_blk.dtype), vg)

    o = lax.map(one_block, (qs, idxs, t0s))
    return jnp.moveaxis(o, 0, 1).reshape(B, T, H, E)

def nsa_window(q, k, v, slopes):
    B, T, H, E = q.shape
    QB = NSA_Q_BLOCK
    nb = T // QB
    nprev = NSA_WINDOW // QB

    def band(t):
        tb = jnp.pad(t.reshape(B, nb, QB, E), ((0, 0), (nprev, 0), (0, 0), (0, 0)))
        return jnp.concatenate([tb[:, j:j + nb] for j in range(nprev + 1)], axis=2)

    kband, vband = band(k), band(v)
    qb = q.reshape(B, nb, QB, H, E)
    tq = jnp.arange(nb)[:, None] * QB + jnp.arange(QB)
    pos = jnp.arange(nb)[:, None] * QB - nprev * QB + jnp.arange((nprev + 1) * QB)
    dist = tq[:, :, None] - pos[:, None, :]
    mask = (dist >= 0) & (dist < NSA_WINDOW) & (pos[:, None, :] >= 0)
    s = (jnp.einsum('bnqhd,bnkd->bnhqk', qb, kband).astype(jnp.float32) * (E ** -0.5)
         - slopes[None, None, :, None, None] * dist.astype(jnp.float32)[None, :, None])
    p = masked_softmax(s, mask[None, :, None])
    o = jnp.einsum('bnhqk,bnkd->bnqhd', p.astype(q.dtype), vband)
    return o.reshape(B, T, H, E)

def native_sparse_attention(q, kv, gate_logit, z, cmp_pos, cmp_w1, cmp_w2):
    B, T, _ = q.shape
    q = q.reshape(B, T, N_HEADS, HEAD_DIM)
    k_c, v_c, k_s, v_s, k_w, v_w = jnp.split(kv, 6, axis=-1)
    slopes = jnp.asarray(ALIBI_SLOPES, jnp.float32)
    o_cmp, p_cmp = nsa_compressed(q, k_c, v_c, cmp_pos, cmp_w1, cmp_w2, slopes)
    o_sel = nsa_selected(q, k_s, v_s, p_cmp, slopes)
    o_win = nsa_window(q, k_w, v_w, slopes)
    g = jax.nn.sigmoid(gate_logit.reshape(B, T, N_HEADS, 3))
    o = g[..., 0:1] * o_cmp + g[..., 1:2] * o_sel + g[..., 2:3] * o_win
    return o.reshape(B, T, MIX_WIDTH) * jax.nn.silu(z)

def hybrid_layer(x, norm_gain, w_in, gdn_conv, gdn_a_log, gdn_dt_bias, gdn_norm,
                 sg_ln_gain, sg_ln_bias, sg_w_s, sg_b_s,
                 rw_mu, rw_w_up, rw_w0, rw_a_up, rw_a0, rw_k_k, rw_k_a, rw_r_k, rw_gn_gain, rw_gn_bias,
                 nsa_cmp_pos, nsa_cmp_w1, nsa_cmp_w2, w_branch, w_out):
    h = rmsnorm(x, norm_gain)
    proj = h @ w_in
    (gdn_qkv, gdn_a, gdn_b, gdn_z, sg_u, sg_v, sg_z, rw, rw_z,
     nsa_q, nsa_kv, nsa_g, nsa_z, merge) = jnp.split(proj, IN_OFFSETS, axis=-1)
    ys = (
        gated_deltanet(gdn_qkv, gdn_a, gdn_b, gdn_z, gdn_conv, gdn_a_log, gdn_dt_bias, gdn_norm),
        spatial_gating(sg_u, sg_v, sg_z, sg_ln_gain, sg_ln_bias, sg_w_s, sg_b_s),
        rwkv7_time_mix(rw, rw_z, rw_mu, rw_w_up, rw_w0, rw_a_up, rw_a0, rw_k_k, rw_k_a, rw_r_k,
                       rw_gn_gain, rw_gn_bias),
        native_sparse_attention(nsa_q, nsa_kv, nsa_g, nsa_z, nsa_cmp_pos, nsa_cmp_w1, nsa_cmp_w2),
    )
    gates = jnp.split(jax.nn.sigmoid(merge), N_MIXERS, axis=-1)
    mixed = gates[0] * (ys[0] @ w_branch[0])
    for i in range(1, N_MIXERS):
        mixed = mixed + gates[i] * (ys[i] @ w_branch[i])
    return x + mixed @ w_out

def first_inputs(seed: int = 0) -> dict:
    key = jax.random.key(seed)
    ks = jax.random.split(key, 32)
    f32 = jnp.float32
    L, D, W, H, E = DEPTH, D_MODEL, MIX_WIDTH, N_HEADS, HEAD_DIM
    nrm = lambda k, shape, scale: scale * jax.random.normal(k, shape, f32)
    dt = jnp.exp(jax.random.uniform(ks[5], (L, H), f32, math.log(1e-3), math.log(1e-1)))
    return {
        'x': nrm(ks[0], (BATCH, SEQ, D), 1.0),
        'norm_gain': 1.0 + nrm(ks[1], (L, D), 0.1),
        'w_in': nrm(ks[2], (L, D, D_IN), D ** -0.5),
        'gdn_conv': nrm(ks[3], (L, GDN_CONV, 3 * W), 0.5),
        'gdn_a_log': jnp.log(jax.random.uniform(ks[4], (L, H), f32, 1.0, 16.0)),
        'gdn_dt_bias': jnp.log(jnp.expm1(dt)),
        'gdn_norm': 1.0 + nrm(ks[6], (L, E), 0.1),
        'sg_ln_gain': 1.0 + nrm(ks[7], (L, W), 0.1),
        'sg_ln_bias': nrm(ks[8], (L, W), 0.02),
        'sg_w_s': nrm(ks[9], (L, SG_GROUPS, SG_CHUNK, SG_CHUNK), SG_CHUNK ** -0.5),
        'sg_b_s': 1.0 + nrm(ks[10], (L, SG_GROUPS, SG_CHUNK), 0.1),
        'rw_mu': jax.random.uniform(ks[11], (L, RW_WIDTH), f32, 0.0, 1.0),
        'rw_w_up': nrm(ks[12], (L, RWKV_DECAY_RANK, W), 0.1),
        'rw_w0': jax.random.uniform(ks[13], (L, W), f32, -6.0, -1.0),
        'rw_a_up': nrm(ks[14], (L, RWKV_A_RANK, W), 0.1),
        'rw_a0': nrm(ks[15], (L, W), 0.1),
        'rw_k_k': 0.85 + nrm(ks[16], (L, W), 0.05),
        'rw_k_a': 1.0 + nrm(ks[17], (L, W), 0.05),
        'rw_r_k': nrm(ks[18], (L, H, E), 0.1),
        'rw_gn_gain': 1.0 + nrm(ks[19], (L, W), 0.1),
        'rw_gn_bias': nrm(ks[20], (L, W), 0.02),
        'nsa_cmp_pos': nrm(ks[21], (L, 2, NSA_CMP_LEN, NSA_KV_DIM), 0.1),
        'nsa_cmp_w1': nrm(ks[22], (L, 2, NSA_CMP_LEN * NSA_KV_DIM, NSA_CMP_HIDDEN), (NSA_CMP_LEN * NSA_KV_DIM) ** -0.5),
        'nsa_cmp_w2': nrm(ks[23], (L, 2, NSA_CMP_HIDDEN, NSA_KV_DIM), NSA_CMP_HIDDEN ** -0.5),
        'w_branch': nrm(ks[24], (L, N_MIXERS, W, D), W ** -0.5),
        'w_out': nrm(ks[25], (L, D, D), D ** -0.5),
        'final_gain': 1.0 + nrm(ks[26], (D,), 0.1),
    }

def first_block(x, norm_gain, w_in, gdn_conv, gdn_a_log, gdn_dt_bias, gdn_norm,
              sg_ln_gain, sg_ln_bias, sg_w_s, sg_b_s,
              rw_mu, rw_w_up, rw_w0, rw_a_up, rw_a0, rw_k_k, rw_k_a, rw_r_k, rw_gn_gain, rw_gn_bias,
              nsa_cmp_pos, nsa_cmp_w1, nsa_cmp_w2, w_branch, w_out, final_gain):
    for l in range(DEPTH):
        x = hybrid_layer(
            x, norm_gain[l], w_in[l], gdn_conv[l], gdn_a_log[l], gdn_dt_bias[l], gdn_norm[l],
            sg_ln_gain[l], sg_ln_bias[l], sg_w_s[l], sg_b_s[l],
            rw_mu[l], rw_w_up[l], rw_w0[l], rw_a_up[l], rw_a0[l], rw_k_k[l], rw_k_a[l], rw_r_k[l],
            rw_gn_gain[l], rw_gn_bias[l],
            nsa_cmp_pos[l], nsa_cmp_w1[l], nsa_cmp_w2[l], w_branch[l], w_out[l])
    return rmsnorm(x, final_gain)


DEPTH_2 = 2

HEADS_A = 8
VDIM_A = 2 * HEAD_DIM
WIDTH_A = HEADS_A * VDIM_A
DILATED_GROUPS = ((128, 1), (512, 4), (2048, 16))
N_GROUPS_B = 3
HEADS_PER_GROUP_B = 4
HEADS_B = N_GROUPS_B * HEADS_PER_GROUP_B
WIDTH_B = HEADS_PER_GROUP_B * HEAD_DIM
D_FF = 4 * D_MODEL
ROPE_THETA = 500000.0
ROT_FRACTION = 4
Q_BLOCK = 128
EPS = 1e-6
NEG_INF_2 = -1e30
Q_A_COLS = HEADS_A * 2 * HEAD_DIM
K_A_COLS = HEADS_A * 2 * HEAD_DIM
V_A_COLS = HEADS_A * VDIM_A
QKV_B_COLS = HEADS_B * HEAD_DIM
GATE_COLS = 2 * D_MODEL
IN_COLS = Q_A_COLS + K_A_COLS + V_A_COLS + 3 * QKV_B_COLS + GATE_COLS
IN_SPLITS_2 = (
    Q_A_COLS,
    Q_A_COLS + K_A_COLS,
    Q_A_COLS + K_A_COLS + V_A_COLS,
    Q_A_COLS + K_A_COLS + V_A_COLS + QKV_B_COLS,
    Q_A_COLS + K_A_COLS + V_A_COLS + 2 * QKV_B_COLS,
    Q_A_COLS + K_A_COLS + V_A_COLS + 3 * QKV_B_COLS,
)


def rms_norm(x, g):
    xf = x.astype(jnp.float32)
    y = xf * lax.rsqrt(jnp.mean(xf * xf, axis=-1, keepdims=True) + EPS)
    return (y * g.astype(jnp.float32)).astype(x.dtype)

def rope_tables(positions):
    rot = HEAD_DIM // ROT_FRACTION
    inv_freq = ROPE_THETA ** (-jnp.arange(0, rot, 2, dtype=jnp.float32) / rot)
    ang = positions.astype(jnp.float32)[..., None] * inv_freq
    return jnp.cos(ang), jnp.sin(ang)

def apply_rope(x, cos, sin):
    half = cos.shape[-1]
    bshape = cos.shape[:2] + (1,) * (x.ndim - 3) + (half,)
    cs = cos.reshape(bshape).astype(x.dtype)
    sn = sin.reshape(bshape).astype(x.dtype)
    x1, x2, rest = x[..., :half], x[..., half:2 * half], x[..., 2 * half:]
    return jnp.concatenate([x1 * cs - x2 * sn, x2 * cs + x1 * sn, rest], axis=-1)

def diff_attention(q, k, v, lam):
    b, s, h, _, dh = q.shape
    nq = s // Q_BLOCK
    scale = dh ** -0.5
    qb = q.reshape(b, nq, Q_BLOCK, h, 2, dh).transpose(1, 0, 3, 4, 2, 5)
    kt = k.transpose(0, 2, 3, 1, 4)
    vt = v.transpose(0, 2, 1, 3)

    def block(qblk):
        sc = jnp.einsum('bhcqd,bhckd->bhcqk', qblk, kt).astype(jnp.float32) * scale
        p = jax.nn.softmax(sc, axis=-1)
        w = p[:, :, 0] - lam * p[:, :, 1]
        return jnp.einsum('bhqk,bhkd->bhqd', w.astype(vt.dtype), vt)

    o = lax.map(block, qb)
    return o.transpose(1, 0, 3, 2, 4).reshape(b, s, h, 2 * dh)

def dilated_window_attention(q, k, v, dilation, side):
    b, s, h, dh = q.shape
    L = s // dilation
    nb = -(-L // side)
    Lp = nb * side

    def split(t):
        return t.reshape(b, L, dilation, h, dh).transpose(0, 2, 3, 1, 4)

    qs = jnp.pad(split(q), ((0, 0),) * 3 + ((0, Lp - L), (0, 0)))
    pad_kv = ((0, 0),) * 3 + ((side, Lp - L + side), (0, 0))
    kp = jnp.pad(split(k), pad_kv)
    vp = jnp.pad(split(v), pad_kv)

    def band(t):
        return jnp.concatenate(
            [t[..., j * side:j * side + Lp, :].reshape(b, dilation, h, nb, side, dh) for j in range(3)],
            axis=-2)

    kb, vb = band(kp), band(vp)
    qb = qs.reshape(b, dilation, h, nb, side, dh)
    sc = jnp.einsum('bghnqd,bghnkd->bghnqk', qb, kb).astype(jnp.float32) * (dh ** -0.5)
    blk = jnp.arange(nb)[:, None, None]
    qpos = blk * side + jnp.arange(side)[None, :, None]
    kpos = blk * side - side + jnp.arange(3 * side)[None, None, :]
    valid = (jnp.abs(qpos - kpos) <= side) & (kpos >= 0) & (kpos < L)
    sc = jnp.where(valid, sc, NEG_INF_2)
    lse = jax.nn.logsumexp(sc, axis=-1)
    p = jnp.exp(sc - lse[..., None])
    o = jnp.einsum('bghnqk,bghnkd->bghnqd', p.astype(v.dtype), vb)
    o = o.reshape(b, dilation, h, Lp, dh)[..., :L, :].transpose(0, 3, 1, 2, 4).reshape(b, s, h, dh)
    lse = lse.reshape(b, dilation, h, Lp)[..., :L].transpose(0, 3, 1, 2).reshape(b, s, h)
    return o, lse

def second_inputs(seed: int = 0) -> dict:
    key = jax.random.key(seed)
    ks = jax.random.split(key, 20)
    D = D_MODEL
    nrm = lambda k, shape, s: jax.random.normal(k, shape, jnp.float32) * s
    x = nrm(ks[0], (BATCH, SEQ, D), 1.0)
    c = nrm(ks[1], (BATCH, D), 1.0)
    offsets = jax.random.randint(ks[2], (BATCH, 1), 0, 1024, dtype=jnp.int32)
    positions = (jnp.arange(SEQ, dtype=jnp.int32)[None, :] + offsets).astype(jnp.int32)
    return {
        "x": x,
        "c": c,
        "positions": positions,
        "ada_w": nrm(ks[3], (DEPTH_2, D, 6 * D), D ** -0.5),
        "ada_b": nrm(ks[4], (DEPTH_2, 6 * D), 0.02),
        "norm_mix_g": 1.0 + nrm(ks[5], (DEPTH_2, D), 0.02),
        "norm_mlp_g": 1.0 + nrm(ks[6], (DEPTH_2, D), 0.02),
        "w_in": nrm(ks[7], (DEPTH_2, D, IN_COLS), D ** -0.5),
        "qk_gain_a": 1.0 + nrm(ks[8], (DEPTH_2, 2, HEAD_DIM), 0.02),
        "lambda_a": nrm(ks[9], (DEPTH_2, 4, HEAD_DIM), 0.1),
        "subln_g_a": 1.0 + nrm(ks[10], (DEPTH_2, VDIM_A), 0.02),
        "qk_gain_b": 1.0 + nrm(ks[11], (DEPTH_2, 2, HEAD_DIM), 0.02),
        "w_branch_a": nrm(ks[12], (DEPTH_2, WIDTH_A, D), WIDTH_A ** -0.5),
        "w_branch_b": nrm(ks[13], (DEPTH_2, WIDTH_B, D), WIDTH_B ** -0.5),
        "gate_bias": nrm(ks[14], (DEPTH_2, GATE_COLS), 0.02),
        "w_out": nrm(ks[15], (DEPTH_2, D, D), D ** -0.5),
        "w_mlp_up": nrm(ks[16], (DEPTH_2, D, D_FF), D ** -0.5),
        "w_mlp_down": nrm(ks[17], (DEPTH_2, D_FF, D), D_FF ** -0.5),
    }

def second_block(x, c, positions, ada_w, ada_b, norm_mix_g, norm_mlp_g, w_in, qk_gain_a,
              lambda_a, subln_g_a, qk_gain_b, w_branch_a, w_branch_b, gate_bias, w_out,
              w_mlp_up, w_mlp_down):
    b, s, _ = x.shape
    cos, sin = rope_tables(positions)
    cond = jax.nn.silu(c)
    for l in range(DEPTH_2):
        mod = (cond @ ada_w[l] + ada_b[l])[:, None, :]
        shift_m, scale_m, gate_m, shift_f, scale_f, gate_f = jnp.split(mod, 6, axis=-1)

        h = rms_norm(x, norm_mix_g[l]) * (1.0 + scale_m) + shift_m
        proj = h @ w_in[l]
        qa, ka, va, qb, kb, vb, gates = jnp.split(proj, IN_SPLITS_2, axis=-1)

        qa = apply_rope(rms_norm(qa.reshape(b, s, HEADS_A, 2, HEAD_DIM), qk_gain_a[l, 0]), cos, sin)
        ka = apply_rope(rms_norm(ka.reshape(b, s, HEADS_A, 2, HEAD_DIM), qk_gain_a[l, 1]), cos, sin)
        va = va.reshape(b, s, HEADS_A, VDIM_A)
        lam_init = 0.8 - 0.6 * math.exp(-0.3 * l)
        lv = lambda_a[l].astype(jnp.float32)
        lam = jnp.exp(jnp.sum(lv[0] * lv[1])) - jnp.exp(jnp.sum(lv[2] * lv[3])) + lam_init
        oa = diff_attention(qa, ka, va, lam)
        oa = (rms_norm(oa, subln_g_a[l]) * (1.0 - lam_init)).reshape(b, s, WIDTH_A)

        qb = apply_rope(rms_norm(qb.reshape(b, s, N_GROUPS_B, HEADS_PER_GROUP_B, HEAD_DIM), qk_gain_b[l, 0]), cos, sin)
        kb = apply_rope(rms_norm(kb.reshape(b, s, N_GROUPS_B, HEADS_PER_GROUP_B, HEAD_DIM), qk_gain_b[l, 1]), cos, sin)
        vb = vb.reshape(b, s, N_GROUPS_B, HEADS_PER_GROUP_B, HEAD_DIM)
        outs, lses = [], []
        for g, (window, dilation) in enumerate(DILATED_GROUPS):
            o_g, lse_g = dilated_window_attention(qb[:, :, g], kb[:, :, g], vb[:, :, g],
                                                  dilation, window // (2 * dilation))
            outs.append(o_g)
            lses.append(lse_g)
        wgt = jax.nn.softmax(jnp.stack(lses, axis=0), axis=0)
        ob = jnp.sum(wgt[..., None].astype(x.dtype) * jnp.stack(outs, axis=0), axis=0)
        ob = ob.reshape(b, s, WIDTH_B)

        g_a, g_b = jnp.split(jax.nn.sigmoid(gates + gate_bias[l]), 2, axis=-1)
        y = (g_a * (oa @ w_branch_a[l]) + g_b * (ob @ w_branch_b[l])) @ w_out[l]
        x = x + gate_m * y

        h = rms_norm(x, norm_mlp_g[l]) * (1.0 + scale_f) + shift_f
        x = x + gate_f * (jnp.square(jax.nn.relu(h @ w_mlp_up[l])) @ w_mlp_down[l])
    return x


def setup_inputs(seed=0):
    out = dict(first_inputs(seed))
    for name, value in second_inputs(seed + 1).items():
        if name != "x":
            out[name + "_2"] = value
    return out


def reference(
    x, norm_gain, w_in, gdn_conv, gdn_a_log, gdn_dt_bias, gdn_norm, sg_ln_gain, sg_ln_bias,
    sg_w_s, sg_b_s, rw_mu, rw_w_up, rw_w0, rw_a_up, rw_a0, rw_k_k, rw_k_a, rw_r_k, rw_gn_gain,
    rw_gn_bias, nsa_cmp_pos, nsa_cmp_w1, nsa_cmp_w2, w_branch, w_out, final_gain, c_2,
    positions_2, ada_w_2, ada_b_2, norm_mix_g_2, norm_mlp_g_2, w_in_2, qk_gain_a_2, lambda_a_2,
    subln_g_a_2, qk_gain_b_2, w_branch_a_2, w_branch_b_2, gate_bias_2, w_out_2, w_mlp_up_2,
    w_mlp_down_2,
):
    x = first_block(
        x, norm_gain, w_in, gdn_conv, gdn_a_log, gdn_dt_bias, gdn_norm, sg_ln_gain, sg_ln_bias,
        sg_w_s, sg_b_s, rw_mu, rw_w_up, rw_w0, rw_a_up, rw_a0, rw_k_k, rw_k_a, rw_r_k,
        rw_gn_gain, rw_gn_bias, nsa_cmp_pos, nsa_cmp_w1, nsa_cmp_w2, w_branch, w_out,
        final_gain,
    )
    return second_block(
        x, c_2, positions_2, ada_w_2, ada_b_2, norm_mix_g_2, norm_mlp_g_2, w_in_2, qk_gain_a_2,
        lambda_a_2, subln_g_a_2, qk_gain_b_2, w_branch_a_2, w_branch_b_2, gate_bias_2, w_out_2,
        w_mlp_up_2, w_mlp_down_2,
    )


_drawn_inputs = setup_inputs


def setup_inputs(seed=0):
    import zlib

    import numpy as np

    out = dict(_drawn_inputs(seed))
    spreads = {}
    factors = {'sg_ln_gain': 4.47,
     'sg_ln_bias': 8.0,
     'sg_b_s': 3.12,
     'rw_w_up': 5.35,
     'rw_a0': 5.534,
     'rw_k_k': 4.156,
     'rw_k_a': 4.079,
     'rw_gn_bias': 8.0,
     'nsa_cmp_pos': 6.628,
     'norm_mix_g_2': 8.0,
     'norm_mlp_g_2': 2.785,
     'qk_gain_a_2': 8.0,
     'lambda_a_2': 6.512,
     'subln_g_a_2': 8.0,
     'qk_gain_b_2': 8.0,
     'gate_bias_2': 8.0}
    for name, (base, spread) in spreads.items():
        noise = np.random.default_rng([zlib.crc32(name.encode()), seed]).standard_normal(out[name].shape)
        drawn = base * np.exp(spread * noise) if base else spread * noise
        out[name] = jnp.asarray(drawn.astype(out[name].dtype))
    for name, factor in factors.items():
        out[name] = (out[name] * factor).astype(out[name].dtype)
    return out
```

```python
import math

import numpy as np
import concourse.bass as bass
import concourse.mybir as mybir
from concourse.alu_op_type import AluOpType as ALU

ACT = mybir.ActivationFunctionType
F32 = mybir.dt.float32
BF16 = mybir.dt.bfloat16
I32 = mybir.dt.int32
AX_X = mybir.AxisListType.X

P = 128
T = 512
D = 1024
NT = T // P
ND = D // P
H = 4
E = 64
MIX = 256
EPS = 1e-6
NEG = -1e30

QKV0, A0, B0, Z0, U0, V0, SZ0 = 0, 768, 772, 776, 1032, 1288, 1544
RW0, RWZ0, NQ0, NKV0, NG0, NZ0, MERGE0 = 1800, 2696, 2952, 3208, 3592, 3604, 3860

TM_VS, TM_VW, TM_NG, TM_NZ, NS_W = 0, 64, 128, 140, 396

RING = 3
SLOT = 4096

STOP = None


class Signal:
    everyone = []

    def __init__(self, nc, name):
        self.sem = nc.alloc_semaphore(name)
        self.count = self.base = 0
        Signal.everyone.append(self)

    def one(self):
        self.count += 1
        return self.sem, 1

    def dma(self):
        self.count += 16
        return self.sem, 16

    def at(self, k):
        assert k > 0
        return self.sem, self.base + k

    def order_of(self, names):
        self.names = {n: j + 1 for j, n in enumerate(names)}
        assert len(self.names) == len(names)

    def step(self, name):
        assert self.names[name] == self.count - self.base + 1, (name, self.count - self.base)
        return self.one()

    def after(self, name):
        return self.sem, self.base + self.names[name]

    def all_of_stage(self, k):
        return self.sem, self.base + k

    def all(self):
        return self.sem, self.count


class Stop(Exception):
    pass


def columns(w, lo, n, k0=0, nk=None):
    v = w.rearrange("(k p) c -> p k c", p=P)
    return v[:, k0:(v.shape[1] if nk is None else k0 + nk), lo:lo + n]


def weight_plan(a):
    plan = []
    w = a["w_in"][0]
    for lo, hi in P1_CHUNKS:
        plan.append((("p1", lo), [(columns(w, lo, hi - lo), 0)]))
    for c in range(ND):
        gates = [(columns(w, MERGE0 + i * D + c * P, P), i * ND * P) for i in range(4)]
        plan.append((("gate", c), gates))
        br = [(columns(a["w_branch"][0, i], c * P, P), i * 2 * P) for i in range(4)]
        plan.append((("branch", c), br))
    for c in range(2):
        plan.append((("out", c), [(columns(a["w_out"][0], c * 512, 512), 0)]))
    for l in range(2):
        for c in range(12):
            plan.append((("ada", l, c), [(columns(a["ada_w_2"][l], c * 512, 512), 0)]))
        w = a["w_in_2"][l]
        for c in range(6):
            plan.append((("a", l, c), [(columns(w, c * 512, 512), 0)]))
        for c in range(6):
            plan.append((("b", l, c), [(columns(w, 3072 + c * 384, 384), 0)]))
        for c in range(4):
            plan.append((("gates", l, c), [(columns(w, 5376 + i * D + c * 256, 256), i * 2048) for i in range(2)]))
            plan.append((("branches", l, c), [(columns(a["w_branch_a_2"][l], c * 256, 256), 0),
                                              (columns(a["w_branch_b_2"][l], c * 256, 256), 2048)]))
        for c in range(2):
            plan.append((("out", l, c), [(columns(a["w_out_2"][l], c * 512, 512), 0)]))
        for c in range(8):
            plan.append((("up", l, c), [(columns(a["w_mlp_up_2"][l], c * 512, 512), 0)]))
        for c in range(4):
            for half in range(2):
                plan.append((("down", l, c, half), [(columns(a["w_mlp_down_2"][l], c * 256, 256, half * 16, 16), 0)]))
    return plan


P1_CHUNKS = [(0, 384), (384, 768), (768, 1032), (1032, 1544), (1544, 1800), (1800, 2312), (2312, 2696),
             (2696, 2952), (2952, 3464), (3464, 3860)]


class Weights:

    def __init__(self, nc, arrays):
        self.ring = nc.alloc_sbuf_tensor("weight_ring", [P, RING, SLOT], F32)
        self.landed = [Signal(nc, f"weights_landed_{s}") for s in range(RING)]
        self.released = []
        self.plan = weight_plan(arrays)
        self.taken = self.loaded = 0
        self.need = []
        count = [0] * RING
        for n, (_, parts) in enumerate(self.plan):
            count[n % RING] += 16 * len(parts)
            self.need.append(count[n % RING])

    def take(self, pe, key, width):
        n = self.taken
        assert self.plan[n][0] == key, (self.plan[n][0], key)
        pe.wait_ge(self.landed[n % RING].sem, self.need[n])
        self.taken += 1
        s = self.ring[:, n % RING, :]
        return s[:, 0:SLOT // width * width].rearrange("p (k c) -> p k c", c=width)

    def release(self, signal):
        self.released.append(signal.all())

    def feed(self, sp):
        while self.loaded < min(len(self.plan), len(self.released) + RING):
            n = self.loaded
            if n >= RING:
                sp.wait_ge(*self.released[n - RING])
            for view, offset in self.plan[n][1]:
                _, k, c = view.shape
                dst = self.ring[:, n % RING, offset:offset + k * c].rearrange("p (k c) -> p k c", c=c)
                sp.dma_start(dst, view).then_inc(*self.landed[n % RING].dma())
            self.loaded += 1


ARENA = 29696

PAR = {}
PAR_ROWS = [("norm_gain", 8), ("final_gain", 8), ("gdn_conv", 24), ("rw_mu", 7), ("sg_b_s", 4),
            ("norm_mix_g_2", 16), ("norm_mlp_g_2", 16), ("gate_bias_2", 32),
            ("c_2", 8), ("ada_b_2", 96)]
for _name, _rows in PAR_ROWS:
    PAR[_name] = sum(r for n, r in PAR_ROWS[:[n for n, _ in PAR_ROWS].index(_name)])
PAR_SPLIT = PAR["c_2"]
PAR_N = PAR["ada_b_2"] + 96


class AttentionSignals:
    def __init__(self, nc):
        self.scores = Signal(nc, "scores_done")
        self.maxima = Signal(nc, "maxima_done")
        self.exps = Signal(nc, "exps_done")
        self.mixed = Signal(nc, "mixed")
        self.turned = Signal(nc, "rows_turned")
        self.copied = Signal(nc, "turned_copied")
        self.summed = Signal(nc, "values_summed")
        self.finished = Signal(nc, "group_finished")


class Kernel:
    def __init__(self, nc, arrays, out):
        self.nc, self.a, self.out = nc, arrays, out
        Signal.everyone = []
        self.w = Weights(nc, arrays)
        self.bank = [nc.alloc_psum_tensor(f"bank{b}", [P, 512], F32) for b in range(8)]
        sb = self.sb
        self.xT = sb("xT", [P, ND, T])
        self.hT = sb("hT", [P, ND, T])
        self.ident = sb("ident", [P, P])
        self.ones = sb("ones", [P, P])
        self.par = sb("par", [P, PAR_N])
        self.arena = sb("arena", [P, ARENA])
        self.top = 0
        self.params_landed = Signal(nc, "params_landed")
        self.x_landed = Signal(nc, "x_landed")
        self.mm_done = Signal(nc, "mm_done")
        self.evac_act = Signal(nc, "evac_act")
        self.evac_dve = Signal(nc, "evac_dve")
        self.act_order = Signal(nc, "act_order")
        self.dve_order = Signal(nc, "dve_order")
        self.pool_order = Signal(nc, "pool_order")
        self.act_ready = Signal(nc, "act_ready")
        self.dve_ready = Signal(nc, "dve_ready")
        self.pool_ready = Signal(nc, "pool_ready")
        self.stored = Signal(nc, "stored")
        self.att = AttentionSignals(nc)
        self.pe_ready = Signal(nc, "pe_ready")
        self.scratch = sb("scratch", [P, 512])
        self.nc_pos = sb("positions", [P, NT], I32)
        self.nc_dist = sb("distances", [P, 7 * P], I32)
        self.nc_bits = sb("distance_bits", [P, 7 * P], I32)

    def sb(self, name, shape, dt=F32):
        return self.nc.alloc_sbuf_tensor(name, shape, dt)

    def take(self, *dims):
        n = math.prod(dims)
        v = self.arena[:, self.top:self.top + n]
        self.top += n
        assert self.top <= ARENA, (self.top, ARENA)
        if len(dims) == 1:
            return v
        names = "abcd"[:len(dims)]
        return v.rearrange(f"p ({' '.join(names)}) -> p {' '.join(names)}",
                           **{names[j]: dims[j] for j in range(1, len(dims))})

    def end_stage(self, name):
        for s in Signal.everyone:
            s.base = s.count
        if name == STOP:
            with self.nc.Block() as block:
                @block.sync
                def _(sp):
                    for s in self.w.landed:
                        sp.wait_ge(*s.all())
            raise Stop

    def order(self, eng, signal):
        def seq(ins):
            ins.then_inc(*signal.one())
            eng.wait_ge(*signal.all())
        return seq

    def load(self):
        nc, a = self.nc, self.a
        keep = self.top
        x_tm = self.take(NT, D)
        rows = self.take(2, P)

        with nc.Block() as block:
            @block.gpsimd
            def _(pool):
                seq = self.order(pool, self.pool_order)
                pool.memset(self.ones[:], 1.0).then_inc(*self.pool_order.one())
                seq(pool.memset(self.ident[:], 0.0))
                pool.affine_select(out=self.ident[:], in_=self.ident[:], compare_op=ALU.not_equal, fill=1.0,
                                   base=0, pattern=[[-1, P]], channel_multiplier=1).then_inc(*self.pool_ready.one())

            @block.tensor
            def _(pe):
                pe.wait_ge(*self.pool_ready.at(1))
                pe.wait_ge(*self.x_landed.all_of_stage(16))
                for k in range(ND):
                    for i in range(NT):
                        ins = pe.transpose(self.bank[k][:, i * P:(i + 1) * P], x_tm[:, i, k * P:(k + 1) * P],
                                           self.ident[:])
                    ins.then_inc(*self.mm_done.one())
                pe.wait_ge(*self.params_landed.all_of_stage(16 * len(PAR_ROWS)))
                pe.wait_ge(*self.evac_dve.at(1))
                n = PAR_SPLIT
                pe.transpose(self.bank[0][:, 0:n], rows[0:n, 0, :], self.ident[0:n, 0:n])
                m = PAR_N - PAR_SPLIT
                pe.transpose(self.bank[0][:, n:n + m], rows[0:m, 1, :],
                             self.ident[0:m, 0:m]).then_inc(*self.mm_done.one())

            @block.vector
            def _(dve):
                for k in range(ND):
                    dve.wait_ge(*self.mm_done.at(k + 1))
                    dve.tensor_copy(self.xT[:, k, :], self.bank[k][:]).then_inc(*self.evac_dve.one())
                dve.wait_ge(*self.mm_done.at(ND + 1))
                dve.tensor_copy(self.par[:], self.bank[0][:, 0:PAR_N]).then_inc(*self.evac_dve.one())

            @block.scalar
            def _(act):
                for name, n in PAR_ROWS:
                    c0 = PAR[name]
                    half, r = (0, c0) if c0 < PAR_SPLIT else (1, c0 - PAR_SPLIT)
                    v = a[name]
                    while len(v.shape) > 1:
                        v = v.rearrange("a b -> (a b)") if len(v.shape) == 2 else v.rearrange("a b c -> a (b c)")
                    act.dma_start(rows[r:r + n, half, :], v.rearrange("(r q) -> r q", q=P))\
                       .then_inc(*self.params_landed.dma())

            @block.sync
            def _(sp):
                sp.dma_start(x_tm, a["x"][0].rearrange("(i p) d -> p i d", p=P)).then_inc(*self.x_landed.dma())
                self.w.feed(sp)
        self.top = keep
        self.end_stage("load")

    def rms(self, name, gain, shift=None, dst=None):
        nc = self.nc
        keep = self.top
        sq = self.take(2, T)
        rs = self.take(T)
        dst = self.hT if dst is None else dst
        with nc.Block() as block:
            @block.scalar
            def _(act):
                for k in range(ND):
                    if k >= 2:
                        act.wait_ge(*self.mm_done.at(k - 1))
                    act.activation(sq[:, k % 2, :], self.xT[:, k, :], ACT.Square).then_inc(*self.act_ready.one())
                seq = self.order(act, self.act_order)
                act.wait_ge(*self.dve_ready.at(1))
                seq(act.activation(rs, rs, ACT.Ln))
                act.activation(rs, rs, ACT.Exp, scale=-0.5).then_inc(*self.act_ready.one())

            @block.tensor
            def _(pe):
                for k in range(ND):
                    pe.wait_ge(*self.act_ready.at(k + 1))
                    pe.matmul(self.bank[0][:], self.ones[:], sq[:, k % 2, :], start=k == 0,
                              stop=k == ND - 1).then_inc(*self.mm_done.one())

            @block.vector
            def _(dve):
                dve.wait_ge(*self.mm_done.at(ND))
                dve.tensor_scalar(rs, self.bank[0][:], 1.0 / D, EPS, ALU.mult, ALU.add)\
                   .then_inc(*self.dve_ready.one())
                dve.wait_ge(*self.act_ready.at(ND + 1))
                for k in range(ND):
                    dve.scalar_tensor_tensor(dst[:, k, :], self.xT[:, k, :], gain(k), rs, ALU.mult,
                                             ALU.mult).then_inc(*self.dve_order.one())
                    if shift is not None:
                        dve.wait_ge(*self.dve_order.all())
                        dve.tensor_scalar(dst[:, k, :], dst[:, k, :], shift(k), None,
                                          ALU.add).then_inc(*self.dve_order.one())

            @block.sync
            def _(sp):
                self.w.feed(sp)
        self.top = keep
        self.end_stage(name)

    def products(self, name, tiles, before=None):
        nc = self.nc
        NB = 8
        def emptied(t):
            which = tiles[t]["by"]
            return which, sum(x["by"] == which for x in tiles[:t + 1])

        with nc.Block() as block:
            @block.tensor
            def _(pe):
                chunks = {}
                for t, tile in enumerate(tiles):
                    for key, width in tile.get("takes", ()):
                        chunks[key] = self.w.take(pe, key, width)
                    if t >= NB:
                        which, n = emptied(t - NB)
                        pe.wait_ge(*(self.evac_act if which == "act" else self.evac_dve).at(n))
                    pairs = tile["pairs"](chunks)
                    m = tile["shape"]
                    for j, (lhsT, rhs) in enumerate(pairs):
                        ins = pe.matmul(self.bank[t % NB][0:m[0], 0:m[1]], lhsT, rhs, start=j == 0,
                                        stop=j == len(pairs) - 1)
                    ins.then_inc(*self.mm_done.one())
                    for _ in range(tile.get("frees", 0)):
                        self.w.release(self.mm_done)

            def empty(eng, which, done, order):
                seq = self.order(eng, order)
                for t, tile in enumerate(tiles):
                    if tile["by"] == which:
                        eng.wait_ge(*self.mm_done.at(t + 1))
                        for other in tile.get("needs", ()):
                            by, n = emptied(other)
                            eng.wait_ge(*(self.evac_act if by == "act" else self.evac_dve).at(n))
                        m = tile["shape"]
                        tile["empty"](eng, seq, self.bank[t % NB][0:m[0], 0:m[1]]).then_inc(*done.one())

            @block.scalar
            def _(act):
                empty(act, "act", self.evac_act, self.act_order)

            @block.vector
            def _(dve):
                empty(dve, "dve", self.evac_dve, self.dve_order)

            @block.sync
            def _(sp):
                self.w.feed(sp)
        self.end_stage(name)

    def first_projection(self):
        self.ysT = self.take(8, T)
        self.after_ys = self.top
        self.ab = self.take(NT, 8)
        self.z_gdn = self.take(NT, MIX)
        self.z_rw = self.take(NT, MIX)
        self.qkvT = self.take(6, T + 3)
        self.rwT = self.take(7, T + 1)
        self.after_mixer_inputs = self.top
        self.sg = self.take(NT, 3 * MIX)
        self.ns = self.take(NT, NS_W)
        self.nsa_qT = self.take(H, T)
        self.nsa_kvT = self.take(4, T)
        hT = self.hT
        tiles = []

        def fm(key, width, lo, m, dst, **more):
            tiles.append(dict(by="dve", shape=(m, T), pairs=lambda ch: [
                (ch[key][:, k, lo:lo + m], hT[:, k, :]) for k in range(ND)],
                empty=lambda e, seq, ps: e.tensor_copy(dst, ps), **more))

        def tmaj(key, lo, n, i, empty, by="act", **more):
            tiles.append(dict(by=by, shape=(P, n), pairs=lambda ch: [
                (hT[:, k, i * P:(i + 1) * P], ch[key][:, k, lo:lo + n]) for k in range(ND)], empty=empty, **more))

        def func(f, dst):
            return lambda e, seq, ps: e.activation(dst, ps, f)

        def copy(dst):
            return lambda e, seq, ps: e.tensor_copy(dst, ps)

        for lo, hi in P1_CHUNKS:
            key, width = ("p1", lo), hi - lo
            first = len(tiles)
            if lo < A0:
                for c in range(lo // P, hi // P):
                    fm(key, width, c * P - lo, P, self.qkvT[:, c, 3:])
            elif lo == A0:
                for i in range(NT):
                    tmaj(key, 0, 8, i, copy(self.ab[:, i, :]), by="dve")
                    tmaj(key, 8, MIX, i, func(ACT.Silu, self.z_gdn[:, i, :]))
            elif lo == U0:
                for i in range(NT):
                    tmaj(key, 0, 512, i, func(ACT.Gelu_apprx_tanh, self.sg[:, i, 0:512]))
            elif lo == SZ0:
                for i in range(NT):
                    tmaj(key, 0, MIX, i, func(ACT.Silu, self.sg[:, i, 512:768]))
            elif lo in (RW0, RW0 + 512):
                for c in range((lo - RW0) // P, (hi - RW0) // P):
                    fm(key, width, RW0 + c * P - lo, P, self.rwT[:, c, 1:])
            elif lo == RWZ0:
                for i in range(NT):
                    tmaj(key, 0, MIX, i, func(ACT.Silu, self.z_rw[:, i, :]))
            elif lo == NQ0:
                for h in range(H):
                    fm(key, width, h * E, E, self.nsa_qT[0:E, h, :])
                for j in range(3):
                    fm(key, width, MIX + j * E, E, self.nsa_kvT[0:E, j, :])
                for i in range(NT):
                    tmaj(key, MIX + 3 * E, E, i, copy(self.ns[:, i, TM_VS:TM_VS + E]), by="dve")
            else:
                fm(key, width, 0, E, self.nsa_kvT[0:E, 3, :])
                for i in range(NT):
                    tmaj(key, E, E, i, copy(self.ns[:, i, TM_VW:TM_VW + E]), by="dve")
                    tmaj(key, 2 * E, 12, i, func(ACT.Sigmoid, self.ns[:, i, TM_NG:TM_NG + 12]))
                for i in range(NT):
                    tmaj(key, 2 * E + 12, MIX, i, func(ACT.Silu, self.ns[:, i, TM_NZ:TM_NZ + MIX]))
            tiles[first]["takes"] = [(key, width)]
            tiles[-1]["frees"] = 1
        self.products("p1", tiles)

    def attention(self, name, units, groups, parts=1, joint=1):
        nc = self.nc
        keep = self.top
        N = len(units)
        self.row_sum = self.take(N * parts)
        row_max = self.take(N * parts)
        wait_joint = joint - 1
        NROW = (3 + 2 * wait_joint) * parts
        rows = self.take(NROW, T)
        turned = self.take(2, T)
        S_BANKS, T_BANK, O_BANK = 4, 4, 6
        sig = self.att
        row = lambda q, m: rows[:, q % NROW, 0:m]
        mixes = [sum(bool(u.get("mix")) for u in units[:n + 1]) for n in range(N)]
        last_unit = {}
        for n, u in enumerate(units):
            last_unit[u["group"]] = n

        def steps(*stages):
            for step in range(N + max(lag for lag, _ in stages)):
                for lag, run in stages:
                    if 0 <= step - lag < N:
                        run(step - lag, units[step - lag])

        with nc.Block() as block:
            @block.tensor
            def _(pe):
                def scores(n, u):
                    for j, part in enumerate(u["parts"]):
                        q = n * parts + j
                        if q >= S_BANKS:
                            if part.get("table") is not None:
                                pe.wait_ge(*sig.maxima.at(n - S_BANKS + 1))
                            else:
                                pe.wait_ge(*sig.exps.at(q - S_BANKS + 1))
                        lhsT, rhs = part["scores"]
                        pe.matmul(self.bank[q % S_BANKS][:, 0:part["n"]], lhsT, rhs, start=True, stop=True)\
                          .then_inc(*sig.scores.one())

                def turn(n, u):
                    if u.get("mix"):
                        pe.wait_ge(*sig.mixed.at(mixes[n]))
                    else:
                        pe.wait_ge(*sig.exps.at(n * parts + 1))
                    if n >= 2:
                        pe.wait_ge(*sig.copied.at(n - 1))
                    for b, v in enumerate(u["values"]):
                        k = v.shape[0]
                        ins = pe.transpose(self.bank[T_BANK + n % 2][0:k, b * P:(b + 1) * P],
                                           rows[:, n * parts % NROW, b * P:b * P + k], self.ident[:])
                    ins.then_inc(*sig.turned.one())

                def sums(n, u):
                    g = u["group"]
                    pe.wait_ge(*sig.copied.at(n + 1))
                    if g >= 2:
                        pe.wait_ge(*sig.finished.at(g - 1))
                    lo, hi = u["cols"]
                    for b, v in enumerate(u["values"]):
                        k = v.shape[0]
                        ins = pe.matmul(self.bank[O_BANK + g % 2][:, lo:hi], turned[0:k, n % 2, b * P:(b + 1) * P],
                                        v, start=b == 0 and n % joint == 0,
                                        stop=b == len(u["values"]) - 1 and n % joint == joint - 1)
                    ins.then_inc(*sig.summed.one())
                steps((0, scores), (2 + wait_joint, turn), (3 + wait_joint, sums))

            @block.vector
            def _(dve):
                seq = self.order(dve, self.dve_order)

                def maxima(n, u):
                    for j, part in enumerate(u["parts"]):
                        q, m = n * parts + j, part["n"]
                        dve.wait_ge(*sig.scores.at(q + 1))
                        s = self.bank[q % S_BANKS][:, 0:m]
                        if part.get("table") is None:
                            ins = dve.tensor_reduce(row_max[:, q:q + 1], s, AX_X, ALU.max, negate=True)
                            if j < parts - 1:
                                ins.then_inc(*self.dve_order.one())
                        else:
                            if q >= NROW:
                                dve.wait_ge(*sig.turned.at(n - NROW + 1))
                            ins = dve.tensor_tensor_reduce(row(q, m), s, part["table"], 0.125, -3e38,
                                                           ALU.add, ALU.max, row_max[:, q:q + 1])
                            if n % joint == joint - 1:
                                seq(ins)
                                if joint > 1:
                                    own = row_max[:, n - joint + 1:n + 1]
                                    seq(dve.tensor_reduce(self.scratch[:, 0:1], own, AX_X, ALU.max))
                                    ins = dve.tensor_scalar(own, self.scratch[:, 0:1].broadcast_to([P, joint]), -1.0,
                                                            None, ALU.mult)
                                else:
                                    ins = dve.tensor_scalar(row_max[:, q:q + 1], row_max[:, q:q + 1], -1.0, None,
                                                            ALU.mult)
                    ins.then_inc(*sig.maxima.one())

                def mix(n, u):
                    if u.get("mix"):
                        q = n * parts
                        dve.wait_ge(*sig.exps.at(q + parts))
                        u["mix"](dve, seq, q, [row(q + j, part["n"]) for j, part in enumerate(u["parts"])])\
                            .then_inc(*sig.mixed.one())

                def finish(n, u):
                    if last_unit[u["group"]] == n:
                        dve.wait_ge(*sig.summed.at(n + 1))
                        groups[u["group"]](dve, seq, self.bank[O_BANK + u["group"] % 2])\
                            .then_inc(*sig.finished.one())
                steps((0, maxima), (1 + wait_joint, mix), (4 + wait_joint, finish))

            @block.scalar
            def _(act):
                def exps(n, u):
                    act.wait_ge(*sig.maxima.at(n // joint * joint + joint))
                    for j, part in enumerate(u["parts"]):
                        q, m = n * parts + j, part["n"]
                        if q >= NROW:
                            act.wait_ge(*sig.turned.at((q - NROW) // parts + 1))
                        act.activation(row(q, m), self.bank[q % S_BANKS][:, 0:m] if part.get("table") is None
                                       else row(q, m), ACT.Exp, bias=row_max[:, q:q + 1],
                                       accum_out=self.row_sum[:, q:q + 1]).then_inc(*sig.exps.one())

                def copy(n, u):
                    act.wait_ge(*sig.turned.at(n + 1))
                    if n >= 2:
                        act.wait_ge(*sig.summed.at(n - 1))
                    m, k = P * len(u["values"]), u["values"][0].shape[0]
                    act.activation(turned[0:k, n % 2, 0:m], self.bank[T_BANK + n % 2][0:k, 0:m], ACT.Copy)\
                       .then_inc(*sig.copied.one())
                steps((wait_joint, exps), (2 + wait_joint, copy))

            @block.sync
            def _(sp):
                self.w.feed(sp)
        self.top = keep
        self.end_stage(name)

    def sparse_attention(self):
        nc, a = self.nc, self.a
        NC = T // 16 - 1
        keep = self.top
        self.y_nsa = self.take(NT, MIX)
        kcT = self.take(NC)
        vc = self.take(E)
        o = self.top
        w1 = self.take(2, 32, E)
        w2 = self.take(2, E)
        pos_rows = self.take(E)
        posT = self.take(2, 32)
        blocks = self.take(2, 32, NC)
        hidden = self.take(2, NC)
        kvT = self.nsa_kvT
        landed, seqs = self.params_landed, self.order
        with nc.Block() as block:
            @block.scalar
            def _(act):
                act.dma_start(pos_rows[0:E, :], a["nsa_cmp_pos"][0].rearrange("j p e -> (j p) e"))\
                   .then_inc(*landed.dma())
                for j in range(2):
                    act.dma_start(w1[0:E, j], a["nsa_cmp_w1"][0, j].rearrange("(p e) h -> e p h", e=E))\
                       .then_inc(*landed.dma())
                    act.dma_start(w2[0:E, j], a["nsa_cmp_w2"][0, j]).then_inc(*landed.dma())
                for j in range(2):
                    act.wait_ge(*self.mm_done.at(j + 2))
                    act.activation(hidden[0:E, j, :], self.bank[1 + j][0:E, 0:NC], ACT.Gelu_apprx_tanh)\
                       .then_inc(*self.act_ready.one())

            @block.tensor
            def _(pe):
                pe.wait_ge(*landed.all_of_stage(16 * 5))
                pe.transpose(self.bank[0][0:E, 0:E], pos_rows[0:E, :], self.ident[0:E, 0:E])\
                  .then_inc(*self.mm_done.one())
                for j in range(2):
                    pe.wait_ge(*self.dve_ready.at(2 * j + 2))
                    for p in range(32):
                        ins = pe.matmul(self.bank[1 + j][0:E, 0:NC], w1[0:E, j, p, :], blocks[0:E, j, p, :],
                                        start=p == 0, stop=p == 31)
                    ins.then_inc(*self.mm_done.one())
                pe.wait_ge(*self.act_ready.at(2))
                pe.matmul(self.bank[3][0:E, 0:NC], w2[0:E, 0, :], hidden[0:E, 0, :], start=True, stop=True)\
                  .then_inc(*self.mm_done.one())
                pe.matmul(self.bank[4][0:NC, 0:E], hidden[0:E, 1, :], w2[0:E, 1, :], start=True, stop=True)\
                  .then_inc(*self.mm_done.one())

            @block.vector
            def _(dve):
                seq = seqs(dve, self.dve_order)
                dve.wait_ge(*self.mm_done.at(1))
                seq(dve.tensor_copy(posT[0:E], self.bank[0][0:E, 0:E].rearrange("p (j q) -> p j q", j=2)))
                for j in range(2):
                    x = kvT[0:E, j, :].rearrange("e (n p) -> e p n", p=16)
                    for half in range(2):
                        ps = slice(16 * half, 16 * half + 16)
                        dve.tensor_tensor(blocks[0:E, j, ps, :], x[:, :, half:half + NC],
                                          posT[0:E, j, ps].unsqueeze(2).broadcast_to([E, 16, NC]), ALU.add)\
                           .then_inc(*self.dve_ready.one())
                dve.wait_ge(*self.mm_done.at(4))
                dve.tensor_copy(kcT[0:E, :], self.bank[3][0:E, 0:NC]).then_inc(*self.dve_order.one())
                dve.wait_ge(*self.mm_done.at(5))
                dve.tensor_copy(vc[0:NC, :], self.bank[4][0:NC, 0:E]).then_inc(*self.dve_order.one())

            @block.sync
            def _(sp):
                self.w.feed(sp)
        self.top = o
        self.end_stage("nsa_compress")

        SLOPES = [2.0 ** (-8.0 * (h + 1) / H) for h in range(H)]
        dist = self.scratch[:]
        sel = self.take(H, T)
        win = self.take(H, 3 * P)
        cmp = self.take(NT, H, NC)
        seen = self.take(NT, NC)
        gsum = self.take(H)
        with nc.Block() as block:
            @block.gpsimd
            def _(pool):
                pool.iota(dist, [[-1, T]], base=3 * P, channel_multiplier=1, allow_small_or_imprecise_dtypes=True)\
                    .then_inc(*self.pool_ready.one())
                pool.iota(seen, [[P, NT], [-16, NC]], base=-31, channel_multiplier=1,
                          allow_small_or_imprecise_dtypes=True).then_inc(*self.pool_ready.one())
                seq = seqs(pool, self.pool_order)
                pool.wait_ge(*self.dve_ready.at(1))
                pool.affine_select(out=sel, in_=sel, compare_op=ALU.is_ge, fill=NEG, base=3 * P,
                                   pattern=[[0, H], [-1, T]], channel_multiplier=1).then_inc(*self.pool_order.one())
                seq(pool.affine_select(out=win, in_=win, compare_op=ALU.is_ge, fill=NEG, base=2 * P,
                                       pattern=[[0, H], [-1, 3 * P]], channel_multiplier=1))
                pool.affine_select(out=win, in_=win, compare_op=ALU.is_ge, fill=NEG, base=255 - 2 * P,
                                   pattern=[[0, H], [1, 3 * P]], channel_multiplier=-1)\
                    .then_inc(*self.pool_order.one())
                pool.affine_select(out=cmp, in_=cmp, compare_op=ALU.is_ge, fill=NEG, base=-31,
                                   pattern=[[P, NT], [0, H], [-16, NC]], channel_multiplier=1)\
                    .then_inc(*self.pool_order.one())
            @block.vector
            def _(dve):
                dve.wait_ge(*self.pool_ready.at(2))
                for h in range(H):
                    s = -8.0 * SLOPES[h]
                    dve.tensor_scalar(sel[:, h, :], dist, s, None, ALU.mult).then_inc(*self.dve_order.one())
                    dve.tensor_scalar(win[:, h, :], dist[:, P:], s, None, ALU.mult)\
                       .then_inc(*self.dve_order.one())
                    dve.tensor_scalar(cmp[:, :, h, :], seen, s, None, ALU.mult).then_inc(*self.dve_order.one())
                dve.wait_ge(*self.dve_order.all())
                dve.tensor_scalar(seen, seen, 0.0, None, ALU.is_ge).then_inc(*self.dve_ready.one())

            @block.sync
            def _(sp):
                self.w.feed(sp)
        self.end_stage("nsa_tables")

        units, groups = [], []
        part_of = {}
        q = 0
        for i in range(NT):
            qs = [self.nsa_qT[0:E, h, i * P:(i + 1) * P] for h in range(H)]
            kinds = [(0, 0, None), (1, 0, TM_VS), (2, max(0, i - 2), TM_VW)]
            for kind, b0, vcol in kinds:
                g = len(groups)
                part_of[g] = q
                for h in range(H):
                    if kind == 0:
                        part = dict(scores=(qs[h], kcT[0:E, :]), n=NC, table=cmp[:, i, h, :])
                        values = [vc[0:NC, :]]
                    else:
                        nk = (i + 1 - b0) * P
                        table = sel[:, h, T - nk:] if kind == 1 else win[:, h, 3 * P - nk:]
                        part = dict(scores=(qs[h], kvT[0:E, 1 + kind, b0 * P:(i + 1) * P]), n=nk, table=table)
                        values = [self.ns[:, b, vcol:vcol + E] for b in range(b0, i + 1)]
                    units.append(dict(parts=[part], values=values, cols=(h * E, (h + 1) * E), group=g))
                    if kind == 0:
                        units[-1]["mix"] = lambda dve, seq, q, rows, i=i: dve.tensor_tensor(
                            rows[0], rows[0], seen[:, i, :], ALU.mult)
                    q += 1

                def take_out(dve, seq, bank, i=i, kind=kind, g=g):
                    q0 = part_of[g]
                    y = self.y_nsa[:, i, :].rearrange("p (h e) -> p h e", h=H)
                    sums = bank[:, 0:MIX].rearrange("p (h e) -> p h e", h=H)
                    gate = self.ns[:, i, TM_NG:TM_NG + 12].rearrange("p (h c) -> p h c", c=3)[:, :, kind]
                    seq(dve.reciprocal(gsum, self.row_sum[:, q0:q0 + H]))
                    seq(dve.tensor_tensor(gsum, gsum, gate, ALU.mult))
                    by = gsum.unsqueeze(2).broadcast_to([P, H, E])
                    if kind == 0:
                        return dve.tensor_tensor(y, sums, by, ALU.mult)
                    part = self.scratch[:, 0:MIX].rearrange("p (h e) -> p h e", h=H)
                    seq(dve.tensor_tensor(part, sums, by, ALU.mult))
                    ins = dve.tensor_tensor(y, y, part, ALU.add)
                    if kind == 2:
                        seq(ins)
                        ins = dve.tensor_tensor(self.y_nsa[:, i, :], self.y_nsa[:, i, :],
                                                self.ns[:, i, TM_NZ:TM_NZ + MIX], ALU.mult)
                    return ins
                groups.append(take_out)
        self.attention("nsa", units, groups)
        self.top = keep + NT * MIX

    def spatial_gating(self):
        nc, a = self.nc, self.a
        keep = self.top
        gain, bias = self.take(MIX), self.take(MIX)
        w_rows = self.take(H, P)
        wT = self.take(H, P)
        vc, sq = self.take(NT, MIX), self.take(NT, MIX)
        mean, rstd = self.take(NT, H), self.take(NT, H)
        y = vc
        groups = lambda x: x.rearrange("p i (g c) -> p i g c", g=H)
        over = lambda x: x.unsqueeze(3).broadcast_to([P, NT, H, E])
        u, v, z = (self.sg[:, :, j * MIX:(j + 1) * MIX] for j in range(3))
        self.dve_ready.order_of(["var", "normed", "wT"] + [("y", i) for i in range(NT)])
        self.mm_done.order_of(["wT"] + [("mixed", g) for g in range(H)] + [("nsa", c) for c in range(2)]
                              + [("y", c) for c in range(2)])
        with nc.Block() as block:
            @block.scalar
            def _(act):
                act.dma_start(gain, a["sg_ln_gain"].broadcast_to([P, MIX])).then_inc(*self.params_landed.dma())
                act.dma_start(bias, a["sg_ln_bias"].broadcast_to([P, MIX])).then_inc(*self.params_landed.dma())
                act.dma_start(w_rows, a["sg_w_s"][0].rearrange("g t s -> t g s")).then_inc(*self.params_landed.dma())
                seq = self.order(act, self.act_order)
                act.wait_ge(*self.dve_ready.after("var"))
                seq(act.activation(rstd, rstd, ACT.Ln))
                act.activation(rstd, rstd, ACT.Exp, scale=-0.5).then_inc(*self.act_ready.one())
                for c in range(2):
                    act.wait_ge(*self.mm_done.after(("nsa", c)))
                    act.activation(self.ysT[:, 6 + c, :], self.bank[5 + c][:], ACT.Copy)\
                       .then_inc(*self.evac_act.one())
                for c in range(2):
                    act.wait_ge(*self.mm_done.after(("y", c)))
                    act.activation(self.ysT[:, 2 + c, :], self.bank[5 + c][:], ACT.Copy)\
                       .then_inc(*self.evac_act.one())

            @block.gpsimd
            def _(pool):
                pool.wait_ge(*self.params_landed.all_of_stage(48))
                pool.affine_select(out=w_rows, in_=w_rows, compare_op=ALU.is_ge, fill=0.0, base=0,
                                   pattern=[[0, H], [-1, P]], channel_multiplier=1)\
                    .then_inc(*self.pool_ready.one())

            @block.tensor
            def _(pe):
                def turn(src, first, name):
                    for c in range(2):
                        for i in range(NT):
                            ins = pe.transpose(self.bank[5 + c][:, i * P:(i + 1) * P],
                                               src[:, i, c * P:(c + 1) * P], self.ident[:])
                        ins.then_inc(*self.mm_done.step((name, c)))
                pe.wait_ge(*self.pool_ready.at(1))
                for g in range(H):
                    ins = pe.transpose(self.bank[0][:, g * P:(g + 1) * P], w_rows[:, g, :], self.ident[:])
                ins.then_inc(*self.mm_done.step("wT"))
                pe.wait_ge(*self.dve_ready.after("wT"))
                for g in range(H):
                    pe.matmul(self.bank[1 + g][:, 0:MIX], wT[:, g, :], v[:, :, g * E:(g + 1) * E],
                              start=True, stop=True).then_inc(*self.mm_done.step(("mixed", g)))
                turn(self.y_nsa, 6, "nsa")
                pe.wait_ge(*self.dve_ready.after(("y", NT - 1)))
                pe.wait_ge(*self.evac_act.at(2))
                turn(y, 2, "y")

            @block.vector
            def _(dve):
                seq = self.order(dve, self.dve_order)
                seq(dve.tensor_reduce(mean, groups(v), AX_X, ALU.add))
                seq(dve.tensor_scalar(mean, mean, 1.0 / E, None, ALU.mult))
                seq(dve.tensor_tensor(groups(vc), groups(v), over(mean), ALU.subtract))
                seq(dve.tensor_tensor(sq, vc, vc, ALU.mult))
                seq(dve.tensor_reduce(rstd, groups(sq), AX_X, ALU.add))
                dve.tensor_scalar(rstd, rstd, 1.0 / E, 1e-5, ALU.mult, ALU.add).then_inc(*self.dve_ready.step("var"))
                dve.wait_ge(*self.act_ready.at(1))
                seq(dve.tensor_tensor(groups(vc), groups(vc), over(rstd), ALU.mult))
                dve.wait_ge(*self.params_landed.all_of_stage(48))
                each = lambda row: row.unsqueeze(1).broadcast_to([P, NT, MIX])
                seq(dve.tensor_tensor(vc, vc, each(gain), ALU.mult))
                dve.tensor_tensor(v, vc, each(bias), ALU.add).then_inc(*self.dve_ready.step("normed"))
                dve.wait_ge(*self.mm_done.after("wT"))
                dve.tensor_copy(wT, self.bank[0][:].rearrange("p (g t) -> p g t", g=H))\
                   .then_inc(*self.dve_ready.step("wT"))
                dve.wait_ge(*self.dve_ready.after("normed"))
                for g in range(H):
                    dve.wait_ge(*self.mm_done.after(("mixed", g)))
                    cols = slice(g * E, (g + 1) * E)
                    b = self.par[:, PAR["sg_b_s"] + g:PAR["sg_b_s"] + g + 1]
                    dve.scalar_tensor_tensor(y[:, :, cols], self.bank[1 + g][:, 0:MIX].rearrange(
                        "p (i c) -> p i c", i=NT), b, u[:, :, cols], ALU.add, ALU.mult)\
                       .then_inc(*self.dve_order.one())
                dve.wait_ge(*self.dve_order.all())
                for i in range(NT):
                    dve.tensor_tensor(y[:, i, :], y[:, i, :], z[:, i, :], ALU.mult)\
                       .then_inc(*self.dve_ready.step(("y", i)))

            @block.sync
            def _(sp):
                self.w.feed(sp)
        self.top = keep
        self.end_stage("sg")

    def mixer_preparation(self):
        nc, a = self.nc, self.a
        CH = 64
        self.top = self.after_mixer_inputs
        self.until = self.take(P)
        self.beyond = self.take(P)
        self.strict = self.take(P)
        self.levels = self.take(6, P)
        self.chunk_of = self.take(2)
        self.beta = self.take(NT, H)
        self.g = self.take(NT, H)
        self.wa = self.take(NT, 2 * MIX)
        self.y_gdn = self.take(NT, MIX)
        self.y_rw = self.take(NT, MIX)
        keep = self.top
        acc = self.take(2, T)
        dtb, alog = self.take(H), self.take(H)
        low, small = self.take(NT, H), self.take(NT, H)
        w0a0 = self.take(2 * MIX)
        up = self.take(MIX)
        qkvT, rwT = self.qkvT, self.rwT
        landed = self.params_landed
        self.pool_ready.order_of(["masks", "zeros"])
        self.dve_ready.order_of(["shifted", "g0"] + [("conv", c) for c in range(6)] + [("wa", i) for i in range(NT)])
        self.act_ready.order_of(["tanh", "softplus", "alog"] + [("conv", c) for c in range(6)] + ["beta"]
                                + [("wa", i) for i in range(NT)])
        with nc.Block() as block:
            @block.gpsimd
            def _(pool):
                seq = self.order(pool, self.pool_order)
                pool.memset(qkvT[:, :, 0:3], 0.0).then_inc(*self.pool_order.one())
                seq(pool.memset(rwT[:, :, 0:1], 0.0))
                pool.memset(self.levels, 0.0).then_inc(*self.pool_order.one())
                pool.memset(self.until, 1.0).then_inc(*self.pool_order.one())
                pool.memset(self.beyond, 1.0).then_inc(*self.pool_order.one())
                pool.memset(self.strict, 1.0).then_inc(*self.pool_order.one())
                seq(pool.memset(self.chunk_of, 1.0))

                def select(v, base, pattern, cm, fill=0.0):
                    seq(pool.affine_select(out=v, in_=v, compare_op=ALU.is_ge, fill=fill, base=base, pattern=pattern,
                                           channel_multiplier=cm))
                for m, sign, base in ((self.until, 1, 0), (self.beyond, -1, -1), (self.strict, 1, -1)):
                    v = m.rearrange("p (b u) -> p b u", u=CH)
                    select(v, 0, [[-CH, 2], [0, CH]], 1)
                    select(v, CH - 1, [[CH, 2], [0, CH]], -1)
                    select(m, base, [[sign, P]], -sign)
                select(self.chunk_of, 0, [[-CH, 2]], 1)
                select(self.chunk_of, CH - 1, [[CH, 2]], -1)
                for l in range(6):
                    b = 1 << l
                    v = self.levels[:, l, :].rearrange("p (n u) -> p n u", u=2 * b)[:, :, b:2 * b]
                    n = P // (2 * b)
                    seq(pool.memset(v, 1.0))
                    select(v, 0, [[-2 * b, n], [0, b]], 1)
                    select(v, b - 1, [[2 * b, n], [0, b]], -1)
                pool.memset(self.scratch[0:1, 0:1], 0.0).then_inc(*self.pool_ready.step("masks"))
                pool.memset(self.scratch[0:1, 1:2], 0.0).then_inc(*self.pool_ready.step("zeros"))

            @block.scalar
            def _(act):
                act.dma_start(dtb, a["gdn_dt_bias"].broadcast_to([P, H])).then_inc(*landed.dma())
                act.dma_start(alog, a["gdn_a_log"].broadcast_to([P, H])).then_inc(*landed.dma())
                act.dma_start(w0a0[:, 0:MIX], a["rw_w0"].broadcast_to([P, MIX])).then_inc(*landed.dma())
                act.dma_start(w0a0[:, MIX:], a["rw_a0"].broadcast_to([P, MIX])).then_inc(*landed.dma())
                act.dma_start(up[0:E, :], a["rw_w_up"][0]).then_inc(*landed.dma())
                act.dma_start(up[E:P, :], a["rw_a_up"][0]).then_inc(*landed.dma())
                seq = self.order(act, self.act_order)
                act.wait_ge(*self.dve_ready.after("shifted"))
                act.activation(rwT[0:E, 6, 1:], rwT[0:E, 6, 1:], ACT.Tanh).then_inc(*self.act_ready.step("tanh"))
                act.wait_ge(*self.dve_ready.after("g0"))
                seq(act.activation(small, small, ACT.Exp, scale=-1.0))
                act.activation(small, small, ACT.Ln, bias=1.0).then_inc(*self.act_ready.step("softplus"))
                act.wait_ge(*landed.all_of_stage(96))
                act.activation(alog, alog, ACT.Exp).then_inc(*self.act_ready.step("alog"))
                for c in range(6):
                    act.wait_ge(*self.dve_ready.after(("conv", c)))
                    act.activation(qkvT[:, c, 3:], acc[:, c % 2, :], ACT.Silu)\
                       .then_inc(*self.act_ready.step(("conv", c)))
                act.activation(self.beta, self.ab[:, :, H:], ACT.Sigmoid).then_inc(*self.act_ready.step("beta"))
                for i in range(NT):
                    act.wait_ge(*self.dve_ready.after(("wa", i)))
                    act.activation(self.wa[:, i, :], self.wa[:, i, :], ACT.Sigmoid)\
                       .then_inc(*self.act_ready.step(("wa", i)))

            @block.tensor
            def _(pe):
                pe.wait_ge(*self.act_ready.after("tanh"))
                pe.wait_ge(*landed.all_of_stage(96))
                for i in range(NT):
                    pe.matmul(self.bank[i][:, 0:MIX], rwT[0:E, 6, 1 + i * P:1 + (i + 1) * P], up[0:E, :],
                              start=True, stop=True)
                    pe.matmul(self.bank[i + 4][:, 0:MIX], rwT[E:P, 6, 1 + i * P:1 + (i + 1) * P], up[E:P, :],
                              start=True, stop=True).then_inc(*self.mm_done.one())

            @block.vector
            def _(dve):
                seq = self.order(dve, self.dve_order)
                dve.wait_ge(*self.pool_ready.after("zeros"))
                for c in (6, 0, 1, 2, 3, 4, 5):
                    mu = self.par[:, PAR["rw_mu"] + c:PAR["rw_mu"] + c + 1]
                    seq(dve.tensor_tensor(acc[:, 0, :], rwT[:, c, 0:T], rwT[:, c, 1:], ALU.subtract))
                    ins = dve.scalar_tensor_tensor(rwT[:, c, 1:], acc[:, 0, :], mu, rwT[:, c, 1:], ALU.mult, ALU.add)
                    if c == 6:
                        ins.then_inc(*self.dve_ready.step("shifted"))
                        dve.wait_ge(*self.dve_ready.after("shifted"))
                    else:
                        seq(ins)
                dve.wait_ge(*landed.all_of_stage(96))
                seq(dve.tensor_tensor(low, self.ab[:, :, 0:H], dtb.unsqueeze(1).broadcast_to([P, NT, H]), ALU.add))
                dve.scalar_tensor_tensor(small, low, -1.0, low, ALU.mult, ALU.max).then_inc(*self.dve_ready.step("g0"))
                dve.wait_ge(*self.dve_ready.after("g0"))
                seq(dve.tensor_scalar(low, low, 0.0, None, ALU.max))
                dve.wait_ge(*self.act_ready.after("alog"))
                seq(dve.tensor_tensor(low, low, small, ALU.add))
                seq(dve.tensor_tensor(low, low, alog.unsqueeze(1).broadcast_to([P, NT, H]), ALU.mult))
                seq(dve.tensor_scalar(self.g, low, -1.0, None, ALU.mult))
                for c in range(6):
                    if c >= 2:
                        dve.wait_ge(*self.act_ready.after(("conv", c - 2)))
                    w = lambda j: self.par[:, PAR["gdn_conv"] + 6 * j + c:PAR["gdn_conv"] + 6 * j + c + 1]
                    seq(dve.tensor_scalar(acc[:, c % 2, :], qkvT[:, c, 0:T], w(0), None, ALU.mult))
                    for j in range(1, 4):
                        ins = dve.scalar_tensor_tensor(acc[:, c % 2, :], qkvT[:, c, j:j + T], w(j), acc[:, c % 2, :],
                                                       ALU.mult, ALU.add)
                        if j < 3:
                            seq(ins)
                    ins.then_inc(*self.dve_ready.step(("conv", c)))
                for i in range(NT):
                    dve.wait_ge(*self.mm_done.at(i + 1))
                    dve.tensor_tensor(self.wa[:, i, 0:MIX], self.bank[i][:, 0:MIX], w0a0[:, 0:MIX], ALU.add)\
                       .then_inc(*self.dve_order.one())
                    dve.tensor_tensor(self.wa[:, i, MIX:], self.bank[i + 4][:, 0:MIX], w0a0[:, MIX:], ALU.add)\
                       .then_inc(*self.dve_ready.step(("wa", i)))

            @block.sync
            def _(sp):
                self.w.feed(sp)
        self.top = keep
        self.end_stage("prep")

    def recurrence(self, kind):
        nc, a = self.nc, self.a
        gdn = kind == "gdn"
        keep = self.top
        CH = 64
        LEVELS = 6
        hd = lambda x: x.rearrange("p (h e) -> p h e", h=H)
        over = lambda x: x.unsqueeze(2).broadcast_to([P, H, E])
        y = self.y_gdn if gdn else self.y_rw
        z = self.z_gdn if gdn else self.z_rw
        srcT = self.qkvT if gdn else self.rwT
        first = 3 if gdn else 1
        F = [self.hT[0:E, j, :].rearrange("e (h t) -> e h t", h=H) for j in range(4)]
        head = lambda x: x.rearrange("p (h t) -> p h t", h=H)
        LT, M, T1, TT = (head(self.hT[:, 4 + j, :]) for j in range(4))
        X = self.take(H, P)
        OB = self.take(H, P)
        raw = self.take(3, MIX)
        q, k, v = (raw[:, j, :] for j in range(3))
        U, Un = self.take(MIX), self.take(MIX)
        WT = self.take(H, P)
        S, Sd = self.take(MIX), self.take(MIX)
        dec = self.take(2 * H)
        sq, ss = self.take(2 * MIX), self.take(2 * H)
        if gdn:
            D = self.take(H, P)
            eg, gc = self.take(2 * H), self.take(H)
            kn, kb, qn, q_in, kbg, vb, ko = (self.take(MIX) for _ in range(7))
            fm_src = [kn, kb, qn, q_in]
            w_tm, state_ops, o_ops = kbg, [(ko, Un)], [(OB, Un)]
            norm_w = self.take(E)
        else:
            GT, HK = self.take(H, P), self.take(H, P)
            ld, cm, ec, er, en, ep = (self.take(MIX) for _ in range(6))
            kk, kp, b = (self.take(MIX) for _ in range(3))
            A, B, K, R, Bh, Kh = ep, sq[:, 0:MIX], sq[:, MIX:], ec, b, er
            fm_src = [B, A, R, K]
            w_tm, state_ops, o_ops = A, [(Bh, Un), (Kh, v)], [(OB, Un), (HK, v)]
            GV = cm
            bonus = self.take(NT, MIX)
            rows = self.take(5, MIX)
            k_k, k_a, r_k, gn_gain, gn_bias = (rows[:, j, :] for j in range(5))
        post = self.take(NT, H)
        mean = self.take(NT, H)
        landed = self.params_landed
        n_params = 1 if gdn else 5

        pe_steps, dve_steps, act_steps = [], ["S0"], []
        for i in range(NT):
            pe_steps += [(i, "in"), (i, "cum")] + [(i, "fm", j) for j in range(4)]
            pe_steps += [(i, "LT"), (i, "OB")] + ([] if gdn else [(i, "GT"), (i, "HK")]) + [(i, "T0")]
            for l in range(1, LEVELS):
                pe_steps += [(i, "X", l)] + [(i, "dT", l)] * (l < LEVELS - 1) + [(i, "dTT", l)]
            pe_steps += ([] if gdn else [(i, "GV")]) + [(i, "U"), (i, "WT")]
            for c in range(2):
                pe_steps += [(i, "WS", c), (i, "O", c), (i, "S", c)]
            dve_steps += ([(i, "gc"), (i, "D")] if gdn else [(i, "ld"), (i, "cm")]) + [(i, "ss")]
            dve_steps += [(i, "src", j) for j in range(4)] + [(i, "F", 1), (i, "F", 3)]
            dve_steps += [(i, "LT"), (i, "OB")] + ([] if gdn else [(i, "GT"), (i, "HK")]) + [(i, "TT", 0)]
            for l in range(1, LEVELS):
                dve_steps += [(i, "M", l)] + [(i, "T", l)] * (l < LEVELS - 1) + [(i, "TT", l)]
            dve_steps += ([] if gdn else [(i, "GV")]) + [(i, "U"), (i, "WT")]
            for c in range(2):
                dve_steps += [(i, "Un", c), (i, "S", c)]
            act_steps += [(i, "raw"), (i, "e"), (i, "eD"), (i, "rs"), (i, "F", 0), (i, "F", 2), (i, "T0")]
            act_steps += [(i, "X", l) for l in range(1, LEVELS)] + [(i, "y")]
        dve_steps += ["ss", "y"]
        act_steps += ["rs"] + [("out", c) for c in range(2)]
        pe_steps += [("out", c) for c in range(2)]
        pe_done, dve_done, act_done = self.mm_done, self.dve_ready, self.act_ready
        pe_done.order_of(pe_steps)
        dve_done.order_of(dve_steps)
        act_done.order_of(act_steps)
        bank = [b_ for b_ in self.bank]

        with nc.Block() as block:
            @block.tensor
            def _(pe):
                if gdn:
                    pass
                for i in range(NT):
                    ts = slice(first + i * P, first + (i + 1) * P)
                    if i:
                        pe.wait_ge(*act_done.after((i - 1, "y")))
                        pe.wait_ge(*dve_done.after((i - 1, "S", 1)))
                    for c in range(6):
                        ins = pe.transpose(bank[c // 4][:, c % 4 * P:c % 4 * P + P], srcT[:, c, ts], self.ident[:])
                    ins.then_inc(*pe_done.step((i, "in")))
                    if gdn:
                        pe.matmul(bank[2][:, 0:H], self.until, self.g[:, i, :], start=True, stop=True)
                        pe.matmul(bank[2][:, H:2 * H], self.beyond, self.g[:, i, :], start=True, stop=True)
                        for h in range(H):
                            gh = self.g[:, i, h:h + 1]
                            pe.matmul(bank[2][0:E, 8 + 2 * h:10 + 2 * h], gh.broadcast_to([P, E]), self.chunk_of,
                                      start=True, stop=True)
                            ins = pe.matmul(bank[3][:, h * P:(h + 1) * P], gh.broadcast_to([P, P]), self.until,
                                            start=True, stop=True)
                    else:
                        pe.wait_ge(*dve_done.after((i, "ld")))
                        pe.matmul(bank[2][:, 0:MIX], self.until, ld, start=True, stop=True)
                        pe.matmul(bank[2][:, MIX:], self.beyond, ld, start=True, stop=True)
                        for h in range(H):
                            ins = pe.matmul(bank[3][0:E, 2 * h:2 * h + 2], ld[:, h * E:(h + 1) * E], self.chunk_of,
                                            start=True, stop=True)
                    ins.then_inc(*pe_done.step((i, "cum")))
                    for j in range(4):
                        pe.wait_ge(*dve_done.after((i, "src", j)))
                        for h in range(H):
                            ins = pe.transpose(bank[4 + j][0:E, h * P:(h + 1) * P],
                                               fm_src[j][:, h * E:(h + 1) * E], self.ident[:])
                        ins.then_inc(*pe_done.step((i, "fm", j)))
                    pe.wait_ge(*act_done.after((i, "F", 2)))
                    pe.wait_ge(*dve_done.after((i, "F", 3)))
                    grams = [("LT", 0, 1, 4), ("OB", 0, 2, 5)] + ([] if gdn else [("GT", 3, 1, 6), ("HK", 3, 2, 7)])
                    for name, l, r, b_ in grams:
                        for h in range(H):
                            ins = pe.matmul(bank[b_][:, h * P:(h + 1) * P], F[l][:, h, :], F[r][:, h, :],
                                            start=True, stop=True)
                        ins.then_inc(*pe_done.step((i, name)))
                    pe.wait_ge(*dve_done.after((i, "TT", 0)))
                    for h in range(H):
                        ins = pe.transpose(bank[0][:, h * P:(h + 1) * P], TT[:, h, :], self.ident[:])
                    ins.then_inc(*pe_done.step((i, "T0")))
                    for l in range(1, LEVELS):
                        pe.wait_ge(*dve_done.after((i, "M", l)))
                        if l == 1:
                            pe.wait_ge(*act_done.after((i, "T0")))
                        else:
                            pe.wait_ge(*dve_done.after((i, "TT", l - 1)))
                        for h in range(H):
                            ins = pe.matmul(bank[0][:, h * P:(h + 1) * P], M[:, h, :], T1[:, h, :],
                                            start=True, stop=True)
                        ins.then_inc(*pe_done.step((i, "X", l)))
                        pe.wait_ge(*act_done.after((i, "X", l)))
                        if l < LEVELS - 1:
                            for h in range(H):
                                ins = pe.matmul(bank[1][:, h * P:(h + 1) * P], TT[:, h, :], X[:, h, :],
                                                start=True, stop=True)
                            ins.then_inc(*pe_done.step((i, "dT", l)))
                        for h in range(H):
                            ins = pe.matmul(bank[2][:, h * P:(h + 1) * P], X[:, h, :], TT[:, h, :],
                                            start=True, stop=True)
                        ins.then_inc(*pe_done.step((i, "dTT", l)))
                    pe.wait_ge(*dve_done.after((i, "TT", LEVELS - 1)))
                    if not gdn:
                        for h in range(H):
                            ins = pe.matmul(bank[3][:, h * E:(h + 1) * E], GT[:, h, :], v[:, h * E:(h + 1) * E],
                                            start=True, stop=True)
                        ins.then_inc(*pe_done.step((i, "GV")))
                        pe.wait_ge(*dve_done.after((i, "GV")))
                    rhs = vb if gdn else GV
                    for h in range(H):
                        ins = pe.matmul(bank[4][:, h * E:(h + 1) * E], TT[:, h, :], rhs[:, h * E:(h + 1) * E],
                                        start=True, stop=True)
                    ins.then_inc(*pe_done.step((i, "U")))
                    for h in range(H):
                        ins = pe.matmul(bank[5][0:E, h * P:(h + 1) * P], w_tm[:, h * E:(h + 1) * E], TT[:, h, :],
                                        start=True, stop=True)
                    ins.then_inc(*pe_done.step((i, "WT")))
                    pe.wait_ge(*dve_done.after((i, "WT")))
                    for c in range(2):
                        ps = slice(c * CH, (c + 1) * CH)
                        if c:
                            pe.wait_ge(*dve_done.after((i, "S", 0)))
                        elif i == 0:
                            pe.wait_ge(*dve_done.after("S0"))
                        for h in range(H):
                            ins = pe.matmul(bank[6][ps, h * E:(h + 1) * E], WT[0:E, h, ps], S[0:E, h * E:(h + 1) * E],
                                            start=True, stop=True)
                        ins.then_inc(*pe_done.step((i, "WS", c)))
                        pe.wait_ge(*dve_done.after((i, "Un", c)))
                        for h in range(H):
                            hs = slice(h * E, (h + 1) * E)
                            RT = F[3] if gdn else F[2]
                            pe.matmul(bank[7][ps, hs], RT[:, h, ps], S[0:E, hs], start=True, stop=False)
                            for n, (l, r) in enumerate(o_ops):
                                ins = pe.matmul(bank[7][ps, hs], l[:, h, ps], r[:, hs], start=False,
                                                stop=n == len(o_ops) - 1)
                        ins.then_inc(*pe_done.step((i, "O", c)))
                        for h in range(H):
                            hs = slice(h * E, (h + 1) * E)
                            for n, (l, r) in enumerate(state_ops):
                                ins = pe.matmul(bank[3][0:E, hs], l[ps, hs], r[ps, hs], start=n == 0,
                                                stop=n == len(state_ops) - 1)
                        ins.then_inc(*pe_done.step((i, "S", c)))
                pe.wait_ge(*dve_done.after("y"))
                for c in range(2):
                    for i in range(NT):
                        ins = pe.transpose(bank[c][:, i * P:(i + 1) * P], y[:, i, c * P:(c + 1) * P], self.ident[:])
                    ins.then_inc(*pe_done.step(("out", c)))

            @block.scalar
            def _(act):
                if gdn:
                    act.dma_start(norm_w, a["gdn_norm"].broadcast_to([P, E])).then_inc(*landed.dma())
                else:
                    for dst, n in ((k_k, "rw_k_k"), (k_a, "rw_k_a"), (gn_gain, "rw_gn_gain"), (gn_bias, "rw_gn_bias")):
                        act.dma_start(dst, a[n].broadcast_to([P, MIX])).then_inc(*landed.dma())
                    act.dma_start(r_k, a["rw_r_k"].rearrange("l h e -> l (h e)").broadcast_to([P, MIX]))\
                       .then_inc(*landed.dma())
                seq = self.order(act, self.act_order)
                for i in range(NT):
                    act.wait_ge(*pe_done.after((i, "in")))
                    flat = raw.rearrange("p j c -> p (j c)")
                    if i:
                        act.wait_ge(*dve_done.after((i - 1, "S", 1)))
                    act.activation(flat[:, 0:512], bank[0][:], ACT.Copy).then_inc(*self.act_order.one())
                    seq(act.activation(flat[:, 512:], bank[1][:, 0:MIX], ACT.Copy))
                    act.activation(self.scratch[:, 0:1], self.ones[:, 0:1], ACT.Copy)\
                       .then_inc(*act_done.step((i, "raw")))
                    act.wait_ge(*pe_done.after((i, "cum")))
                    if gdn:
                        act.activation(eg, bank[2][:, 0:2 * H], ACT.Exp).then_inc(*self.act_order.one())
                        seq(act.activation(dec[0:E, :], bank[2][0:E, 8:8 + 2 * H], ACT.Exp))
                    else:
                        act.activation(ec, bank[2][:, 0:MIX], ACT.Exp).then_inc(*self.act_order.one())
                        act.activation(en, bank[2][:, 0:MIX], ACT.Exp, scale=-1.0).then_inc(*self.act_order.one())
                        act.activation(er, bank[2][:, MIX:], ACT.Exp).then_inc(*self.act_order.one())
                        seq(act.activation(dec[0:E, :], bank[3][0:E, 0:2 * H], ACT.Exp))
                    act.activation(self.scratch[:, 0:1], self.ones[:, 0:1], ACT.Copy)\
                       .then_inc(*act_done.step((i, "e")))
                    act.wait_ge(*dve_done.after((i, "D" if gdn else "cm")))
                    if gdn:
                        act.activation(D, D, ACT.Exp).then_inc(*act_done.step((i, "eD")))
                    else:
                        act.activation(ep, cm, ACT.Exp).then_inc(*act_done.step((i, "eD")))
                    n = 2 * H if gdn else H
                    act.wait_ge(*dve_done.after((i, "ss")))
                    seq(act.activation(ss[:, 0:n], ss[:, 0:n], ACT.Ln))
                    act.activation(ss[:, 0:n], ss[:, 0:n], ACT.Exp, scale=-0.5).then_inc(*act_done.step((i, "rs")))
                    for j in (0, 2):
                        act.wait_ge(*pe_done.after((i, "fm", j)))
                        act.activation(F[j], head(bank[4 + j][0:E, :]), ACT.Copy).then_inc(*act_done.step((i, "F", j)))
                    act.wait_ge(*pe_done.after((i, "T0")))
                    act.activation(T1, head(bank[0][:]), ACT.Copy).then_inc(*act_done.step((i, "T0")))
                    for l in range(1, LEVELS):
                        act.wait_ge(*pe_done.after((i, "X", l)))
                        if l > 1:
                            act.wait_ge(*pe_done.after((i, "dTT", l - 1)))
                        act.activation(X, head(bank[0][:]), ACT.Copy).then_inc(*act_done.step((i, "X", l)))
                    act.wait_ge(*pe_done.after((i, "O", 1)))
                    act.activation(y[:, i, :], bank[7][:, 0:MIX], ACT.Copy).then_inc(*act_done.step((i, "y")))
                act.wait_ge(*dve_done.after("ss"))
                seq(act.activation(post, post, ACT.Ln))
                act.activation(post, post, ACT.Exp, scale=-0.5).then_inc(*act_done.step("rs"))
                for c in range(2):
                    act.wait_ge(*pe_done.after(("out", c)))
                    act.activation(self.ysT[:, (0 if gdn else 4) + c, :], bank[c][:], ACT.Copy)\
                       .then_inc(*act_done.step(("out", c)))

            @block.vector
            def _(dve):
                seq = self.order(dve, self.dve_order)

                def fin(ins, name):
                    ins.then_inc(*dve_done.step(name))
                    dve.wait_ge(*dve_done.after(name))
                tt, ts_, stt = dve.tensor_tensor, dve.tensor_scalar, dve.scalar_tensor_tensor
                dve.memset(Un, 0.0).then_inc(*self.dve_order.one())
                fin(dve.memset(S[0:E, :], 0.0), "S0")
                dve.wait_ge(*landed.all_of_stage(16 * n_params))
                many = lambda m: m.unsqueeze(1).broadcast_to([P, H, P])
                for i in range(NT):
                    if gdn:
                        dve.wait_ge(*pe_done.after((i, "cum")))
                        dve.wait_ge(*act_done.after((i, "e")))
                        fin(dve.tensor_copy(gc, bank[2][:, 0:H]), (i, "gc"))
                        for h in range(H):
                            ins = ts_(D[:, h, :], bank[3][:, h * P:(h + 1) * P], gc[:, h:h + 1], 0.0, ALU.subtract,
                                      ALU.min)
                            if h < H - 1:
                                ins.then_inc(*self.dve_order.one())
                        dve.wait_ge(*self.dve_order.all())
                        fin(ins, (i, "D"))
                    else:
                        if i:
                            dve.wait_ge(*pe_done.after((i - 1, "S", 1)))
                        fin(ts_(ld, self.wa[:, i, 0:MIX], -math.exp(-0.5), None, ALU.mult), (i, "ld"))
                        dve.wait_ge(*pe_done.after((i, "cum")))
                        dve.wait_ge(*act_done.after((i, "e")))
                        fin(tt(cm, bank[2][:, 0:MIX], ld, ALU.subtract), (i, "cm"))
                    dve.wait_ge(*act_done.after((i, "raw")))
                    if gdn:
                        flat = raw.rearrange("p j c -> p (j c)")[:, 0:512]
                        seq(tt(sq, flat, flat, ALU.mult))
                        seq(dve.tensor_reduce(ss, sq.rearrange("p (h e) -> p h e", e=E), AX_X, ALU.add))
                        fin(ts_(ss, ss, 1e-6, None, ALU.add), (i, "ss"))
                        dve.wait_ge(*act_done.after((i, "rs")))
                        beta, e_until, e_beyond = self.beta[:, i, :], eg[:, 0:H], eg[:, H:]
                        ins = tt(hd(kn), hd(k), over(ss[:, H:]), ALU.mult)
                        fin(ins, (i, "src", 0))
                        fin(tt(hd(kb), hd(kn), over(beta), ALU.mult), (i, "src", 1))
                        seq(ts_(ss[:, 0:H], ss[:, 0:H], E ** -0.5, None, ALU.mult))
                        fin(tt(hd(qn), hd(q), over(ss[:, 0:H]), ALU.mult), (i, "src", 2))
                        fin(tt(hd(q_in), hd(qn), over(e_until), ALU.mult), (i, "src", 3))
                        tt(hd(kbg), hd(kb), over(e_until), ALU.mult).then_inc(*self.dve_order.one())
                        tt(hd(vb), hd(v), over(beta), ALU.mult).then_inc(*self.dve_order.one())
                        tt(hd(ko), hd(kn), over(e_beyond), ALU.mult).then_inc(*self.dve_order.one())
                    else:
                        av = self.wa[:, i, MIX:]
                        seq(tt(kk, k, k_k, ALU.mult))
                        seq(tt(sq[:, 0:MIX], kk, kk, ALU.mult))
                        seq(dve.tensor_reduce(ss[:, 0:H], hd(sq[:, 0:MIX]), AX_X, ALU.add))
                        fin(ts_(ss[:, 0:H], ss[:, 0:H], 1e-6, None, ALU.add), (i, "ss"))
                        seq(stt(kp, av, -1.0, k_a, ALU.add, ALU.mult))
                        seq(stt(kp, kp, 1.0, k, ALU.add, ALU.mult))
                        seq(tt(b, q, kp, ALU.mult))
                        seq(tt(b, b, r_k, ALU.mult))
                        seq(dve.tensor_reduce(mean[:, 0, :], hd(b), AX_X, ALU.add))
                        seq(tt(hd(bonus[:, i, :]), hd(v), over(mean[:, 0, :]), ALU.mult))
                        dve.wait_ge(*act_done.after((i, "rs")))
                        seq(tt(hd(kk), hd(kk), over(ss[:, 0:H]), ALU.mult))
                        seq(tt(b, kk, av, ALU.mult))
                        fin(tt(B, b, en, ALU.mult), (i, "src", 0))
                        fin(tt(A, kk, ep, ALU.mult), (i, "src", 1))
                        fin(tt(R, q, ec, ALU.mult), (i, "src", 2))
                        fin(tt(K, kp, en, ALU.mult), (i, "src", 3))
                        tt(Bh, b, er, ALU.mult).then_inc(*self.dve_order.one())
                        dve.wait_ge(*self.dve_order.all())
                        tt(Kh, kp, er, ALU.mult).then_inc(*self.dve_order.one())
                    for j in (1, 3):
                        dve.wait_ge(*pe_done.after((i, "fm", j)))
                        dve.tensor_copy(F[j], head(bank[4 + j][0:E, :])).then_inc(*dve_done.step((i, "F", j)))
                    dve.wait_ge(*pe_done.after((i, "LT")))
                    if gdn:
                        fin(tt(LT, head(bank[4][:]), D, ALU.mult), (i, "LT"))
                        dve.wait_ge(*pe_done.after((i, "OB")))
                        seq(tt(D, D, many(self.until), ALU.mult))
                        fin(tt(OB, head(bank[5][:]), D, ALU.mult), (i, "OB"))
                    else:
                        fin(dve.tensor_copy(LT, head(bank[4][:])), (i, "LT"))
                        for name, dst, b_, mask in (("OB", OB, 5, self.until), ("GT", GT, 6, self.strict),
                                                    ("HK", HK, 7, self.until)):
                            dve.wait_ge(*pe_done.after((i, name)))
                            fin(tt(dst, head(bank[b_][:]), many(mask), ALU.mult), (i, name))
                    seq(tt(M, LT, many(self.levels[:, 0, :]), ALU.mult))
                    fin(tt(TT, many(self.ident[:]), M, ALU.subtract), (i, "TT", 0))
                    for l in range(1, LEVELS):
                        if l > 1:
                            dve.wait_ge(*pe_done.after((i, "X", l - 1)))
                        fin(tt(M, LT, many(self.levels[:, l, :]), ALU.mult), (i, "M", l))
                        dve.wait_ge(*pe_done.after((i, "dTT", l)))
                        if l < LEVELS - 1:
                            fin(tt(T1, T1, head(bank[1][:]), ALU.subtract), (i, "T", l))
                        fin(tt(TT, TT, head(bank[2][:]), ALU.subtract), (i, "TT", l))
                    if not gdn:
                        dve.wait_ge(*pe_done.after((i, "GV")))
                        fin(dve.tensor_copy(GV, bank[3][:, 0:MIX]), (i, "GV"))
                    dve.wait_ge(*pe_done.after((i, "U")))
                    fin(ts_(U, bank[4][:, 0:MIX], 1.0 if gdn else -1.0, None, ALU.mult), (i, "U"))
                    dve.wait_ge(*pe_done.after((i, "WT")))
                    fin(ts_(WT[0:E], head(bank[5][0:E, :]), -1.0, None, ALU.mult), (i, "WT"))
                    for c in range(2):
                        ps = slice(c * CH, (c + 1) * CH)
                        dve.wait_ge(*pe_done.after((i, "WS", c)))
                        fin(tt(Un[ps, :], bank[6][ps, 0:MIX], U[ps, :], ALU.add), (i, "Un", c))
                        by = dec[0:E, :].rearrange("e (h c) -> e h c", c=2)[:, :, c].unsqueeze(2)\
                            .broadcast_to([E, H, E])
                        seq(tt(hd(Sd[0:E, :]), hd(S[0:E, :]), by, ALU.mult))
                        dve.wait_ge(*pe_done.after((i, "S", c)))
                        fin(tt(S[0:E, :], Sd[0:E, :], bank[3][0:E, 0:MIX], ALU.add), (i, "S", c))
                dve.wait_ge(*act_done.after((NT - 1, "y")))
                g4 = lambda x: x.rearrange("p i (h e) -> p i h e", h=H)
                o4 = lambda x: x.unsqueeze(3).broadcast_to([P, NT, H, E])
                square = self.hT[:, 0:2, :].rearrange("p a (b c) -> p (a b) c", c=MIX)
                if not gdn:
                    seq(dve.tensor_reduce(mean, g4(y), AX_X, ALU.add))
                    seq(ts_(mean, mean, 1.0 / E, None, ALU.mult))
                    seq(tt(g4(y), g4(y), o4(mean), ALU.subtract))
                seq(tt(square, y, y, ALU.mult))
                seq(dve.tensor_reduce(post, g4(square), AX_X, ALU.add))
                fin(ts_(post, post, 1.0 / E, 1e-6 if gdn else 64e-5, ALU.mult, ALU.add), "ss")
                dve.wait_ge(*act_done.after("rs"))
                seq(tt(g4(y), g4(y), o4(post), ALU.mult))
                if gdn:
                    w = norm_w.unsqueeze(1).broadcast_to([P, NT * H, E])
                    y3 = y.rearrange("p i (h e) -> p (i h) e", h=H)
                    seq(tt(y3, y3, w, ALU.mult))
                else:
                    each = lambda row: row.unsqueeze(1).broadcast_to([P, NT, MIX])
                    seq(tt(y, y, each(gn_gain), ALU.mult))
                    seq(tt(y, y, each(gn_bias), ALU.add))
                    seq(tt(y, y, bonus, ALU.add))
                fin(tt(y, y, z, ALU.mult), "y")

            @block.sync
            def _(sp):
                self.w.feed(sp)
        self.top = keep
        self.end_stage(kind)

    def gated_sum(self, name, mixT, plan):
        tiles = []
        gates = self.take(2, T)
        readers = {}
        for c in range(ND):
            takes, frees, branches = plan(c)
            for j, (gate_pairs, branch_pairs, bias) in enumerate(branches):
                buf = len(readers) % 2
                g, b = len(tiles), len(tiles) + 1
                more = dict(takes=takes) if j == 0 else {}
                tiles.append(dict(
                    by="act", shape=(P, T), pairs=gate_pairs, needs=[readers[len(readers) - 2]] if len(readers) >= 2 else [],
                    empty=lambda e, seq, ps, buf=buf, bias=bias: e.activation(
                        gates[:, buf, :], ps, ACT.Sigmoid, bias=bias), **more))

                def add(e, seq, ps, c=c, j=j, buf=buf):
                    if j == 0:
                        return e.tensor_tensor(mixT[:, c, :], ps, gates[:, buf, :], ALU.mult)
                    seq(e.tensor_tensor(self.scratch[:], ps, gates[:, buf, :], ALU.mult))
                    return e.tensor_tensor(mixT[:, c, :], mixT[:, c, :], self.scratch[:], ALU.add)
                tiles.append(dict(by="dve", shape=(P, T), pairs=branch_pairs, needs=[g] + [b - 2] * (j > 0),
                                  empty=add))
                readers[len(readers)] = b
            tiles[-1]["frees"] = frees
        self.products(name, tiles)
        self.top -= 2 * T

    def merge(self):
        mixT = self.take(ND, T)
        hT, ysT = self.hT, self.ysT

        def plan(c):
            gk, bk = ("gate", c), ("branch", c)
            branches = []
            for i in range(4):
                branches.append((lambda ch, i=i: [(ch[gk][:, i * ND + k, :], hT[:, k, :]) for k in range(ND)],
                                 lambda ch, i=i: [(ch[bk][:, 2 * i + k, :], ysT[:, 2 * i + k, :]) for k in range(2)],
                                 0.0))
            return [(gk, P), (bk, P)], 2, branches
        self.gated_sum("merge", mixT, plan)
        self.add_products("out", lambda c: ("out", c), mixT, None)

    def add_products(self, name, key, srcT, scale):
        tiles = []
        for c in range(ND):
            k_ = key(c // 4)

            def add(e, seq, ps, c=c):
                x = self.xT[:, c, :]
                if scale is None:
                    return e.tensor_tensor(x, ps, x, ALU.add)
                return e.scalar_tensor_tensor(x, ps, scale(c), x, ALU.mult, ALU.add)
            tiles.append(dict(by="dve", shape=(P, T), empty=add, pairs=lambda ch, c=c, k_=k_: [
                (ch[k_][:, k, c % 4 * P:c % 4 * P + P], srcT[:, k, :]) for k in range(ND)]))
            if c % 4 == 0:
                tiles[-1]["takes"] = [(k_, 512)]
            if c % 4 == 3:
                tiles[-1]["frees"] = 1
        self.products(name, tiles)

    def layer_tables(self):
        nc, a = self.nc, self.a
        R = E // 4 // 2
        self.cos, self.sin = self.take(NT, R), self.take(NT, R)
        self.cond = self.take(ND)
        self.mod = self.take(48)
        self.gain_m, self.gain_f = self.take(ND), self.take(ND)
        self.gain_a, self.gain_b = self.take(2, 2, E), self.take(2, 2, E)
        self.subln = self.take(2, P)
        self.neg_lam = self.take(2)
        self.near = self.take(3 * P)
        self.mid = self.take(7 * P)
        self.far = self.take(4 * P)
        keep = self.top
        pos_i = self.nc_pos
        pos, ang, n = self.take(NT), self.take(NT, R), self.take(NT, R)
        lam = self.take(2, 2, 2, E)
        lsum = self.take(4)
        dist = self.take(7 * P)
        dist_i = self.nc_dist
        landed = self.params_landed
        freq = [float(np.float32(500000.0) ** np.float32(-2.0 * j / (2 * R))) for j in range(R)]
        MAGIC = 1.5 * 2 ** 23
        C1 = 6.28125
        C2 = float(np.float32(2 * math.pi - C1))
        PI = float(np.nextafter(np.float32(math.pi), np.float32(0)))
        LAM = [0.8 - 0.6 * math.exp(-0.3 * l) for l in range(2)]
        self.pool_ready.order_of(["dist", "masks"])
        self.dve_ready.order_of(["angles", "lam_sums", "near", "mods"])
        self.act_ready.order_of(["sin", "lam", "cond"])
        with nc.Block() as block:
            @block.scalar
            def _(act):
                act.dma_start(pos_i[:], a["positions_2"].rearrange("b (i p) -> p (b i)", p=P),
                              allow_slow_non_contiguous=True).then_inc(*landed.dma())
                for l in range(2):
                    for dst, name in ((self.gain_a, "qk_gain_a_2"), (self.gain_b, "qk_gain_b_2")):
                        act.dma_start(dst[:, l], a[name][l:l + 1].rearrange("l a e -> l (a e)")
                                      .broadcast_to([P, 2 * E])).then_inc(*landed.dma())
                    act.dma_start(self.subln[:, l, :], a["subln_g_a_2"][l:l + 1].broadcast_to([P, P]))\
                       .then_inc(*landed.dma())
                    act.dma_start(lam[:, l], a["lambda_a_2"][l:l + 1].rearrange("l a e -> l (a e)")
                                  .broadcast_to([P, 4 * E])).then_inc(*landed.dma())
                act.wait_ge(*self.dve_ready.after("angles"))
                act.activation(self.sin, ang, ACT.Sin).then_inc(*self.act_order.one())
                act.activation(self.cos, n, ACT.Sin).then_inc(*self.act_ready.step("sin"))
                act.wait_ge(*self.dve_ready.after("lam_sums"))
                act.activation(lsum, lsum, ACT.Exp).then_inc(*self.act_ready.step("lam"))
                act.activation(self.cond, self.par[:, PAR["c_2"]:PAR["c_2"] + ND], ACT.Silu)\
                   .then_inc(*self.act_ready.step("cond"))

            @block.gpsimd
            def _(pool):
                pool.iota(dist_i[:], [[-1, 7 * P]], base=3 * P + 7 * P, channel_multiplier=1)\
                    .then_inc(*self.pool_ready.step("dist"))
                pool.wait_ge(*self.dve_ready.after("mods"))
                seq = self.order(pool, self.pool_order)
                for m, first, reach in ((self.near, -P, 64), (self.mid, -3 * P, 256)):
                    w = m.shape[-1]
                    seq(pool.affine_select(out=m, in_=m, compare_op=ALU.is_ge, fill=NEG, base=reach + first,
                                           pattern=[[1, w]], channel_multiplier=-1))
                    seq(pool.affine_select(out=m, in_=m, compare_op=ALU.is_ge, fill=NEG, base=reach - first,
                                           pattern=[[-1, w]], channel_multiplier=1))
                pool.memset(self.scratch[0:1, 0:1], 0.0).then_inc(*self.pool_ready.step("masks"))

            @block.vector
            def _(dve):
                seq = self.order(dve, self.dve_order)
                ts_, stt = dve.tensor_scalar, dve.scalar_tensor_tensor
                dve.wait_ge(*landed.all_of_stage(16 * 9))
                seq(dve.tensor_copy(pos, pos_i[:]))
                for j in range(R):
                    ts_(ang[:, :, j], pos, freq[j], None, ALU.mult).then_inc(*self.dve_order.one())
                dve.wait_ge(*self.dve_order.all())
                seq(ts_(n, ang, 1.0 / (2 * math.pi), MAGIC, ALU.mult, ALU.add))
                seq(ts_(n, n, MAGIC, None, ALU.subtract))
                seq(stt(ang, n, -C1, ang, ALU.mult, ALU.add))
                seq(stt(ang, n, -C2, ang, ALU.mult, ALU.add))
                seq(ts_(ang, ang, PI, -PI, ALU.min, ALU.max))
                seq(stt(n, ang, -1.0, ang, ALU.mult, ALU.max))
                ts_(n, n, -1.0, math.pi / 2, ALU.mult, ALU.add).then_inc(*self.dve_ready.step("angles"))
                for l in range(2):
                    seq(dve.tensor_tensor(lam[:, l, :, 0, :], lam[:, l, :, 0, :], lam[:, l, :, 1, :], ALU.mult))
                    ins = dve.tensor_reduce(lsum[:, 2 * l:2 * l + 2], lam[:, l, :, 0, :], AX_X, ALU.add)
                    if l == 0:
                        seq(ins)
                ins.then_inc(*self.dve_ready.step("lam_sums"))
                dve.wait_ge(*self.act_ready.after("lam"))
                for l in range(2):
                    seq(dve.tensor_tensor(self.neg_lam[:, l:l + 1], lsum[:, 2 * l + 1:2 * l + 2],
                                          lsum[:, 2 * l:2 * l + 1], ALU.subtract))
                    seq(ts_(self.neg_lam[:, l:l + 1], self.neg_lam[:, l:l + 1], -LAM[l], None, ALU.add))
                    seq(ts_(self.gain_a[:, l, 0, :], self.gain_a[:, l, 0, :], E ** -0.5, None, ALU.mult))
                    seq(ts_(self.subln[:, l, :], self.subln[:, l, :], 1.0 - LAM[l], None, ALU.mult))
                seq(dve.memset(self.near, 0.0))
                dve.wait_ge(*self.pool_ready.after("dist"))
                for m, d, w in ((self.mid, 4, 7 * P), (self.far, 16, 4 * P)):
                    bits = self.nc_bits[:, 0:w]
                    seq(ts_(bits, dist_i[:, 0:w], d - 1, None, ALU.bitwise_and))
                    seq(dve.tensor_copy(m, bits))
                    ins = ts_(m, m, 0.5, NEG, ALU.is_ge, ALU.mult)
                    if d == 4:
                        ins.then_inc(*self.dve_ready.step("near"))
                        dve.wait_ge(*self.dve_ready.after("near"))
                ins.then_inc(*self.dve_ready.step("mods"))

            @block.sync
            def _(sp):
                self.w.feed(sp)
        self.top = keep
        self.end_stage("tables")

    def modulation(self, l):
        nc = self.nc
        keep = self.top
        row = self.take(2, 512)
        N = 6 * D // 512
        cols = self.bank[7]
        with nc.Block() as block:
            @block.tensor
            def _(pe):
                def columns_of(c):
                    pe.wait_ge(*self.evac_dve.at(c + 1))
                    for j in range(4):
                        ins = pe.matmul(cols[:, 4 * c + j:4 * c + j + 1], row[0:1, c % 2, j * P:(j + 1) * P],
                                        self.ones[0:1, 0:1], start=True, stop=True)
                    ins.then_inc(*self.pe_ready.one())
                for c in range(N):
                    w = self.w.take(pe, ("ada", l, c), 512)
                    if c >= 2:
                        pe.wait_ge(*self.evac_dve.at(c - 1))
                    for k in range(ND):
                        ins = pe.matmul(self.bank[c % 2][0:1, :], self.cond[:, k:k + 1], w[:, k, :], start=k == 0,
                                        stop=k == ND - 1)
                    ins.then_inc(*self.mm_done.one())
                    self.w.release(self.mm_done)
                    if c:
                        columns_of(c - 1)
                columns_of(N - 1)

            @block.vector
            def _(dve):
                for c in range(N):
                    dve.wait_ge(*self.mm_done.at(c + 1))
                    if c >= 2:
                        dve.wait_ge(*self.pe_ready.at(c - 1))
                    dve.tensor_copy(row[0:1, c % 2, :], self.bank[c % 2][0:1, :]).then_inc(*self.evac_dve.one())
                seq = self.order(dve, self.dve_order)
                dve.wait_ge(*self.pe_ready.at(N))
                b = PAR["ada_b_2"] + 48 * l
                seq(dve.tensor_tensor(self.mod, cols[:, 0:48], self.par[:, b:b + 48], ALU.add))
                for dst, at, name in ((self.gain_m, 8, "norm_mix_g_2"), (self.gain_f, 32, "norm_mlp_g_2")):
                    g = self.par[:, PAR[name] + 8 * l:PAR[name] + 8 * l + 8]
                    seq(dve.scalar_tensor_tensor(dst, self.mod[:, at:at + 8], 1.0, g, ALU.add, ALU.mult))

            @block.sync
            def _(sp):
                self.w.feed(sp)
        self.top = keep
        self.end_stage(f"mod{l}")

    def queries_keys(self, name, chunks, width, gain, dst):
        nc = self.nc
        keep = self.top
        G, NC_ = width // E, width // P
        R = E // 4 // 2
        raw, sq = self.take(3, width), self.take(2, width)
        ss = self.take(3, G)
        t1, t2, t3, t4 = (self.take(G, R) for _ in range(4))
        units = [(c, i) for c in range(len(chunks)) for i in range(NT)]
        N = len(units)
        grp = lambda x: x.rearrange("p (g e) -> p g e", e=E)
        pe_done, turned = self.mm_done, self.pe_ready
        squared, summed, rooted, normed, emptied = (self.act_ready, self.dve_ready, self.act_order, self.evac_dve,
                                                    self.evac_act)

        def steps(*stages):
            for step in range(N + max(lag for lag, _ in stages)):
                for lag, run in stages:
                    if 0 <= step - lag < N:
                        run(step - lag, *units[step - lag])

        with nc.Block() as block:
            @block.tensor
            def _(pe):
                w = {}

                def project(n, c, i):
                    if i == 0:
                        w[0] = self.w.take(pe, chunks[c][0], width)
                    if n >= 3:
                        pe.wait_ge(*squared.at(n - 2))
                    for k in range(ND):
                        ins = pe.matmul(self.bank[n % 3][:, 0:width], self.hT[:, k, i * P:(i + 1) * P], w[0][:, k, :],
                                        start=k == 0, stop=k == ND - 1)
                    ins.then_inc(*pe_done.one())
                    if i == NT - 1:
                        self.w.release(pe_done)

                def turn(n, c, i):
                    pe.wait_ge(*normed.at(n + 1))
                    if n >= 2:
                        pe.wait_ge(*emptied.at(n - 1))
                    for j in range(NC_):
                        ins = pe.transpose(self.bank[4 + n % 2][:, j * P:(j + 1) * P],
                                           raw[:, n % 3, j * P:(j + 1) * P], self.ident[:])
                    ins.then_inc(*turned.one())
                steps((0, project), (2, turn))

            @block.scalar
            def _(act):
                def copy(n, c, i):
                    act.wait_ge(*pe_done.at(n + 1))
                    if n >= 3:
                        act.wait_ge(*turned.at(n - 2))
                    if n >= 2:
                        act.wait_ge(*summed.at(n - 1))
                    act.activation(raw[:, n % 3, :], self.bank[n % 3][:, 0:width], ACT.Copy)\
                       .then_inc(*self.x_landed.one())
                    act.activation(sq[:, n % 2, :], self.bank[n % 3][:, 0:width], ACT.Square)\
                       .then_inc(*squared.one())

                def root(n, c, i):
                    act.wait_ge(*summed.at(n + 1))
                    act.activation(ss[:, n % 3, :], ss[:, n % 3, :], ACT.Ln).then_inc(*self.x_landed.one())
                    act.wait_ge(*self.x_landed.all())
                    act.activation(ss[:, n % 3, :], ss[:, n % 3, :], ACT.Exp, scale=-0.5).then_inc(*rooted.one())

                def empty(n, c, i):
                    act.wait_ge(*turned.at(n + 1))
                    out = dst[:, chunks[c][2]:chunks[c][2] + NC_, i * P:(i + 1) * P]
                    act.activation(out, self.bank[4 + n % 2][:, 0:width].rearrange("p (j t) -> p j t", j=NC_),
                                   ACT.Copy).then_inc(*emptied.one())
                steps((0, copy), (1, root), (3, empty))

            @block.vector
            def _(dve):
                seq = self.order(dve, self.dve_order)
                tt = dve.tensor_tensor

                def sums(n, c, i):
                    dve.wait_ge(*squared.at(n + 1))
                    seq(dve.tensor_reduce(ss[:, n % 3, :], grp(sq[:, n % 2, :]), AX_X, ALU.add))
                    dve.tensor_scalar(ss[:, n % 3, :], ss[:, n % 3, :], 1.0 / E, EPS, ALU.mult, ALU.add)\
                       .then_inc(*summed.one())

                def norm(n, c, i):
                    x = grp(raw[:, n % 3, :])
                    dve.wait_ge(*rooted.at(n + 1))
                    seq(tt(x, x, ss[:, n % 3, :].unsqueeze(2).broadcast_to([P, G, E]), ALU.mult))
                    seq(tt(x, x, gain[:, chunks[c][1], :].unsqueeze(1).broadcast_to([P, G, E]), ALU.mult))
                    cos = self.cos[:, i, :].unsqueeze(1).broadcast_to([P, G, R])
                    sin = self.sin[:, i, :].unsqueeze(1).broadcast_to([P, G, R])
                    x1, x2 = x[:, :, 0:R], x[:, :, R:2 * R]
                    for t, u, v in ((t1, x1, cos), (t2, x2, sin), (t3, x2, cos), (t4, x1, sin)):
                        tt(t, u, v, ALU.mult).then_inc(*self.dve_order.one())
                    dve.wait_ge(*self.dve_order.all())
                    tt(x1, t1, t2, ALU.subtract).then_inc(*self.dve_order.one())
                    dve.wait_ge(*self.dve_order.all())
                    tt(x2, t3, t4, ALU.add).then_inc(*normed.one())
                steps((0, sums), (1, norm))

            @block.sync
            def _(sp):
                self.w.feed(sp)
        self.top = keep
        self.end_stage(name)

    def values(self, name, chunks, width, dst):
        tiles = []
        for c, key in enumerate(chunks):
            for i in range(NT):
                def copy(e, seq, ps, c=c, i=i):
                    out = dst[:, i, c * width:(c + 1) * width]
                    return e.activation(out, ps, ACT.Copy) if i % 2 else e.tensor_copy(out, ps)
                tiles.append(dict(by="act" if i % 2 else "dve", shape=(P, width), empty=copy,
                                  pairs=lambda ch, key=key, i=i: [
                                      (self.hT[:, k, i * P:(i + 1) * P], ch[key][:, k, :]) for k in range(ND)]))
            tiles[-NT]["takes"] = [(key, width)]
            tiles[-1]["frees"] = 1
        self.products(name, tiles)

    def differential(self, l):
        oaT = self.oaT
        keep = self.top
        qT, kT, v, o = self.take(ND, T), self.take(ND, T), self.take(NT, D), self.take(NT, D)
        self.queries_keys(f"qk_a{l}", [(("a", l, 0), 0, 0), (("a", l, 1), 0, 4)], 512, self.gain_a[:, l], qT)
        self.queries_keys(f"kk_a{l}", [(("a", l, 2), 1, 0), (("a", l, 3), 1, 4)], 512, self.gain_a[:, l], kT)
        self.values(f"v_a{l}", [("a", l, 4), ("a", l, 5)], 512, v)
        units, groups = [], []
        coef = self.take(4)
        inv = self.take(4)
        for i in range(NT):
            for half in range(2):
                g = len(groups)
                for h in range(4 * half, 4 * half + 4):
                    parts = [dict(scores=(qT[c * E:(c + 1) * E, h, i * P:(i + 1) * P], kT[c * E:(c + 1) * E, h, :]),
                                  n=T) for c in range(2)]

                    def mix(dve, seq, q, rows):
                        l0, l1 = self.row_sum[:, q:q + 1], self.row_sum[:, q + 1:q + 2]
                        by = coef[:, q // 2 % 4:q // 2 % 4 + 1]
                        seq(dve.reciprocal(by, l1))
                        seq(dve.scalar_tensor_tensor(by, l0, self.neg_lam[:, l:l + 1], by, ALU.mult, ALU.mult))
                        return dve.scalar_tensor_tensor(rows[0], rows[1], by, rows[0], ALU.mult, ALU.add)
                    units.append(dict(parts=parts, mix=mix, group=g, cols=((h - 4 * half) * P, (h - 4 * half + 1) * P),
                                      values=[v[:, b, h * P:(h + 1) * P] for b in range(NT)]))

                def take_out(dve, seq, bank, i=i, half=half, g=g):
                    sums = self.row_sum[:, 8 * g:8 * g + 8].rearrange("p (h c) -> p h c", c=2)[:, :, 0]
                    seq(dve.reciprocal(inv, sums))
                    return dve.tensor_tensor(
                        o[:, i, half * 512:(half + 1) * 512].rearrange("p (h e) -> p h e", h=4),
                        bank[:].rearrange("p (h e) -> p h e", h=4), inv.unsqueeze(2).broadcast_to([P, 4, P]), ALU.mult)
                groups.append(take_out)
        self.attention(f"diff{l}", units, groups, parts=2)
        nc = self.nc
        sq = self.take(2, D)
        ms = self.take(NT, 8)
        with nc.Block() as block:
            @block.scalar
            def _(act):
                seq = self.order(act, self.act_order)
                for i in range(NT):
                    if i >= 2:
                        act.wait_ge(*self.dve_ready.at(i - 1))
                    act.activation(sq[:, i % 2, :], o[:, i, :], ACT.Square).then_inc(*self.act_ready.one())
                for i in range(NT):
                    act.wait_ge(*self.dve_ready.at(i + 1))
                act.activation(ms, ms, ACT.Ln).then_inc(*self.act_order.one())
                act.wait_ge(*self.act_order.all())
                act.activation(ms, ms, ACT.Exp, scale=-0.5).then_inc(*self.act_ready.one())
                for h in range(ND):
                    act.wait_ge(*self.mm_done.at(h + 1))
                    act.activation(oaT[:, h, :], self.bank[h % 4][:], ACT.Copy).then_inc(*self.evac_act.one())

            @block.vector
            def _(dve):
                seq = self.order(dve, self.dve_order)
                for i in range(NT):
                    dve.wait_ge(*self.act_ready.at(i + 1))
                    seq(dve.tensor_reduce(ms[:, i, :], sq[:, i % 2, :].rearrange("p (h e) -> p h e", h=8), AX_X,
                                          ALU.add))
                    dve.tensor_scalar(ms[:, i, :], ms[:, i, :], 1.0 / P, EPS, ALU.mult, ALU.add)\
                       .then_inc(*self.dve_ready.one())
                dve.wait_ge(*self.act_ready.at(NT + 1))
                for i in range(NT):
                    x = o[:, i, :].rearrange("p (h e) -> p h e", h=8)
                    seq(dve.tensor_tensor(x, x, ms[:, i, :].unsqueeze(2).broadcast_to([P, 8, P]), ALU.mult))
                    dve.tensor_tensor(x, x, self.subln[:, l, :].unsqueeze(1).broadcast_to([P, 8, P]), ALU.mult)\
                       .then_inc(*self.dve_ready.one())

            @block.tensor
            def _(pe):
                pe.wait_ge(*self.dve_ready.at(2 * NT))
                for h in range(ND):
                    if h >= 4:
                        pe.wait_ge(*self.evac_act.at(h - 3))
                    for i in range(NT):
                        ins = pe.transpose(self.bank[h % 4][:, i * P:(i + 1) * P], o[:, i, h * P:(h + 1) * P],
                                           self.ident[:])
                    ins.then_inc(*self.mm_done.one())

            @block.sync
            def _(sp):
                self.w.feed(sp)
        self.top = keep
        self.end_stage(f"oa{l}")

    def dilated(self, l):
        obT = self.obT
        keep = self.top
        qT, kT, v, o = self.take(6, T), self.take(6, T), self.take(NT, 768), self.take(NT, MIX)
        self.queries_keys(f"qk_b{l}", [(("b", l, 0), 0, 0), (("b", l, 1), 0, 3)], 384, self.gain_b[:, l], qT)
        self.queries_keys(f"kk_b{l}", [(("b", l, 2), 1, 0), (("b", l, 3), 1, 3)], 384, self.gain_b[:, l], kT)
        self.values(f"v_b{l}", [("b", l, 4), ("b", l, 5)], 384, v)
        units, groups = [], []
        inv = self.take(4)
        for i in range(NT):
            windows = [(max(0, i - 1), min(NT, i + 2), self.near, i - 1),
                       (max(0, i - 2) if i == 3 else 0, NT if i else 3, self.mid, i - 3),
                       (0, NT, self.far, 0)]
            for h in range(H):
                for w, (b0, b1, table, origin) in enumerate(windows):
                    f, lo = (w * H + h) // 2, (w * H + h) % 2 * E
                    part = dict(scores=(qT[lo:lo + E, f, i * P:(i + 1) * P], kT[lo:lo + E, f, b0 * P:b1 * P]),
                                n=(b1 - b0) * P, table=table[:, (b0 - origin) * P:(b1 - origin) * P])
                    units.append(dict(parts=[part], group=i, cols=(h * E, (h + 1) * E),
                                      values=[v[:, b, (w * H + h) * E:(w * H + h + 1) * E] for b in range(b0, b1)]))

            def take_out(dve, seq, bank, i=i):
                sums = self.row_sum[:, 12 * i:12 * i + 12].rearrange("p (h w) -> p h w", w=3)
                seq(dve.tensor_reduce(inv, sums, AX_X, ALU.add))
                seq(dve.reciprocal(inv, inv))
                return dve.tensor_tensor(o[:, i, :].rearrange("p (h e) -> p h e", h=H),
                                         bank[:, 0:MIX].rearrange("p (h e) -> p h e", h=H),
                                         inv.unsqueeze(2).broadcast_to([P, H, E]), ALU.mult)
            groups.append(take_out)
        self.attention(f"dil{l}", units, groups, joint=3)
        nc = self.nc
        with nc.Block() as block:
            @block.tensor
            def _(pe):
                for c in range(2):
                    for i in range(NT):
                        ins = pe.transpose(self.bank[c][:, i * P:(i + 1) * P], o[:, i, c * P:(c + 1) * P],
                                           self.ident[:])
                    ins.then_inc(*self.mm_done.one())

            @block.vector
            def _(dve):
                for c in range(2):
                    dve.wait_ge(*self.mm_done.at(c + 1))
                    dve.tensor_copy(obT[:, c, :], self.bank[c][:]).then_inc(*self.evac_dve.one())

            @block.sync
            def _(sp):
                self.w.feed(sp)
        self.top = keep
        self.end_stage(f"ob{l}")

    def layer(self, l):
        mod = lambda part: (lambda k: self.mod[:, 8 * part + k:8 * part + k + 1])
        keep = self.top
        self.modulation(l)
        self.rms(f"rms_mix{l}", lambda k: self.gain_m[:, k:k + 1], mod(0))
        self.oaT, self.obT = self.take(ND, T), self.take(2, T)
        self.differential(l)
        self.dilated(l)
        mixT = self.take(ND, T)

        def plan(c):
            gk, bk = ("gates", l, c // 2), ("branches", l, c // 2)
            cs = slice(c % 2 * P, c % 2 * P + P)
            branches = []
            for i, (src, first, n) in enumerate(((self.oaT, 0, 8), (self.obT, 8, 2))):
                b = PAR["gate_bias_2"] + 16 * l + 8 * i + c
                branches.append((lambda ch, i=i: [(ch[gk][:, i * ND + k, cs], self.hT[:, k, :]) for k in range(ND)],
                                 lambda ch, src=src, first=first, n=n: [
                                     (ch[bk][:, first + k, cs], src[:, k, :]) for k in range(n)],
                                 self.par[:, b:b + 1]))
            return ([(gk, 256), (bk, 256)], 0, branches) if c % 2 == 0 else ([], 2, branches)
        self.gated_sum(f"gates{l}", mixT, plan)
        self.add_products(f"out{l}", lambda c: ("out", l, c), mixT, mod(2))
        self.top = keep
        self.rms(f"rms_mlp{l}", lambda k: self.gain_f[:, k:k + 1], mod(3))
        upT = self.take(4 * ND, T)
        tiles = []
        for c in range(4 * ND):
            key = ("up", l, c // 4)

            def relu2(e, seq, ps, c=c):
                if c % 2:
                    seq(e.activation(upT[:, c, :], ps, ACT.Relu))
                    return e.activation(upT[:, c, :], upT[:, c, :], ACT.Square)
                seq(e.tensor_scalar(upT[:, c, :], ps, 0.0, None, ALU.max))
                return e.tensor_tensor(upT[:, c, :], upT[:, c, :], upT[:, c, :], ALU.mult)
            tiles.append(dict(by="act" if c % 2 else "dve", shape=(P, T), empty=relu2, pairs=lambda ch, c=c, key=key: [
                (ch[key][:, k, c % 4 * P:c % 4 * P + P], self.hT[:, k, :]) for k in range(ND)]))
            if c % 4 == 0:
                tiles[-1]["takes"] = [(key, 512)]
            if c % 4 == 3:
                tiles[-1]["frees"] = 1
        self.products(f"up{l}", tiles)
        tiles = []
        gate_f = mod(5)
        for c in range(ND):
            keys = [("down", l, c // 2, half) for half in range(2)]

            def add(e, seq, ps, c=c):
                return e.scalar_tensor_tensor(self.xT[:, c, :], ps, gate_f(c), self.xT[:, c, :], ALU.mult, ALU.add)
            tiles.append(dict(by="dve", shape=(P, T), empty=add, pairs=lambda ch, c=c, keys=keys: [
                (ch[keys[k // 16]][:, k % 16, c % 2 * P:c % 2 * P + P], upT[:, k, :]) for k in range(32)]))
            if c % 2 == 0:
                tiles[-1]["takes"] = [(key, 256) for key in keys]
            else:
                tiles[-1]["frees"] = 2
        self.products(f"down{l}", tiles)
        self.top = keep

    def store(self):
        nc = self.nc
        y = self.take(NT, D)
        with nc.Block() as block:
            @block.tensor
            def _(pe):
                for n in range(8):
                    i, half = n // 2, n % 2
                    for k in range(4):
                        ins = pe.transpose(self.bank[n][:, k * P:(k + 1) * P],
                                           self.xT[:, 4 * half + k, i * P:(i + 1) * P], self.ident[:])
                    ins.then_inc(*self.mm_done.one())

            @block.vector
            def _(dve):
                for n in range(8):
                    dve.wait_ge(*self.mm_done.at(n + 1))
                    dve.tensor_copy(y[:, n // 2, n % 2 * 512:n % 2 * 512 + 512], self.bank[n][:])\
                       .then_inc(*self.evac_dve.one())

            @block.sync
            def _(sp):
                for i in range(NT):
                    sp.wait_ge(*self.evac_dve.at(2 * i + 2))
                    sp.dma_start(self.out[0, i * P:(i + 1) * P, :], y[:, i, :]).then_inc(*self.stored.dma())
                sp.wait_ge(*self.stored.all())
        self.end_stage("store")

    def build(self):
        self.load()
        col = lambda name: (lambda k: self.par[:, PAR[name] + k:PAR[name] + k + 1])
        self.rms("rms1", col("norm_gain"))
        self.first_projection()
        self.sparse_attention()
        self.spatial_gating()
        self.mixer_preparation()
        self.recurrence("gdn")
        self.recurrence("rwkv")
        self.rms("rms1_again", col("norm_gain"))
        self.top = self.after_ys
        self.merge()
        self.top = 0
        self.rms("final", col("final_gain"), dst=self.xT)
        self.layer_tables()
        for l in range(2):
            self.layer(l)
        self.store()


def hybrid_then_conditioned_layers(nc, arrays, out):
    k = Kernel(nc, arrays, out)
    try:
        k.build()
    except Stop:
        pass
    return k


_INS = ['x', 'norm_gain', 'w_in', 'gdn_conv', 'gdn_a_log', 'gdn_dt_bias', 'gdn_norm', 'sg_ln_gain', 'sg_ln_bias',
        'sg_w_s', 'sg_b_s', 'rw_mu', 'rw_w_up', 'rw_w0', 'rw_a_up', 'rw_a0', 'rw_k_k', 'rw_k_a', 'rw_r_k',
        'rw_gn_gain', 'rw_gn_bias', 'nsa_cmp_pos', 'nsa_cmp_w1', 'nsa_cmp_w2', 'w_branch', 'w_out', 'final_gain',
        'c_2', 'positions_2', 'ada_w_2', 'ada_b_2', 'norm_mix_g_2', 'norm_mlp_g_2', 'w_in_2', 'qk_gain_a_2',
        'lambda_a_2', 'subln_g_a_2', 'qk_gain_b_2', 'w_branch_a_2', 'w_branch_b_2', 'gate_bias_2', 'w_out_2',
        'w_mlp_up_2', 'w_mlp_down_2']


def kernel(**inputs):
    import concourse.bacc as bacc
    from concourse.bass_utils import run_bass_kernel_spmd

    nc = bacc.Bacc("TRN2", target_bir_lowering=False, num_devices=1)
    arrays, views = {}, {}
    for name in _INS:
        v = np.ascontiguousarray(inputs[name])
        arrays[f"in_{name}"] = v
        views[name] = nc.dram_tensor(f"in_{name}", v.shape, mybir.dt.from_np(v.dtype), kind="ExternalInput").ap()
    out = nc.dram_tensor("out_0", (1, T, D), F32, kind="ExternalOutput").ap()
    hybrid_then_conditioned_layers(nc, views, out)
    r = run_bass_kernel_spmd(nc, [arrays], core_ids=[0])
    return r.results[0]["out_0"]
```

```python
import math

import numpy as np
import concourse.bass as bass
import concourse.mybir as mybir
from concourse.alu_op_type import AluOpType as ALU

ACT = mybir.ActivationFunctionType
F32 = mybir.dt.float32
F32R = mybir.dt.float32r
I32 = mybir.dt.int32
AX_X = mybir.AxisListType.X

P = 128
T = 512
D = 1024
NT = T // P
ND = D // P
H = 4
E = 64
MIX = 256
EPS = 1e-6
NEG = -1e30

QKV0, A0, B0, Z0, U0, V0, SZ0 = 0, 768, 772, 776, 1032, 1288, 1544
RW0, RWZ0, NQ0, NKV0, NG0, NZ0, MERGE0 = 1800, 2696, 2952, 3208, 3592, 3604, 3860

TM_VS, TM_VW, TM_NG, TM_NZ, NS_W = 0, 64, 128, 140, 396

RING = 3
SLOT = 4096

STOP = None


class Signal:
    everyone = []

    def __init__(self, nc, name):
        self.sem = nc.alloc_semaphore(name)
        self.count = self.base = 0
        Signal.everyone.append(self)

    def one(self):
        self.count += 1
        return self.sem, 1

    def dma(self):
        self.count += 16
        return self.sem, 16

    def at(self, k):
        assert k > 0
        return self.sem, self.base + k

    def order_of(self, names):
        self.names = {n: j + 1 for j, n in enumerate(names)}
        assert len(self.names) == len(names)

    def step(self, name):
        assert self.names[name] == self.count - self.base + 1, (name, self.count - self.base)
        return self.one()

    def after(self, name):
        return self.sem, self.base + self.names[name]

    def all_of_stage(self, k):
        return self.sem, self.base + k

    def all(self):
        return self.sem, self.count


class Stop(Exception):
    pass


def columns(w, lo, n, k0=0, nk=None):
    v = w.rearrange("(k p) c -> p k c", p=P)
    return v[:, k0:(v.shape[1] if nk is None else k0 + nk), lo:lo + n]


def weight_plan(a):
    plan = []
    w = a["w_in"][0]
    for lo, hi in P1_CHUNKS:
        plan.append((("p1", lo), [(columns(w, lo, hi - lo), 0)]))
    for c in range(ND):
        for half in range(2):
            gates = [(columns(w, MERGE0 + (2 * half + i) * D + c * P, P), i * ND * P) for i in range(2)]
            own = [(columns(a["w_branch"][0, 2 * half + i], c * P, P), (2 * ND + 2 * i) * P) for i in range(2)]
            plan.append((("merge", c, half), gates + own))
    for c in range(2):
        plan.append((("out", c), [(columns(a["w_out"][0], c * 512, 512), 0)]))
    for l in range(2):
        for c in range(12):
            plan.append((("ada", l, c), [(columns(a["ada_w_2"][l], c * 512, 512), 0)]))
        w = a["w_in_2"][l]
        for c in range(6):
            plan.append((("a", l, c), [(columns(w, c * 512, 512), 0)]))
        for c in range(6):
            plan.append((("b", l, c), [(columns(w, 3072 + c * 384, 384), 0)]))
        for c in range(ND):
            gates = [(columns(w, 5376 + i * D + c * P, P), i * ND * P) for i in range(2)]
            own = [(columns(a[f"w_branch_{'ab'[i]}_2"][l], c * P, P), (2 + i) * ND * P) for i in range(2)]
            plan.append((("branches", l, c), gates + own))
        for c in range(2):
            plan.append((("out", l, c), [(columns(a["w_out_2"][l], c * 512, 512), 0)]))
        for r in range(4):
            for c in range(2):
                plan.append((("up", l, 2 * r + c), [(columns(a["w_mlp_up_2"][l], (2 * r + c) * 512, 512), 0)]))
            for c in range(2):
                plan.append((("down", l, r, c), [(columns(a["w_mlp_down_2"][l], c * 512, 512, r * ND, ND), 0)]))
    return plan


P1_CHUNKS = [(0, 384), (384, 768), (768, 1032), (1032, 1544), (1544, 1800), (1800, 2312), (2312, 2696),
             (2696, 2952), (2952, 3464), (3464, 3860)]


class Weights:

    def __init__(self, nc, arrays):
        self.ring = nc.alloc_sbuf_tensor("weight_ring", [P, RING, SLOT], F32)
        self.landed = [Signal(nc, f"weights_landed_{s}") for s in range(RING)]
        self.released = []
        self.plan = weight_plan(arrays)
        self.taken = self.loaded = 0
        self.limit = len(P1_CHUNKS)
        self.need = []
        count = [0] * RING
        for n, (_, parts) in enumerate(self.plan):
            count[n % RING] += 16 * len(parts)
            self.need.append(count[n % RING])

    def take(self, pe, key, width):
        n = self.taken
        assert self.plan[n][0] == key, (self.plan[n][0], key)
        pe.wait_ge(self.landed[n % RING].sem, self.need[n])
        self.taken += 1
        s = self.ring[:, n % RING, :]
        return s[:, 0:SLOT // width * width].rearrange("p (k c) -> p k c", c=width)

    def release(self, signal):
        self.released.append((signal, signal.count))

    def feed(self, sp):
        limit = len(self.plan) if self.limit is None else self.limit
        while self.loaded < min(limit, len(self.released) + RING):
            n = self.loaded
            if n >= RING:
                signal, value = self.released[n - RING]
                if value == signal.count > signal.base:
                    break
                sp.wait_ge(signal.sem, value)
            for view, offset in self.plan[n][1]:
                _, k, c = view.shape
                dst = self.ring[:, n % RING, offset:offset + k * c].rearrange("p (k c) -> p k c", c=c)
                sp.dma_start(dst, view).then_inc(*self.landed[n % RING].dma())
            self.loaded += 1


SPLIT_AT = 29696 - 4 * 4096 - 2 * 2048
ARENA = 29696

PAR = {}
PAR_ROWS = [("norm_gain", 8), ("final_gain", 8), ("gdn_conv", 24), ("rw_mu", 7), ("sg_b_s", 4),
            ("norm_mix_g_2", 16), ("norm_mlp_g_2", 16), ("gate_bias_2", 32),
            ("c_2", 8), ("ada_b_2", 96)]
for _name, _rows in PAR_ROWS:
    PAR[_name] = sum(r for n, r in PAR_ROWS[:[n for n, _ in PAR_ROWS].index(_name)])
PAR_SPLIT = PAR["c_2"]
PAR_N = PAR["ada_b_2"] + 96


class AttentionSignals:
    def __init__(self, nc):
        self.scores = Signal(nc, "scores_done")
        self.maxima = Signal(nc, "maxima_done")
        self.exps = Signal(nc, "exps_done")
        self.mixed = Signal(nc, "mixed")
        self.turned = Signal(nc, "rows_turned")
        self.copied = Signal(nc, "turned_copied")
        self.summed = Signal(nc, "values_summed")
        self.finished = Signal(nc, "group_finished")


class Normalisation:

    def __init__(self, kernel, gain, shift, rs, dst):
        self.gain, self.shift, self.rs, self.dst, self.xT = gain, shift, rs, dst, kernel.xT
        self.scaled, self.shifted = kernel.scaled, kernel.shifted

    def vector(self, dve):
        for k in range(ND):
            dve.scalar_tensor_tensor(self.dst[:, k, :], self.xT[:, k, :], self.gain(k), self.rs, ALU.mult,
                                     ALU.mult).then_inc(*self.scaled.one())

    def scalar(self, act):
        if self.shift is not None:
            for k in range(ND):
                act.wait_ge(*self.scaled.at(k + 1))
                act.activation(self.dst[:, k, :], self.dst[:, k, :], ACT.Identity, bias=self.shift(k))\
                   .then_inc(*self.shifted.one())

    def ready(self, k):
        return (self.scaled if self.shift is None else self.shifted).at(k + 1)


class Kernel:
    def __init__(self, nc, arrays, out):
        self.nc, self.a, self.out = nc, arrays, out
        Signal.everyone = []
        self.w = Weights(nc, arrays)
        self.bank = [nc.alloc_psum_tensor(f"bank{b}", [P, 512], F32) for b in range(8)]
        sb = self.sb
        self.xT = sb("xT", [P, ND, T])
        self.hT = sb("hT", [P, ND, T])
        self.ident = sb("ident", [P, P])
        self.ones = sb("ones", [P, P])
        self.par = sb("par", [P, PAR_N])
        at = (nc.sbuf_base + 31) // 32 * 32
        self.arena = sb("arena", [P, ARENA])
        at += 4 * SPLIT_AT

        def part(name, shape):
            nonlocal at
            v = nc.alloc_sbuf_tensor_at(name, [P] + shape, F32R, offset=at)
            at += 4 * math.prod(shape)
            return v
        self.split_h = [part(f"h_{p}", [ND, T]) for p in ("hi", "lo")]
        self.split_u = [part(f"hidden_{p}", [ND, T]) for p in ("hi", "lo")]
        self.split_w = [part(f"weights_{p}", [2, ND, P]) for p in ("hi", "lo")]
        self.top = 0
        self.params_landed = Signal(nc, "params_landed")
        self.x_landed = Signal(nc, "x_landed")
        self.mm_done = Signal(nc, "mm_done")
        self.evac_act = Signal(nc, "evac_act")
        self.evac_dve = Signal(nc, "evac_dve")
        self.act_order = Signal(nc, "act_order")
        self.dve_order = Signal(nc, "dve_order")
        self.pool_order = Signal(nc, "pool_order")
        self.act_ready = Signal(nc, "act_ready")
        self.dve_ready = Signal(nc, "dve_ready")
        self.pool_ready = Signal(nc, "pool_ready")
        self.stored = Signal(nc, "stored")
        self.scaled = Signal(nc, "norm_scaled")
        self.shifted = Signal(nc, "norm_shifted")
        self.att = AttentionSignals(nc)
        self.recurrence_done = {kind: [Signal(nc, f"{kind}_{e}_done") for e in ("tensor", "vector", "scalar")]
                                for kind in ("gdn", "rwkv")}
        self.pe_ready = Signal(nc, "pe_ready")
        self.scratch = sb("scratch", [P, 512])
        self.nc_pos = sb("positions", [P, NT], I32)
        self.nc_dist = sb("distances", [P, 7 * P], I32)
        self.nc_bits = sb("distance_bits", [P, 7 * P], I32)

    def sb(self, name, shape, dt=F32):
        return self.nc.alloc_sbuf_tensor(name, shape, dt)

    def take(self, *dims):
        n = math.prod(dims)
        v = self.arena[:, self.top:self.top + n]
        self.top += n
        assert self.top <= ARENA, (self.top, ARENA)
        if len(dims) == 1:
            return v
        names = "abcd"[:len(dims)]
        return v.rearrange(f"p ({' '.join(names)}) -> p {' '.join(names)}",
                           **{names[j]: dims[j] for j in range(1, len(dims))})

    def end_stage(self, name):
        for s in Signal.everyone:
            s.base = s.count
        if name == STOP:
            with self.nc.Block() as block:
                @block.sync
                def _(sp):
                    for s in self.w.landed:
                        sp.wait_ge(*s.all())
            raise Stop

    def order(self, eng, signal):
        def seq(ins):
            ins.then_inc(*signal.one())
            eng.wait_ge(*signal.all())
        return seq

    def load(self):
        nc, a = self.nc, self.a
        keep = self.top
        x_tm = self.take(NT, D)
        rows = self.take(2, P)

        with nc.Block() as block:
            @block.gpsimd
            def _(pool):
                seq = self.order(pool, self.pool_order)
                pool.memset(self.ones[:], 1.0).then_inc(*self.pool_order.one())
                seq(pool.memset(self.ident[:], 0.0))
                pool.affine_select(out=self.ident[:], in_=self.ident[:], compare_op=ALU.not_equal, fill=1.0,
                                   base=0, pattern=[[-1, P]], channel_multiplier=1).then_inc(*self.pool_ready.one())

            @block.tensor
            def _(pe):
                pe.wait_ge(*self.pool_ready.at(1))
                pe.wait_ge(*self.x_landed.all_of_stage(16))
                for k in range(ND):
                    for i in range(NT):
                        ins = pe.transpose(self.bank[k][:, i * P:(i + 1) * P], x_tm[:, i, k * P:(k + 1) * P],
                                           self.ident[:])
                    ins.then_inc(*self.mm_done.one())
                pe.wait_ge(*self.params_landed.all_of_stage(16 * len(PAR_ROWS)))
                pe.wait_ge(*self.evac_dve.at(1))
                n = PAR_SPLIT
                pe.transpose(self.bank[0][:, 0:n], rows[0:n, 0, :], self.ident[0:n, 0:n])
                m = PAR_N - PAR_SPLIT
                pe.transpose(self.bank[0][:, n:n + m], rows[0:m, 1, :],
                             self.ident[0:m, 0:m]).then_inc(*self.mm_done.one())

            @block.vector
            def _(dve):
                for k in range(ND):
                    dve.wait_ge(*self.mm_done.at(k + 1))
                    dve.tensor_copy(self.xT[:, k, :], self.bank[k][:]).then_inc(*self.evac_dve.one())
                dve.wait_ge(*self.mm_done.at(ND + 1))
                dve.tensor_copy(self.par[:], self.bank[0][:, 0:PAR_N]).then_inc(*self.evac_dve.one())

            @block.scalar
            def _(act):
                for name, n in PAR_ROWS:
                    c0 = PAR[name]
                    half, r = (0, c0) if c0 < PAR_SPLIT else (1, c0 - PAR_SPLIT)
                    v = a[name]
                    while len(v.shape) > 1:
                        v = v.rearrange("a b -> (a b)") if len(v.shape) == 2 else v.rearrange("a b c -> a (b c)")
                    act.dma_start(rows[r:r + n, half, :], v.rearrange("(r q) -> r q", q=P))\
                       .then_inc(*self.params_landed.dma())

            @block.sync
            def _(sp):
                sp.dma_start(x_tm, a["x"][0].rearrange("(i p) d -> p i d", p=P)).then_inc(*self.x_landed.dma())
                self.w.feed(sp)
        self.top = keep
        self.end_stage("load")

    def rms(self, name, gain, shift=None, dst=None):
        nc = self.nc
        keep = self.top
        sq = self.take(2, T)
        rs, early = self.scratch[:], self.take(1)
        self.norm = Normalisation(self, gain, shift, rs, self.hT if dst is None else dst)
        with nc.Block() as block:
            @block.scalar
            def _(act):
                for k in range(ND):
                    if k >= 2:
                        act.wait_ge(*self.mm_done.at(k - 1))
                    act.activation(sq[:, k % 2, :], self.xT[:, k, :], ACT.Square).then_inc(*self.act_ready.one())
                seq = self.order(act, self.act_order)
                act.activation(early[0:1, :], self.ones[0:1, 0:1], ACT.Ln).then_inc(*self.act_order.one())
                act.wait_ge(*self.dve_ready.at(1))
                seq(act.activation(rs, rs, ACT.Ln))
                act.activation(rs, rs, ACT.Exp, scale=-0.5).then_inc(*self.act_ready.one())
                if dst is not None:
                    self.norm.scalar(act)

            @block.tensor
            def _(pe):
                for k in range(ND):
                    pe.wait_ge(*self.act_ready.at(k + 1))
                    pe.matmul(self.bank[0][:], self.ones[:], sq[:, k % 2, :], start=k == 0,
                              stop=k == ND - 1).then_inc(*self.mm_done.one())

            @block.vector
            def _(dve):
                dve.wait_ge(*self.mm_done.at(ND))
                dve.tensor_scalar(rs, self.bank[0][:], 1.0 / D, EPS, ALU.mult, ALU.add)\
                   .then_inc(*self.dve_ready.one())
                if dst is not None:
                    dve.wait_ge(*self.act_ready.at(ND + 1))
                    self.norm.vector(dve)

            @block.sync
            def _(sp):
                self.w.feed(sp)
        self.top = keep
        self.end_stage(name)

    def products(self, name, tiles, norm=None):
        nc = self.nc
        NB = 8
        def emptied(t):
            which = tiles[t]["by"]
            return which, sum(x["by"] == which for x in tiles[:t + 1])

        with nc.Block() as block:
            @block.tensor
            def _(pe):
                chunks = {}
                for t, tile in enumerate(tiles):
                    for key, width in tile.get("takes", ()):
                        chunks[key] = self.w.take(pe, key, width)
                    if t >= NB:
                        which, n = emptied(t - NB)
                        pe.wait_ge(*(self.evac_act if which == "act" else self.evac_dve).at(n))
                    pairs = tile["pairs"](chunks)
                    m = tile["shape"]
                    for j, (lhsT, rhs) in enumerate(pairs):
                        if norm is not None and t == 0:
                            pe.wait_ge(*norm.ready(j))
                        ins = pe.matmul(self.bank[t % NB][0:m[0], 0:m[1]], lhsT, rhs, start=j == 0,
                                        stop=j == len(pairs) - 1)
                    ins.then_inc(*self.mm_done.one())
                    for _ in range(tile.get("frees", 0)):
                        self.w.release(self.mm_done)

            def empty(eng, which, done, order):
                if norm is not None:
                    (norm.scalar if which == "act" else norm.vector)(eng)
                seq = self.order(eng, order)
                for t, tile in enumerate(tiles):
                    if tile["by"] == which:
                        eng.wait_ge(*self.mm_done.at(t + 1))
                        for other in tile.get("needs", ()):
                            by, n = emptied(other)
                            eng.wait_ge(*(self.evac_act if by == "act" else self.evac_dve).at(n))
                        m = tile["shape"]
                        tile["empty"](eng, seq, self.bank[t % NB][0:m[0], 0:m[1]]).then_inc(*done.one())

            @block.scalar
            def _(act):
                empty(act, "act", self.evac_act, self.act_order)

            @block.vector
            def _(dve):
                empty(dve, "dve", self.evac_dve, self.dve_order)

            @block.sync
            def _(sp):
                self.w.feed(sp)
        self.end_stage(name)

    def first_projection(self):
        self.ysT = self.take(8, T)
        self.after_ys = self.top
        self.ab = self.take(NT, 8)
        self.z_gdn = self.take(NT, MIX)
        self.z_rw = self.take(NT, MIX)
        self.qkvT = self.take(6, T + 3)
        self.rwT = self.take(7, T + 1)
        self.after_mixer_inputs = self.top
        self.sg = self.take(NT, 3 * MIX)
        self.ns = self.take(NT, NS_W)
        self.nsa_qT = self.take(H, T)
        self.nsa_kvT = self.take(4, T)
        hT = self.hT
        tiles = []

        def fm(key, width, lo, m, dst, **more):
            tiles.append(dict(by="dve", shape=(m, T), pairs=lambda ch: [
                (ch[key][:, k, lo:lo + m], hT[:, k, :]) for k in range(ND)],
                empty=lambda e, seq, ps: e.tensor_copy(dst, ps), **more))

        def tmaj(key, lo, n, i, empty, by="act", **more):
            tiles.append(dict(by=by, shape=(P, n), pairs=lambda ch: [
                (hT[:, k, i * P:(i + 1) * P], ch[key][:, k, lo:lo + n]) for k in range(ND)], empty=empty, **more))

        def func(f, dst):
            return lambda e, seq, ps: e.activation(dst, ps, f)

        def copy(dst):
            return lambda e, seq, ps: e.tensor_copy(dst, ps)

        for lo, hi in P1_CHUNKS:
            key, width = ("p1", lo), hi - lo
            first = len(tiles)
            if lo < A0:
                for c in range(lo // P, hi // P):
                    fm(key, width, c * P - lo, P, self.qkvT[:, c, 3:])
            elif lo == A0:
                for i in range(NT):
                    tmaj(key, 0, 8, i, copy(self.ab[:, i, :]), by="dve")
                    tmaj(key, 8, MIX, i, func(ACT.Silu, self.z_gdn[:, i, :]))
            elif lo == U0:
                for i in range(NT):
                    tmaj(key, 0, 512, i, func(ACT.Gelu_apprx_tanh, self.sg[:, i, 0:512]))
            elif lo == SZ0:
                for i in range(NT):
                    tmaj(key, 0, MIX, i, func(ACT.Silu, self.sg[:, i, 512:768]))
            elif lo in (RW0, RW0 + 512):
                for c in range((lo - RW0) // P, (hi - RW0) // P):
                    fm(key, width, RW0 + c * P - lo, P, self.rwT[:, c, 1:])
            elif lo == RWZ0:
                for i in range(NT):
                    tmaj(key, 0, MIX, i, func(ACT.Silu, self.z_rw[:, i, :]))
            elif lo == NQ0:
                for h in range(H):
                    fm(key, width, h * E, E, self.nsa_qT[0:E, h, :])
                for j in range(3):
                    fm(key, width, MIX + j * E, E, self.nsa_kvT[0:E, j, :])
                for i in range(NT):
                    tmaj(key, MIX + 3 * E, E, i, copy(self.ns[:, i, TM_VS:TM_VS + E]), by="dve")
            else:
                fm(key, width, 0, E, self.nsa_kvT[0:E, 3, :])
                for i in range(NT):
                    tmaj(key, E, E, i, copy(self.ns[:, i, TM_VW:TM_VW + E]), by="dve")
                    tmaj(key, 2 * E, 12, i, func(ACT.Sigmoid, self.ns[:, i, TM_NG:TM_NG + 12]))
                for i in range(NT):
                    tmaj(key, 2 * E + 12, MIX, i, func(ACT.Silu, self.ns[:, i, TM_NZ:TM_NZ + MIX]))
            tiles[first]["takes"] = [(key, width)]
            tiles[-1]["frees"] = 1
        self.products("p1", tiles, self.norm)

    def attention(self, name, units, groups, parts=1, joint=1):
        nc = self.nc
        keep = self.top
        N = len(units)
        self.row_sum = self.take(N * parts)
        row_max = self.take(N * parts)
        wait_joint = joint if joint > 1 else 0
        NROW = (3 + 2 * wait_joint) * parts
        rows = self.take(NROW, T)
        turned = self.take(2, T)
        S_BANKS, T_BANK, O_BANK = 4, 4, 6
        sig = self.att
        row = lambda q, m: rows[:, q % NROW, 0:m]
        mixes = [sum(bool(u.get("mix")) for u in units[:n + 1]) for n in range(N)]
        last_unit = {}
        for n, u in enumerate(units):
            last_unit[u["group"]] = n

        def steps(*stages):
            for step in range(N + max(lag for lag, _ in stages)):
                for lag, run in stages:
                    if 0 <= step - lag < N:
                        run(step - lag, units[step - lag])

        with nc.Block() as block:
            @block.tensor
            def _(pe):
                def scores(n, u):
                    for j, part in enumerate(u["parts"]):
                        q = n * parts + j
                        if q >= S_BANKS:
                            if part.get("table") is not None:
                                pe.wait_ge(*sig.maxima.at(n - S_BANKS + 1))
                            else:
                                pe.wait_ge(*sig.exps.at(q - S_BANKS + 1))
                        lhsT, rhs = part["scores"]
                        pe.matmul(self.bank[q % S_BANKS][:, 0:part["n"]], lhsT, rhs, start=True, stop=True)\
                          .then_inc(*sig.scores.one())

                def turn(n, u):
                    if u.get("mix"):
                        pe.wait_ge(*sig.mixed.at(mixes[n]))
                    else:
                        pe.wait_ge(*sig.exps.at(n * parts + 1))
                    if n >= 2:
                        pe.wait_ge(*sig.copied.at(n - 1))
                    for b, v in enumerate(u["values"]):
                        k = v.shape[0]
                        ins = pe.transpose(self.bank[T_BANK + n % 2][0:k, b * P:(b + 1) * P],
                                           rows[:, n * parts % NROW, b * P:b * P + k], self.ident[:])
                    ins.then_inc(*sig.turned.one())

                def sums(n, u):
                    g = u["group"]
                    pe.wait_ge(*sig.copied.at(n + 1))
                    if g >= 2:
                        pe.wait_ge(*sig.finished.at(g - 1))
                    lo, hi = u["cols"]
                    for b, v in enumerate(u["values"]):
                        k = v.shape[0]
                        ins = pe.matmul(self.bank[O_BANK + g % 2][:, lo:hi], turned[0:k, n % 2, b * P:(b + 1) * P],
                                        v, start=b == 0 and n % joint == 0,
                                        stop=b == len(u["values"]) - 1 and n % joint == joint - 1)
                    ins.then_inc(*sig.summed.one())
                steps((0, scores), (2 + wait_joint, turn), (3 + wait_joint, sums))

            @block.vector
            def _(dve):
                seq = self.order(dve, self.dve_order)

                def maxima(n, u):
                    for j, part in enumerate(u["parts"]):
                        q, m = n * parts + j, part["n"]
                        dve.wait_ge(*sig.scores.at(q + 1))
                        s = self.bank[q % S_BANKS][:, 0:m]
                        if part.get("table") is None:
                            ins = dve.tensor_reduce(row_max[:, q:q + 1], s, AX_X, ALU.max, negate=True)
                            if j < parts - 1:
                                ins.then_inc(*self.dve_order.one())
                        else:
                            if q >= NROW:
                                dve.wait_ge(*sig.turned.at(n - NROW + 1))
                            ins = dve.tensor_tensor_reduce(row(q, m), s, part["table"], 0.125, -3e38,
                                                           ALU.add, ALU.max, row_max[:, q:q + 1])
                            if n % joint == joint - 1:
                                seq(ins)
                                if joint > 1:
                                    own = row_max[:, n - joint + 1:n + 1]
                                    seq(dve.tensor_reduce(self.scratch[:, 0:1], own, AX_X, ALU.max))
                                    ins = dve.tensor_scalar(own, self.scratch[:, 0:1].broadcast_to([P, joint]), -1.0,
                                                            None, ALU.mult)
                                else:
                                    ins = dve.tensor_scalar(row_max[:, q:q + 1], row_max[:, q:q + 1], -1.0, None,
                                                            ALU.mult)
                    ins.then_inc(*sig.maxima.one())

                def mix(n, u):
                    if u.get("mix"):
                        q = n * parts
                        dve.wait_ge(*sig.exps.at(q + parts))
                        u["mix"](dve, seq, q, [row(q + j, part["n"]) for j, part in enumerate(u["parts"])])\
                            .then_inc(*sig.mixed.one())

                def finish(n, u):
                    if last_unit[u["group"]] == n:
                        dve.wait_ge(*sig.summed.at(n + 1))
                        groups[u["group"]](dve, seq, self.bank[O_BANK + u["group"] % 2])\
                            .then_inc(*sig.finished.one())
                steps((0, maxima), (1 + wait_joint, mix), (4 + wait_joint, finish))

            @block.scalar
            def _(act):
                def exps(n, u):
                    act.wait_ge(*sig.maxima.at(n // joint * joint + joint))
                    for j, part in enumerate(u["parts"]):
                        q, m = n * parts + j, part["n"]
                        if q >= NROW:
                            act.wait_ge(*sig.turned.at((q - NROW) // parts + 1))
                        act.activation(row(q, m), self.bank[q % S_BANKS][:, 0:m] if part.get("table") is None
                                       else row(q, m), ACT.Exp, bias=row_max[:, q:q + 1],
                                       accum_out=self.row_sum[:, q:q + 1]).then_inc(*sig.exps.one())

                def copy(n, u):
                    act.wait_ge(*sig.turned.at(n + 1))
                    if n >= 2:
                        act.wait_ge(*sig.summed.at(n - 1))
                    m, k = P * len(u["values"]), u["values"][0].shape[0]
                    act.activation(turned[0:k, n % 2, 0:m], self.bank[T_BANK + n % 2][0:k, 0:m], ACT.Copy)\
                       .then_inc(*sig.copied.one())
                steps((wait_joint, exps), (2 + wait_joint, copy))

            @block.sync
            def _(sp):
                self.w.feed(sp)
        self.top = keep
        self.end_stage(name)

    def sparse_attention(self):
        nc, a = self.nc, self.a
        NC = T // 16 - 1
        keep = self.top
        self.y_nsa = self.take(NT, MIX)
        kcT = self.take(NC)
        vc = self.take(E)
        o = self.top
        w1 = self.take(2, 32, E)
        w2 = self.take(2, E)
        pos_rows = self.take(E)
        posT = self.take(2, 32)
        blocks = self.take(2, 32, NC)
        hidden = self.take(2, NC)
        kvT = self.nsa_kvT
        landed, seqs = self.params_landed, self.order
        with nc.Block() as block:
            @block.scalar
            def _(act):
                act.dma_start(pos_rows[0:E, :], a["nsa_cmp_pos"][0].rearrange("j p e -> (j p) e"))\
                   .then_inc(*landed.dma())
                for j in range(2):
                    act.dma_start(w1[0:E, j], a["nsa_cmp_w1"][0, j].rearrange("(p e) h -> e p h", e=E))\
                       .then_inc(*landed.dma())
                    act.dma_start(w2[0:E, j], a["nsa_cmp_w2"][0, j]).then_inc(*landed.dma())
                for j in range(2):
                    act.wait_ge(*self.mm_done.at(j + 2))
                    act.activation(hidden[0:E, j, :], self.bank[1 + j][0:E, 0:NC], ACT.Gelu_apprx_tanh)\
                       .then_inc(*self.act_ready.one())

            @block.tensor
            def _(pe):
                pe.wait_ge(*landed.all_of_stage(16 * 5))
                pe.transpose(self.bank[0][0:E, 0:E], pos_rows[0:E, :], self.ident[0:E, 0:E])\
                  .then_inc(*self.mm_done.one())
                for j in range(2):
                    pe.wait_ge(*self.dve_ready.at(2 * j + 2))
                    for p in range(32):
                        ins = pe.matmul(self.bank[1 + j][0:E, 0:NC], w1[0:E, j, p, :], blocks[0:E, j, p, :],
                                        start=p == 0, stop=p == 31)
                    ins.then_inc(*self.mm_done.one())
                pe.wait_ge(*self.act_ready.at(2))
                pe.matmul(self.bank[3][0:E, 0:NC], w2[0:E, 0, :], hidden[0:E, 0, :], start=True, stop=True)\
                  .then_inc(*self.mm_done.one())
                pe.matmul(self.bank[4][0:NC, 0:E], hidden[0:E, 1, :], w2[0:E, 1, :], start=True, stop=True)\
                  .then_inc(*self.mm_done.one())

            @block.vector
            def _(dve):
                seq = seqs(dve, self.dve_order)
                dve.wait_ge(*self.mm_done.at(1))
                seq(dve.tensor_copy(posT[0:E], self.bank[0][0:E, 0:E].rearrange("p (j q) -> p j q", j=2)))
                for j in range(2):
                    x = kvT[0:E, j, :].rearrange("e (n p) -> e p n", p=16)
                    for half in range(2):
                        ps = slice(16 * half, 16 * half + 16)
                        dve.tensor_tensor(blocks[0:E, j, ps, :], x[:, :, half:half + NC],
                                          posT[0:E, j, ps].unsqueeze(2).broadcast_to([E, 16, NC]), ALU.add)\
                           .then_inc(*self.dve_ready.one())
                dve.wait_ge(*self.mm_done.at(4))
                dve.tensor_copy(kcT[0:E, :], self.bank[3][0:E, 0:NC]).then_inc(*self.dve_order.one())
                dve.wait_ge(*self.mm_done.at(5))
                dve.tensor_copy(vc[0:NC, :], self.bank[4][0:NC, 0:E]).then_inc(*self.dve_order.one())

            @block.sync
            def _(sp):
                self.w.feed(sp)
        self.top = o
        self.end_stage("nsa_compress")

        SLOPES = [2.0 ** (-8.0 * (h + 1) / H) for h in range(H)]
        dist = self.scratch[:]
        sel = self.take(H, T)
        win = self.take(H, 3 * P)
        cmp = self.take(NT, H, NC)
        seen = self.take(NT, NC)
        gsum = self.take(H)
        with nc.Block() as block:
            @block.gpsimd
            def _(pool):
                pool.iota(dist, [[-1, T]], base=3 * P, channel_multiplier=1, allow_small_or_imprecise_dtypes=True)\
                    .then_inc(*self.pool_ready.one())
                pool.iota(seen, [[P, NT], [-16, NC]], base=-31, channel_multiplier=1,
                          allow_small_or_imprecise_dtypes=True).then_inc(*self.pool_ready.one())
                seq = seqs(pool, self.pool_order)
                pool.wait_ge(*self.dve_ready.at(1))
                pool.affine_select(out=sel, in_=sel, compare_op=ALU.is_ge, fill=NEG, base=3 * P,
                                   pattern=[[0, H], [-1, T]], channel_multiplier=1).then_inc(*self.pool_order.one())
                seq(pool.affine_select(out=win, in_=win, compare_op=ALU.is_ge, fill=NEG, base=2 * P,
                                       pattern=[[0, H], [-1, 3 * P]], channel_multiplier=1))
                pool.affine_select(out=win, in_=win, compare_op=ALU.is_ge, fill=NEG, base=255 - 2 * P,
                                   pattern=[[0, H], [1, 3 * P]], channel_multiplier=-1)\
                    .then_inc(*self.pool_order.one())
                pool.affine_select(out=cmp, in_=cmp, compare_op=ALU.is_ge, fill=NEG, base=-31,
                                   pattern=[[P, NT], [0, H], [-16, NC]], channel_multiplier=1)\
                    .then_inc(*self.pool_order.one())
            @block.vector
            def _(dve):
                dve.wait_ge(*self.pool_ready.at(2))
                for h in range(H):
                    s = -8.0 * SLOPES[h]
                    dve.tensor_scalar(sel[:, h, :], dist, s, None, ALU.mult).then_inc(*self.dve_order.one())
                    dve.tensor_scalar(win[:, h, :], dist[:, P:], s, None, ALU.mult)\
                       .then_inc(*self.dve_order.one())
                    dve.tensor_scalar(cmp[:, :, h, :], seen, s, None, ALU.mult).then_inc(*self.dve_order.one())
                dve.wait_ge(*self.dve_order.all())
                dve.tensor_scalar(seen, seen, 0.0, None, ALU.is_ge).then_inc(*self.dve_ready.one())

            @block.sync
            def _(sp):
                self.w.feed(sp)
        self.end_stage("nsa_tables")

        units, groups = [], []
        part_of = {}
        q = 0
        for i in range(NT):
            qs = [self.nsa_qT[0:E, h, i * P:(i + 1) * P] for h in range(H)]
            kinds = [(0, 0, None), (1, 0, TM_VS), (2, max(0, i - 2), TM_VW)]
            for kind, b0, vcol in kinds:
                g = len(groups)
                part_of[g] = q
                for h in range(H):
                    if kind == 0:
                        part = dict(scores=(qs[h], kcT[0:E, :]), n=NC, table=cmp[:, i, h, :])
                        values = [vc[0:NC, :]]
                    else:
                        nk = (i + 1 - b0) * P
                        table = sel[:, h, T - nk:] if kind == 1 else win[:, h, 3 * P - nk:]
                        part = dict(scores=(qs[h], kvT[0:E, 1 + kind, b0 * P:(i + 1) * P]), n=nk, table=table)
                        values = [self.ns[:, b, vcol:vcol + E] for b in range(b0, i + 1)]
                    units.append(dict(parts=[part], values=values, cols=(h * E, (h + 1) * E), group=g))
                    if kind == 0:
                        units[-1]["mix"] = lambda dve, seq, q, rows, i=i: dve.tensor_tensor(
                            rows[0], rows[0], seen[:, i, :], ALU.mult)
                    q += 1

                def take_out(dve, seq, bank, i=i, kind=kind, g=g):
                    q0 = part_of[g]
                    y = self.y_nsa[:, i, :].rearrange("p (h e) -> p h e", h=H)
                    sums = bank[:, 0:MIX].rearrange("p (h e) -> p h e", h=H)
                    gate = self.ns[:, i, TM_NG:TM_NG + 12].rearrange("p (h c) -> p h c", c=3)[:, :, kind]
                    seq(dve.reciprocal(gsum, self.row_sum[:, q0:q0 + H]))
                    seq(dve.tensor_tensor(gsum, gsum, gate, ALU.mult))
                    by = gsum.unsqueeze(2).broadcast_to([P, H, E])
                    if kind == 0:
                        return dve.tensor_tensor(y, sums, by, ALU.mult)
                    part = self.scratch[:, 0:MIX].rearrange("p (h e) -> p h e", h=H)
                    seq(dve.tensor_tensor(part, sums, by, ALU.mult))
                    ins = dve.tensor_tensor(y, y, part, ALU.add)
                    if kind == 2:
                        seq(ins)
                        ins = dve.tensor_tensor(self.y_nsa[:, i, :], self.y_nsa[:, i, :],
                                                self.ns[:, i, TM_NZ:TM_NZ + MIX], ALU.mult)
                    return ins
                groups.append(take_out)
        self.attention("nsa", units, groups)
        self.top = keep + NT * MIX

    def spatial_gating(self):
        nc, a = self.nc, self.a
        keep = self.top
        gain, bias = self.take(MIX), self.take(MIX)
        w_rows = self.take(H, P)
        wT = self.take(H, P)
        vc, sq = self.take(NT, MIX), self.take(NT, MIX)
        mean, rstd = self.take(NT, H), self.take(NT, H)
        y = vc
        groups = lambda x: x.rearrange("p i (g c) -> p i g c", g=H)
        over = lambda x: x.unsqueeze(3).broadcast_to([P, NT, H, E])
        u, v, z = (self.sg[:, :, j * MIX:(j + 1) * MIX] for j in range(3))
        self.dve_ready.order_of(["var", "normed", "wT"] + [("y", i) for i in range(NT)])
        self.mm_done.order_of(["wT"] + [("mixed", g) for g in range(H)] + [("nsa", c) for c in range(2)]
                              + [("y", c) for c in range(2)])
        with nc.Block() as block:
            @block.scalar
            def _(act):
                act.dma_start(gain, a["sg_ln_gain"].broadcast_to([P, MIX])).then_inc(*self.params_landed.dma())
                act.dma_start(bias, a["sg_ln_bias"].broadcast_to([P, MIX])).then_inc(*self.params_landed.dma())
                act.dma_start(w_rows, a["sg_w_s"][0].rearrange("g t s -> t g s")).then_inc(*self.params_landed.dma())
                seq = self.order(act, self.act_order)
                act.wait_ge(*self.dve_ready.after("var"))
                seq(act.activation(rstd, rstd, ACT.Ln))
                act.activation(rstd, rstd, ACT.Exp, scale=-0.5).then_inc(*self.act_ready.one())
                for c in range(2):
                    act.wait_ge(*self.mm_done.after(("nsa", c)))
                    act.activation(self.ysT[:, 6 + c, :], self.bank[5 + c][:], ACT.Copy)\
                       .then_inc(*self.evac_act.one())
                for c in range(2):
                    act.wait_ge(*self.mm_done.after(("y", c)))
                    act.activation(self.ysT[:, 2 + c, :], self.bank[5 + c][:], ACT.Copy)\
                       .then_inc(*self.evac_act.one())

            @block.gpsimd
            def _(pool):
                pool.wait_ge(*self.params_landed.all_of_stage(48))
                pool.affine_select(out=w_rows, in_=w_rows, compare_op=ALU.is_ge, fill=0.0, base=0,
                                   pattern=[[0, H], [-1, P]], channel_multiplier=1)\
                    .then_inc(*self.pool_ready.one())

            @block.tensor
            def _(pe):
                def turn(src, first, name):
                    for c in range(2):
                        for i in range(NT):
                            ins = pe.transpose(self.bank[5 + c][:, i * P:(i + 1) * P],
                                               src[:, i, c * P:(c + 1) * P], self.ident[:])
                        ins.then_inc(*self.mm_done.step((name, c)))
                pe.wait_ge(*self.pool_ready.at(1))
                for g in range(H):
                    ins = pe.transpose(self.bank[0][:, g * P:(g + 1) * P], w_rows[:, g, :], self.ident[:])
                ins.then_inc(*self.mm_done.step("wT"))
                pe.wait_ge(*self.dve_ready.after("wT"))
                for g in range(H):
                    pe.matmul(self.bank[1 + g][:, 0:MIX], wT[:, g, :], v[:, :, g * E:(g + 1) * E],
                              start=True, stop=True).then_inc(*self.mm_done.step(("mixed", g)))
                turn(self.y_nsa, 6, "nsa")
                pe.wait_ge(*self.dve_ready.after(("y", NT - 1)))
                pe.wait_ge(*self.evac_act.at(2))
                turn(y, 2, "y")

            @block.vector
            def _(dve):
                seq = self.order(dve, self.dve_order)
                seq(dve.tensor_reduce(mean, groups(v), AX_X, ALU.add))
                seq(dve.tensor_scalar(mean, mean, 1.0 / E, None, ALU.mult))
                seq(dve.tensor_tensor(groups(vc), groups(v), over(mean), ALU.subtract))
                seq(dve.tensor_tensor(sq, vc, vc, ALU.mult))
                seq(dve.tensor_reduce(rstd, groups(sq), AX_X, ALU.add))
                dve.tensor_scalar(rstd, rstd, 1.0 / E, 1e-5, ALU.mult, ALU.add).then_inc(*self.dve_ready.step("var"))
                dve.wait_ge(*self.act_ready.at(1))
                seq(dve.tensor_tensor(groups(vc), groups(vc), over(rstd), ALU.mult))
                dve.wait_ge(*self.params_landed.all_of_stage(48))
                each = lambda row: row.unsqueeze(1).broadcast_to([P, NT, MIX])
                seq(dve.tensor_tensor(vc, vc, each(gain), ALU.mult))
                dve.tensor_tensor(v, vc, each(bias), ALU.add).then_inc(*self.dve_ready.step("normed"))
                dve.wait_ge(*self.mm_done.after("wT"))
                dve.tensor_copy(wT, self.bank[0][:].rearrange("p (g t) -> p g t", g=H))\
                   .then_inc(*self.dve_ready.step("wT"))
                dve.wait_ge(*self.dve_ready.after("normed"))
                for g in range(H):
                    dve.wait_ge(*self.mm_done.after(("mixed", g)))
                    cols = slice(g * E, (g + 1) * E)
                    b = self.par[:, PAR["sg_b_s"] + g:PAR["sg_b_s"] + g + 1]
                    dve.scalar_tensor_tensor(y[:, :, cols], self.bank[1 + g][:, 0:MIX].rearrange(
                        "p (i c) -> p i c", i=NT), b, u[:, :, cols], ALU.add, ALU.mult)\
                       .then_inc(*self.dve_order.one())
                dve.wait_ge(*self.dve_order.all())
                for i in range(NT):
                    dve.tensor_tensor(y[:, i, :], y[:, i, :], z[:, i, :], ALU.mult)\
                       .then_inc(*self.dve_ready.step(("y", i)))

            @block.sync
            def _(sp):
                self.w.feed(sp)
        self.top = keep
        self.end_stage("sg")

    def mixer_preparation(self):
        nc, a = self.nc, self.a
        CH = 64
        self.top = self.after_mixer_inputs
        self.until = self.take(P)
        self.beyond = self.take(P)
        self.strict = self.take(P)
        self.levels = self.take(6, P)
        self.chunk_of = self.take(2)
        self.beta = self.take(NT, H)
        self.g = self.take(NT, H)
        self.wa = self.take(NT, 2 * MIX)
        self.y_gdn = self.take(NT, MIX)
        self.y_rw = self.take(NT, MIX)
        keep = self.top
        acc = self.take(2, T)
        dtb, alog = self.take(H), self.take(H)
        low, small = self.take(NT, H), self.take(NT, H)
        w0a0 = self.take(2 * MIX)
        up = self.take(MIX)
        qkvT, rwT = self.qkvT, self.rwT
        landed = self.params_landed
        self.pool_ready.order_of(["masks", "zeros"])
        self.dve_ready.order_of(["shifted", "g0"] + [("conv", c) for c in range(6)] + [("wa", i) for i in range(NT)])
        self.act_ready.order_of(["tanh", "softplus", "alog"] + [("conv", c) for c in range(6)] + ["beta"]
                                + [("wa", i) for i in range(NT)])
        with nc.Block() as block:
            @block.gpsimd
            def _(pool):
                seq = self.order(pool, self.pool_order)
                pool.memset(qkvT[:, :, 0:3], 0.0).then_inc(*self.pool_order.one())
                seq(pool.memset(rwT[:, :, 0:1], 0.0))
                pool.memset(self.levels, 0.0).then_inc(*self.pool_order.one())
                pool.memset(self.until, 1.0).then_inc(*self.pool_order.one())
                pool.memset(self.beyond, 1.0).then_inc(*self.pool_order.one())
                pool.memset(self.strict, 1.0).then_inc(*self.pool_order.one())
                seq(pool.memset(self.chunk_of, 1.0))

                def select(v, base, pattern, cm, fill=0.0):
                    seq(pool.affine_select(out=v, in_=v, compare_op=ALU.is_ge, fill=fill, base=base, pattern=pattern,
                                           channel_multiplier=cm))
                for m, sign, base in ((self.until, 1, 0), (self.beyond, -1, -1), (self.strict, 1, -1)):
                    v = m.rearrange("p (b u) -> p b u", u=CH)
                    select(v, 0, [[-CH, 2], [0, CH]], 1)
                    select(v, CH - 1, [[CH, 2], [0, CH]], -1)
                    select(m, base, [[sign, P]], -sign)
                select(self.chunk_of, 0, [[-CH, 2]], 1)
                select(self.chunk_of, CH - 1, [[CH, 2]], -1)
                for l in range(6):
                    b = 1 << l
                    v = self.levels[:, l, :].rearrange("p (n u) -> p n u", u=2 * b)[:, :, b:2 * b]
                    n = P // (2 * b)
                    seq(pool.memset(v, 1.0))
                    select(v, 0, [[-2 * b, n], [0, b]], 1)
                    select(v, b - 1, [[2 * b, n], [0, b]], -1)
                pool.memset(self.scratch[0:1, 0:1], 0.0).then_inc(*self.pool_ready.step("masks"))
                pool.memset(self.scratch[0:1, 1:2], 0.0).then_inc(*self.pool_ready.step("zeros"))

            @block.scalar
            def _(act):
                act.dma_start(dtb, a["gdn_dt_bias"].broadcast_to([P, H])).then_inc(*landed.dma())
                act.dma_start(alog, a["gdn_a_log"].broadcast_to([P, H])).then_inc(*landed.dma())
                act.dma_start(w0a0[:, 0:MIX], a["rw_w0"].broadcast_to([P, MIX])).then_inc(*landed.dma())
                act.dma_start(w0a0[:, MIX:], a["rw_a0"].broadcast_to([P, MIX])).then_inc(*landed.dma())
                act.dma_start(up[0:E, :], a["rw_w_up"][0]).then_inc(*landed.dma())
                act.dma_start(up[E:P, :], a["rw_a_up"][0]).then_inc(*landed.dma())
                seq = self.order(act, self.act_order)
                act.wait_ge(*self.dve_ready.after("shifted"))
                act.activation(rwT[0:E, 6, 1:], rwT[0:E, 6, 1:], ACT.Tanh).then_inc(*self.act_ready.step("tanh"))
                act.wait_ge(*self.dve_ready.after("g0"))
                seq(act.activation(small, small, ACT.Exp, scale=-1.0))
                act.activation(small, small, ACT.Ln, bias=1.0).then_inc(*self.act_ready.step("softplus"))
                act.wait_ge(*landed.all_of_stage(96))
                act.activation(alog, alog, ACT.Exp).then_inc(*self.act_ready.step("alog"))
                for c in range(6):
                    act.wait_ge(*self.dve_ready.after(("conv", c)))
                    act.activation(qkvT[:, c, 3:], acc[:, c % 2, :], ACT.Silu)\
                       .then_inc(*self.act_ready.step(("conv", c)))
                act.activation(self.beta, self.ab[:, :, H:], ACT.Sigmoid).then_inc(*self.act_ready.step("beta"))
                for i in range(NT):
                    act.wait_ge(*self.dve_ready.after(("wa", i)))
                    act.activation(self.wa[:, i, :], self.wa[:, i, :], ACT.Sigmoid)\
                       .then_inc(*self.act_ready.step(("wa", i)))

            @block.tensor
            def _(pe):
                pe.wait_ge(*self.act_ready.after("tanh"))
                pe.wait_ge(*landed.all_of_stage(96))
                for i in range(NT):
                    pe.matmul(self.bank[i][:, 0:MIX], rwT[0:E, 6, 1 + i * P:1 + (i + 1) * P], up[0:E, :],
                              start=True, stop=True)
                    pe.matmul(self.bank[i + 4][:, 0:MIX], rwT[E:P, 6, 1 + i * P:1 + (i + 1) * P], up[E:P, :],
                              start=True, stop=True).then_inc(*self.mm_done.one())

            @block.vector
            def _(dve):
                seq = self.order(dve, self.dve_order)
                dve.wait_ge(*self.pool_ready.after("zeros"))
                for c in (6, 0, 1, 2, 3, 4, 5):
                    mu = self.par[:, PAR["rw_mu"] + c:PAR["rw_mu"] + c + 1]
                    seq(dve.tensor_tensor(acc[:, 0, :], rwT[:, c, 0:T], rwT[:, c, 1:], ALU.subtract))
                    ins = dve.scalar_tensor_tensor(rwT[:, c, 1:], acc[:, 0, :], mu, rwT[:, c, 1:], ALU.mult, ALU.add)
                    if c == 6:
                        ins.then_inc(*self.dve_ready.step("shifted"))
                        dve.wait_ge(*self.dve_ready.after("shifted"))
                    else:
                        seq(ins)
                dve.wait_ge(*landed.all_of_stage(96))
                seq(dve.tensor_tensor(low, self.ab[:, :, 0:H], dtb.unsqueeze(1).broadcast_to([P, NT, H]), ALU.add))
                dve.scalar_tensor_tensor(small, low, -1.0, low, ALU.mult, ALU.max).then_inc(*self.dve_ready.step("g0"))
                dve.wait_ge(*self.dve_ready.after("g0"))
                seq(dve.tensor_scalar(low, low, 0.0, None, ALU.max))
                dve.wait_ge(*self.act_ready.after("alog"))
                seq(dve.tensor_tensor(low, low, small, ALU.add))
                seq(dve.tensor_tensor(low, low, alog.unsqueeze(1).broadcast_to([P, NT, H]), ALU.mult))
                seq(dve.tensor_scalar(self.g, low, -1.0, None, ALU.mult))
                for c in range(6):
                    if c >= 2:
                        dve.wait_ge(*self.act_ready.after(("conv", c - 2)))
                    w = lambda j: self.par[:, PAR["gdn_conv"] + 6 * j + c:PAR["gdn_conv"] + 6 * j + c + 1]
                    seq(dve.tensor_scalar(acc[:, c % 2, :], qkvT[:, c, 0:T], w(0), None, ALU.mult))
                    for j in range(1, 4):
                        ins = dve.scalar_tensor_tensor(acc[:, c % 2, :], qkvT[:, c, j:j + T], w(j), acc[:, c % 2, :],
                                                       ALU.mult, ALU.add)
                        if j < 3:
                            seq(ins)
                    ins.then_inc(*self.dve_ready.step(("conv", c)))
                for i in range(NT):
                    dve.wait_ge(*self.mm_done.at(i + 1))
                    dve.tensor_tensor(self.wa[:, i, 0:MIX], self.bank[i][:, 0:MIX], w0a0[:, 0:MIX], ALU.add)\
                       .then_inc(*self.dve_order.one())
                    dve.tensor_tensor(self.wa[:, i, MIX:], self.bank[i + 4][:, 0:MIX], w0a0[:, MIX:], ALU.add)\
                       .then_inc(*self.dve_ready.step(("wa", i)))

            @block.sync
            def _(sp):
                self.w.feed(sp)
        self.top = keep
        self.end_stage("prep")

    def recurrence(self, kind, take, bank, square):
        a = self.a
        gdn = kind == "gdn"
        CH = 64
        LEVELS = 6
        hd = lambda x: x.rearrange("p (h e) -> p h e", h=H)
        over = lambda x: x.unsqueeze(2).broadcast_to([P, H, E])
        y = self.y_gdn if gdn else self.y_rw
        z = self.z_gdn if gdn else self.z_rw
        srcT = self.qkvT if gdn else self.rwT
        first = 3 if gdn else 1
        head = lambda x: x.rearrange("p (h t) -> p h t", h=H)
        F = [take(H, P)[0:E] for j in range(4)]
        LT, M, T1, TT = (take(H, P) for _ in range(4))
        X = take(H, P)
        OB = take(H, P)
        raw = take(3, MIX)
        q, k, v = (raw[:, j, :] for j in range(3))
        U, Un = take(MIX), take(MIX)
        WT = take(H, P)
        S, Sd = take(MIX), take(MIX)
        dec = take(2 * H)
        sq, ss = take(2 * MIX), take(2 * H)
        if gdn:
            D = take(H, P)
            eg, gc = take(2 * H), take(H)
            kn, kb, qn, q_in, kbg, vb, ko = (take(MIX) for _ in range(7))
            fm_src = [kn, kb, qn, q_in]
            w_tm, state_ops, o_ops = kbg, [(ko, Un)], [(OB, Un)]
            norm_w = take(E)
        else:
            GT, HK = take(H, P), take(H, P)
            ld, cm, ec, er, en, ep = (take(MIX) for _ in range(6))
            kk, kp, b = (take(MIX) for _ in range(3))
            A, B, K, R, Bh, Kh = ep, sq[:, 0:MIX], sq[:, MIX:], ec, b, er
            fm_src = [B, A, R, K]
            w_tm, state_ops, o_ops = A, [(Bh, Un), (Kh, v)], [(OB, Un), (HK, v)]
            GV = cm
            bonus = take(NT, MIX)
            rows = take(5, MIX)
            k_k, k_a, r_k, gn_gain, gn_bias = (rows[:, j, :] for j in range(5))
        post = take(NT, H)
        mean = take(NT, H)
        landed = self.params_landed

        pe_steps, dve_steps, act_steps = [], ["S0"], []
        for i in range(NT):
            pe_steps += [(i, "in"), (i, "cum")] + [(i, "fm", j) for j in range(4)]
            pe_steps += [(i, "LT"), (i, "OB")] + ([] if gdn else [(i, "GT"), (i, "HK")]) + [(i, "T0")]
            for l in range(1, LEVELS):
                pe_steps += [(i, "X", l)] + [(i, "dT", l)] * (l < LEVELS - 1) + [(i, "dTT", l)]
            pe_steps += ([] if gdn else [(i, "GV")]) + [(i, "U"), (i, "WT")]
            for c in range(2):
                pe_steps += [(i, "WS", c), (i, "O", c), (i, "S", c)]
            dve_steps += ([(i, "gc"), (i, "D")] if gdn else [(i, "ld"), (i, "cm")]) + [(i, "ss")]
            dve_steps += [(i, "src", j) for j in range(4)] + [(i, "F", 1), (i, "F", 3)]
            dve_steps += [(i, "LT"), (i, "OB")] + ([] if gdn else [(i, "GT"), (i, "HK")]) + [(i, "TT", 0)]
            for l in range(1, LEVELS):
                dve_steps += [(i, "M", l)] + [(i, "T", l)] * (l < LEVELS - 1) + [(i, "TT", l)]
            dve_steps += ([] if gdn else [(i, "GV")]) + [(i, "U"), (i, "WT")]
            for c in range(2):
                dve_steps += [(i, "Un", c), (i, "S", c)]
            act_steps += [(i, "raw"), (i, "e"), (i, "eD"), (i, "rs"), (i, "F", 0), (i, "F", 2), (i, "T0")]
            act_steps += [(i, "X", l) for l in range(1, LEVELS)] + [(i, "y")]
        dve_steps += ["ss", "y"]
        act_steps += ["rs"] + [("out", c) for c in range(2)]
        pe_steps += [("out", c) for c in range(2)]
        pe_done, dve_done, act_done = self.recurrence_done[kind]
        pe_done.order_of(pe_steps)
        dve_done.order_of(dve_steps)
        act_done.order_of(act_steps)
        def tensor(pe):
            for i in range(NT):
                ts = slice(first + i * P, first + (i + 1) * P)
                if i:
                    pe.wait_ge(*act_done.after((i - 1, "y")))
                    pe.wait_ge(*dve_done.after((i - 1, "S", 1)))
                for c in range(6):
                    ins = pe.transpose(bank[c // 4][:, c % 4 * P:c % 4 * P + P], srcT[:, c, ts], self.ident[:])
                ins.then_inc(*pe_done.step((i, "in")))
                if not gdn:
                    yield
                if gdn:
                    pe.matmul(bank[2][:, 0:H], self.until, self.g[:, i, :], start=True, stop=True)
                    pe.matmul(bank[2][:, H:2 * H], self.beyond, self.g[:, i, :], start=True, stop=True)
                    for h in range(H):
                        gh = self.g[:, i, h:h + 1]
                        pe.matmul(bank[2][0:E, 8 + 2 * h:10 + 2 * h], gh.broadcast_to([P, E]), self.chunk_of,
                                  start=True, stop=True)
                        ins = pe.matmul(bank[3][:, h * P:(h + 1) * P], gh.broadcast_to([P, P]), self.until,
                                        start=True, stop=True)
                else:
                    pe.wait_ge(*dve_done.after((i, "ld")))
                    pe.matmul(bank[2][:, 0:MIX], self.until, ld, start=True, stop=True)
                    pe.matmul(bank[2][:, MIX:], self.beyond, ld, start=True, stop=True)
                    for h in range(H):
                        ins = pe.matmul(bank[3][0:E, 2 * h:2 * h + 2], ld[:, h * E:(h + 1) * E], self.chunk_of,
                                        start=True, stop=True)
                ins.then_inc(*pe_done.step((i, "cum")))
                if gdn:
                    yield
                yield
                for j in range(4):
                    pe.wait_ge(*dve_done.after((i, "src", j)))
                    for h in range(H):
                        ins = pe.transpose(bank[j][0:E, h * P:(h + 1) * P],
                                           fm_src[j][:, h * E:(h + 1) * E], self.ident[:])
                    ins.then_inc(*pe_done.step((i, "fm", j)))
                yield
                pe.wait_ge(*act_done.after((i, "F", 2)))
                pe.wait_ge(*dve_done.after((i, "F", 3)))
                grams = [("LT", 0, 1, 0), ("OB", 0, 2, 1)] + ([] if gdn else [("GT", 3, 1, 2), ("HK", 3, 2, 3)])
                for name, l, r, b_ in grams:
                    for h in range(H):
                        ins = pe.matmul(bank[b_][:, h * P:(h + 1) * P], F[l][:, h, :], F[r][:, h, :],
                                        start=True, stop=True)
                    ins.then_inc(*pe_done.step((i, name)))
                yield
                pe.wait_ge(*dve_done.after((i, "TT", 0)))
                for h in range(H):
                    ins = pe.transpose(bank[0][:, h * P:(h + 1) * P], TT[:, h, :], self.ident[:])
                ins.then_inc(*pe_done.step((i, "T0")))
                yield
                for l in range(1, LEVELS):
                    pe.wait_ge(*dve_done.after((i, "M", l)))
                    if l == 1:
                        pe.wait_ge(*act_done.after((i, "T0")))
                    else:
                        pe.wait_ge(*dve_done.after((i, "TT", l - 1)))
                    for h in range(H):
                        ins = pe.matmul(bank[0][:, h * P:(h + 1) * P], M[:, h, :], T1[:, h, :],
                                        start=True, stop=True)
                    ins.then_inc(*pe_done.step((i, "X", l)))
                    yield
                    pe.wait_ge(*act_done.after((i, "X", l)))
                    if l < LEVELS - 1:
                        for h in range(H):
                            ins = pe.matmul(bank[1][:, h * P:(h + 1) * P], TT[:, h, :], X[:, h, :],
                                            start=True, stop=True)
                        ins.then_inc(*pe_done.step((i, "dT", l)))
                    for h in range(H):
                        ins = pe.matmul(bank[2][:, h * P:(h + 1) * P], X[:, h, :], TT[:, h, :],
                                        start=True, stop=True)
                    ins.then_inc(*pe_done.step((i, "dTT", l)))
                    yield
                pe.wait_ge(*dve_done.after((i, "TT", LEVELS - 1)))
                if not gdn:
                    for h in range(H):
                        ins = pe.matmul(bank[3][:, h * E:(h + 1) * E], GT[:, h, :], v[:, h * E:(h + 1) * E],
                                        start=True, stop=True)
                    ins.then_inc(*pe_done.step((i, "GV")))
                yield
                if not gdn:
                    pe.wait_ge(*dve_done.after((i, "GV")))
                rhs = vb if gdn else GV
                for h in range(H):
                    ins = pe.matmul(bank[0][:, h * E:(h + 1) * E], TT[:, h, :], rhs[:, h * E:(h + 1) * E],
                                    start=True, stop=True)
                ins.then_inc(*pe_done.step((i, "U")))
                for h in range(H):
                    ins = pe.matmul(bank[1][0:E, h * P:(h + 1) * P], w_tm[:, h * E:(h + 1) * E], TT[:, h, :],
                                    start=True, stop=True)
                ins.then_inc(*pe_done.step((i, "WT")))
                yield
                pe.wait_ge(*dve_done.after((i, "WT")))
                for c in range(2):
                    ps = slice(c * CH, (c + 1) * CH)
                    if c:
                        pe.wait_ge(*dve_done.after((i, "S", 0)))
                    elif i == 0:
                        pe.wait_ge(*dve_done.after("S0"))
                    for h in range(H):
                        ins = pe.matmul(bank[2][ps, h * E:(h + 1) * E], WT[0:E, h, ps], S[0:E, h * E:(h + 1) * E],
                                        start=True, stop=True)
                    ins.then_inc(*pe_done.step((i, "WS", c)))
                    yield
                    pe.wait_ge(*dve_done.after((i, "Un", c)))
                    for h in range(H):
                        hs = slice(h * E, (h + 1) * E)
                        RT = F[3] if gdn else F[2]
                        pe.matmul(bank[3][ps, hs], RT[:, h, ps], S[0:E, hs], start=True, stop=False)
                        for n, (l, r) in enumerate(o_ops):
                            ins = pe.matmul(bank[3][ps, hs], l[:, h, ps], r[:, hs], start=False,
                                            stop=n == len(o_ops) - 1)
                    ins.then_inc(*pe_done.step((i, "O", c)))
                    for h in range(H):
                        hs = slice(h * E, (h + 1) * E)
                        for n, (l, r) in enumerate(state_ops):
                            ins = pe.matmul(bank[0][0:E, hs], l[ps, hs], r[ps, hs], start=n == 0,
                                            stop=n == len(state_ops) - 1)
                    ins.then_inc(*pe_done.step((i, "S", c)))
                    yield
            pe.wait_ge(*dve_done.after("y"))
            for c in range(2):
                for i in range(NT):
                    ins = pe.transpose(bank[c][:, i * P:(i + 1) * P], y[:, i, c * P:(c + 1) * P], self.ident[:])
                ins.then_inc(*pe_done.step(("out", c)))

        def scalar(act):
            if gdn:
                act.dma_start(norm_w, a["gdn_norm"].broadcast_to([P, E])).then_inc(*landed.dma())
            else:
                for dst, n in ((k_k, "rw_k_k"), (k_a, "rw_k_a"), (gn_gain, "rw_gn_gain"), (gn_bias, "rw_gn_bias")):
                    act.dma_start(dst, a[n].broadcast_to([P, MIX])).then_inc(*landed.dma())
                act.dma_start(r_k, a["rw_r_k"].rearrange("l h e -> l (h e)").broadcast_to([P, MIX]))\
                   .then_inc(*landed.dma())
            seq = self.order(act, self.act_order)
            for i in range(NT):
                act.wait_ge(*pe_done.after((i, "in")))
                flat = raw.rearrange("p j c -> p (j c)")
                if i:
                    act.wait_ge(*dve_done.after((i - 1, "S", 1)))
                act.activation(flat[:, 0:512], bank[0][:], ACT.Copy).then_inc(*self.act_order.one())
                seq(act.activation(flat[:, 512:], bank[1][:, 0:MIX], ACT.Copy))
                act.activation(self.scratch[:, 0:1], self.ones[:, 0:1], ACT.Copy)\
                   .then_inc(*act_done.step((i, "raw")))
                if not gdn:
                    yield
                act.wait_ge(*pe_done.after((i, "cum")))
                if gdn:
                    act.activation(eg, bank[2][:, 0:2 * H], ACT.Exp).then_inc(*self.act_order.one())
                    seq(act.activation(dec[0:E, :], bank[2][0:E, 8:8 + 2 * H], ACT.Exp))
                else:
                    act.activation(ec, bank[2][:, 0:MIX], ACT.Exp).then_inc(*self.act_order.one())
                    act.activation(en, bank[2][:, 0:MIX], ACT.Exp, scale=-1.0).then_inc(*self.act_order.one())
                    act.activation(er, bank[2][:, MIX:], ACT.Exp).then_inc(*self.act_order.one())
                    seq(act.activation(dec[0:E, :], bank[3][0:E, 0:2 * H], ACT.Exp))
                act.activation(self.scratch[:, 0:1], self.ones[:, 0:1], ACT.Copy)\
                   .then_inc(*act_done.step((i, "e")))
                if gdn:
                    yield
                act.wait_ge(*dve_done.after((i, "D" if gdn else "cm")))
                if gdn:
                    act.activation(D, D, ACT.Exp).then_inc(*act_done.step((i, "eD")))
                else:
                    act.activation(ep, cm, ACT.Exp).then_inc(*act_done.step((i, "eD")))
                n = 2 * H if gdn else H
                act.wait_ge(*dve_done.after((i, "ss")))
                seq(act.activation(ss[:, 0:n], ss[:, 0:n], ACT.Ln))
                act.activation(ss[:, 0:n], ss[:, 0:n], ACT.Exp, scale=-0.5).then_inc(*act_done.step((i, "rs")))
                yield
                for j in (0, 2):
                    act.wait_ge(*pe_done.after((i, "fm", j)))
                    act.activation(F[j], head(bank[j][0:E, :]), ACT.Copy).then_inc(*act_done.step((i, "F", j)))
                yield
                yield
                act.wait_ge(*pe_done.after((i, "T0")))
                act.activation(T1, head(bank[0][:]), ACT.Copy).then_inc(*act_done.step((i, "T0")))
                yield
                for l in range(1, LEVELS):
                    act.wait_ge(*pe_done.after((i, "X", l)))
                    if l > 1:
                        act.wait_ge(*pe_done.after((i, "dTT", l - 1)))
                    act.activation(X, head(bank[0][:]), ACT.Copy).then_inc(*act_done.step((i, "X", l)))
                    yield
                    yield
                for _ in range(5):
                    yield
                act.wait_ge(*pe_done.after((i, "O", 1)))
                act.activation(y[:, i, :], bank[3][:, 0:MIX], ACT.Copy).then_inc(*act_done.step((i, "y")))
                yield
            act.wait_ge(*dve_done.after("ss"))
            seq(act.activation(post, post, ACT.Ln))
            act.activation(post, post, ACT.Exp, scale=-0.5).then_inc(*act_done.step("rs"))
            for c in range(2):
                act.wait_ge(*pe_done.after(("out", c)))
                act.activation(self.ysT[:, (0 if gdn else 4) + c, :], bank[c][:], ACT.Copy)\
                   .then_inc(*act_done.step(("out", c)))

        def vector(dve):
            seq = self.order(dve, self.dve_order)

            def fin(ins, name):
                ins.then_inc(*dve_done.step(name))
                dve.wait_ge(*dve_done.after(name))
            tt, ts_, stt = dve.tensor_tensor, dve.tensor_scalar, dve.scalar_tensor_tensor
            dve.memset(Un, 0.0).then_inc(*self.dve_order.one())
            fin(dve.memset(S[0:E, :], 0.0), "S0")
            dve.wait_ge(*landed.all_of_stage(16 * 6))
            many = lambda m: m.unsqueeze(1).broadcast_to([P, H, P])
            for i in range(NT):
                if gdn:
                    dve.wait_ge(*pe_done.after((i, "cum")))
                    dve.wait_ge(*act_done.after((i, "e")))
                    fin(dve.tensor_copy(gc, bank[2][:, 0:H]), (i, "gc"))
                    for h in range(H):
                        ins = ts_(D[:, h, :], bank[3][:, h * P:(h + 1) * P], gc[:, h:h + 1], 0.0, ALU.subtract,
                                  ALU.min)
                        if h < H - 1:
                            ins.then_inc(*self.dve_order.one())
                    dve.wait_ge(*self.dve_order.all())
                    fin(ins, (i, "D"))
                    yield
                else:
                    if i:
                        dve.wait_ge(*pe_done.after((i - 1, "S", 1)))
                    fin(ts_(ld, self.wa[:, i, 0:MIX], -math.exp(-0.5), None, ALU.mult), (i, "ld"))
                    yield
                    dve.wait_ge(*pe_done.after((i, "cum")))
                    dve.wait_ge(*act_done.after((i, "e")))
                    fin(tt(cm, bank[2][:, 0:MIX], ld, ALU.subtract), (i, "cm"))
                dve.wait_ge(*act_done.after((i, "raw")))
                if gdn:
                    flat = raw.rearrange("p j c -> p (j c)")[:, 0:512]
                    seq(tt(sq, flat, flat, ALU.mult))
                    seq(dve.tensor_reduce(ss, sq.rearrange("p (h e) -> p h e", e=E), AX_X, ALU.add))
                    fin(ts_(ss, ss, 1e-6, None, ALU.add), (i, "ss"))
                    dve.wait_ge(*act_done.after((i, "rs")))
                    beta, e_until, e_beyond = self.beta[:, i, :], eg[:, 0:H], eg[:, H:]
                    ins = tt(hd(kn), hd(k), over(ss[:, H:]), ALU.mult)
                    fin(ins, (i, "src", 0))
                    fin(tt(hd(kb), hd(kn), over(beta), ALU.mult), (i, "src", 1))
                    seq(ts_(ss[:, 0:H], ss[:, 0:H], E ** -0.5, None, ALU.mult))
                    fin(tt(hd(qn), hd(q), over(ss[:, 0:H]), ALU.mult), (i, "src", 2))
                    fin(tt(hd(q_in), hd(qn), over(e_until), ALU.mult), (i, "src", 3))
                    tt(hd(kbg), hd(kb), over(e_until), ALU.mult).then_inc(*self.dve_order.one())
                    tt(hd(vb), hd(v), over(beta), ALU.mult).then_inc(*self.dve_order.one())
                    tt(hd(ko), hd(kn), over(e_beyond), ALU.mult).then_inc(*self.dve_order.one())
                else:
                    av = self.wa[:, i, MIX:]
                    seq(tt(kk, k, k_k, ALU.mult))
                    seq(tt(sq[:, 0:MIX], kk, kk, ALU.mult))
                    seq(dve.tensor_reduce(ss[:, 0:H], hd(sq[:, 0:MIX]), AX_X, ALU.add))
                    fin(ts_(ss[:, 0:H], ss[:, 0:H], 1e-6, None, ALU.add), (i, "ss"))
                    seq(stt(kp, av, -1.0, k_a, ALU.add, ALU.mult))
                    seq(stt(kp, kp, 1.0, k, ALU.add, ALU.mult))
                    seq(tt(b, q, kp, ALU.mult))
                    seq(tt(b, b, r_k, ALU.mult))
                    seq(dve.tensor_reduce(mean[:, 0, :], hd(b), AX_X, ALU.add))
                    seq(tt(hd(bonus[:, i, :]), hd(v), over(mean[:, 0, :]), ALU.mult))
                    dve.wait_ge(*act_done.after((i, "rs")))
                    seq(tt(hd(kk), hd(kk), over(ss[:, 0:H]), ALU.mult))
                    seq(tt(b, kk, av, ALU.mult))
                    fin(tt(B, b, en, ALU.mult), (i, "src", 0))
                    fin(tt(A, kk, ep, ALU.mult), (i, "src", 1))
                    fin(tt(R, q, ec, ALU.mult), (i, "src", 2))
                    fin(tt(K, kp, en, ALU.mult), (i, "src", 3))
                    tt(Bh, b, er, ALU.mult).then_inc(*self.dve_order.one())
                    dve.wait_ge(*self.dve_order.all())
                    tt(Kh, kp, er, ALU.mult).then_inc(*self.dve_order.one())
                yield
                for j in (1, 3):
                    dve.wait_ge(*pe_done.after((i, "fm", j)))
                    dve.tensor_copy(F[j], head(bank[j][0:E, :])).then_inc(*dve_done.step((i, "F", j)))
                yield
                dve.wait_ge(*pe_done.after((i, "LT")))
                if gdn:
                    fin(tt(LT, head(bank[0][:]), D, ALU.mult), (i, "LT"))
                    dve.wait_ge(*pe_done.after((i, "OB")))
                    seq(tt(D, D, many(self.until), ALU.mult))
                    fin(tt(OB, head(bank[1][:]), D, ALU.mult), (i, "OB"))
                else:
                    fin(dve.tensor_copy(LT, head(bank[0][:])), (i, "LT"))
                    for name, dst, b_, mask in (("OB", OB, 1, self.until), ("GT", GT, 2, self.strict),
                                                ("HK", HK, 3, self.until)):
                        dve.wait_ge(*pe_done.after((i, name)))
                        fin(tt(dst, head(bank[b_][:]), many(mask), ALU.mult), (i, name))
                seq(tt(M, LT, many(self.levels[:, 0, :]), ALU.mult))
                fin(tt(TT, many(self.ident[:]), M, ALU.subtract), (i, "TT", 0))
                yield
                for l in range(1, LEVELS):
                    fin(tt(M, LT, many(self.levels[:, l, :]), ALU.mult), (i, "M", l))
                    yield
                    yield
                    dve.wait_ge(*pe_done.after((i, "dTT", l)))
                    if l < LEVELS - 1:
                        fin(tt(T1, T1, head(bank[1][:]), ALU.subtract), (i, "T", l))
                    fin(tt(TT, TT, head(bank[2][:]), ALU.subtract), (i, "TT", l))
                yield
                if not gdn:
                    dve.wait_ge(*pe_done.after((i, "GV")))
                    fin(dve.tensor_copy(GV, bank[3][:, 0:MIX]), (i, "GV"))
                yield
                dve.wait_ge(*pe_done.after((i, "U")))
                fin(ts_(U, bank[0][:, 0:MIX], 1.0 if gdn else -1.0, None, ALU.mult), (i, "U"))
                dve.wait_ge(*pe_done.after((i, "WT")))
                fin(ts_(WT[0:E], head(bank[1][0:E, :]), -1.0, None, ALU.mult), (i, "WT"))
                yield
                for c in range(2):
                    ps = slice(c * CH, (c + 1) * CH)
                    dve.wait_ge(*pe_done.after((i, "WS", c)))
                    fin(tt(Un[ps, :], bank[2][ps, 0:MIX], U[ps, :], ALU.add), (i, "Un", c))
                    yield
                    by = dec[0:E, :].rearrange("e (h c) -> e h c", c=2)[:, :, c].unsqueeze(2)\
                        .broadcast_to([E, H, E])
                    seq(tt(hd(Sd[0:E, :]), hd(S[0:E, :]), by, ALU.mult))
                    dve.wait_ge(*pe_done.after((i, "S", c)))
                    fin(tt(S[0:E, :], Sd[0:E, :], bank[0][0:E, 0:MIX], ALU.add), (i, "S", c))
                    yield
            dve.wait_ge(*act_done.after((NT - 1, "y")))
            g4 = lambda x: x.rearrange("p i (h e) -> p i h e", h=H)
            o4 = lambda x: x.unsqueeze(3).broadcast_to([P, NT, H, E])
            if not gdn:
                seq(dve.tensor_reduce(mean, g4(y), AX_X, ALU.add))
                seq(ts_(mean, mean, 1.0 / E, None, ALU.mult))
                seq(tt(g4(y), g4(y), o4(mean), ALU.subtract))
            seq(tt(square, y, y, ALU.mult))
            seq(dve.tensor_reduce(post, g4(square), AX_X, ALU.add))
            fin(ts_(post, post, 1.0 / E, 1e-6 if gdn else 64e-5, ALU.mult, ALU.add), "ss")
            dve.wait_ge(*act_done.after("rs"))
            seq(tt(g4(y), g4(y), o4(post), ALU.mult))
            if gdn:
                w = norm_w.unsqueeze(1).broadcast_to([P, NT * H, E])
                y3 = y.rearrange("p i (h e) -> p (i h) e", h=H)
                seq(tt(y3, y3, w, ALU.mult))
            else:
                each = lambda row: row.unsqueeze(1).broadcast_to([P, NT, MIX])
                seq(tt(y, y, each(gn_gain), ALU.mult))
                seq(tt(y, y, each(gn_bias), ALU.add))
                seq(tt(y, y, bonus, ALU.add))
            fin(tt(y, y, z, ALU.mult), "y")
        return tensor, scalar, vector

    def recurrences(self):
        nc = self.nc
        keep = self.top
        ring = self.w.ring[:, :, :].rearrange("p s c -> p (s c)")
        blocks = [self.hT[:, j, :] for j in range(ND)] + [ring[:, 512 * j:512 * j + 512] for j in range(20)]
        squares = [ring[:, 10240 + 1024 * j:10240 + 1024 * (j + 1)].rearrange("p (i c) -> p i c", c=MIX)
                   for j in range(2)]

        def take(*dims):
            if dims == (H, P) and blocks:
                return blocks.pop().rearrange("p (h t) -> p h t", h=H)
            return self.take(*dims)
        programs = [self.recurrence("gdn", take, self.bank[0:4], squares[0]),
                    self.recurrence("rwkv", take, self.bank[4:8], squares[1])]

        def side_by_side(which, engine):
            running = [p[which](engine) for p in programs]
            while running:
                running = [g for g in running if next(g, "end") != "end"]

        with nc.Block() as block:
            @block.tensor
            def _(pe):
                side_by_side(0, pe)

            @block.scalar
            def _(act):
                side_by_side(1, act)

            @block.vector
            def _(dve):
                side_by_side(2, dve)
        self.top = keep
        self.end_stage("rwkv")

    def split_products(self, name, tiles, inputs, norm=None):
        nc = self.nc
        NB = 8
        PK, PIECES = 4, 4
        hi_done, lo_done, pe_done = self.act_ready, self.dve_ready, self.mm_done
        pieces = []
        for t, tile in enumerate(tiles):
            K = tile.get("K", 0)
            pieces += [(t, k, min(k + PK, K)) for k in range(0, K, PK)] or [(t, 0, 0)]
        ws = [part.rearrange("p b k c -> p (b k) c").rearrange("p (b k) c -> p b k c", k=PK) for part in
              (self.split_w[0][:], self.split_w[1][:])]
        chunks = {}

        def splits(n):
            t, k0, k1 = pieces[n]
            if k1 == k0:
                return []
            w = tiles[t]["weights"](chunks)[:, k0:k1, :]
            return [(w, ws[0][:, n % PIECES, 0:k1 - k0, :], ws[1][:, n % PIECES, 0:k1 - k0, :])] \
                + list(inputs.get(t, ()))[k0:k1]
        w_at, x_at, count = [], [], 0
        for t, k0, k1 in pieces:
            w_at.append(count + (k1 > k0))
            count += (k1 > k0) + len(list(inputs.get(t, ()))[k0:k1])
            x_at.append(count)
        last = [n + 1 == len(pieces) or pieces[n + 1][0] > t for n, (t, _, _) in enumerate(pieces)]
        done_with = [n + 1 for n in range(len(pieces)) if last[n]]

        def emptied(t):
            which = tiles[t]["by"]
            return (self.evac_act if which == "act" else self.evac_dve).at(sum(x["by"] == which
                                                                               for x in tiles[:t + 1]))

        def empty(eng, seq, which, done, t):
            tile = tiles[t]
            if tile["by"] == which:
                eng.wait_ge(*pe_done.at(done_with[t]))
                for other in tile.get("needs", ()):
                    eng.wait_ge(*emptied(other))
                tile["empty"](eng, seq, self.bank[t % NB][:]).then_inc(*done.one())

        with nc.Block() as block:
            @block.scalar
            def _(act):
                seq = self.order(act, self.act_order)
                if norm is not None:
                    norm.scalar(act)
                for n in range(len(pieces) + PIECES):
                    if n < len(pieces):
                        t, k0, k1 = pieces[n]
                        for key, width in tiles[t].get("takes", ()) if k0 == 0 else ():
                            chunks[key] = self.w.take(act, key, width)
                        if n >= PIECES and k1 > k0:
                            act.wait_ge(*pe_done.at(n - PIECES + 1))
                        for j, (src, hi, _) in enumerate(splits(n)):
                            if norm is not None and t == 0 and j:
                                act.wait_ge(*norm.ready(k0 + j - 1))
                            act.activation(hi, src, ACT.Copy).then_inc(*hi_done.one())
                    if n >= PIECES and last[n - PIECES]:
                        empty(act, seq, "act", self.evac_act, pieces[n - PIECES][0])

            @block.vector
            def _(dve):
                seq = self.order(dve, self.dve_order)
                if norm is not None:
                    norm.vector(dve)
                for n in range(len(pieces) + PIECES):
                    if n < len(pieces):
                        if n >= PIECES and pieces[n][2] > pieces[n][1]:
                            dve.wait_ge(*pe_done.at(n - PIECES + 1))
                        for j, (src, hi, lo) in enumerate(splits(n)):
                            dve.wait_ge(*hi_done.at(w_at[n] + j))
                            dve.tensor_tensor(lo, src, hi.bitcast(F32), ALU.subtract).then_inc(*lo_done.one())
                    if n >= PIECES and last[n - PIECES]:
                        empty(dve, seq, "dve", self.evac_dve, pieces[n - PIECES][0])

            @block.tensor
            def _(pe):
                for n, (t, k0, k1) in enumerate(pieces):
                    tile = tiles[t]
                    if k0 == 0 and t >= NB:
                        pe.wait_ge(*emptied(t - NB))
                    out = self.bank[t % NB][:]
                    if k1 > k0:
                        pe.wait_ge(*lo_done.at(w_at[n]))
                    for k in range(k0, k1):
                        if x_at[n] > w_at[n]:
                            pe.wait_ge(*lo_done.at(w_at[n] + 1 + k - k0))
                        for a_, b_ in ((0, 0), (0, 1), (1, 0)):
                            ins = pe.matmul(out, ws[a_][:, n % PIECES, k - k0, :], tile["x"][b_][:, k, :],
                                            start=k + a_ + b_ == 0, stop=last[n] and k == k1 - 1 and a_ == 1)
                    direct = tile["direct"](chunks) if k1 == k0 else []
                    for j, (lhsT, rhs) in enumerate(direct):
                        ins = pe.matmul(out, lhsT, rhs, start=j == 0, stop=j == len(direct) - 1)
                    ins.then_inc(*pe_done.one())
                    for _ in range(tile.get("frees", 0) if last[n] else 0):
                        self.w.release(pe_done)

            @block.sync
            def _(sp):
                self.w.feed(sp)
        self.end_stage(name)

    def by_k(self, src, parts, n=ND):
        return [(src[:, k, :], parts[0][:, k, :], parts[1][:, k, :]) for k in range(n)]

    def gated_sum(self, name, mixT, plan, inputs, norm=None):
        tiles = []
        gates = self.take(2, T)
        assert self.top <= SPLIT_AT
        readers = []
        for c in range(ND):
            for j, (chunk, frees, gate_weights, branch, bias) in enumerate(plan(c)):
                buf = len(readers) % 2
                g, b = len(tiles), len(tiles) + 1
                tiles.append(dict(
                    by="act", weights=gate_weights, K=ND, x=self.split_h, needs=readers[-2:-1],
                    takes=[(chunk, P)] if chunk else [],
                    empty=lambda e, seq, ps, buf=buf, bias=bias: e.activation(
                        gates[:, buf, :], ps, ACT.Sigmoid, bias=bias)))

                def add(e, seq, ps, c=c, j=j, buf=buf):
                    if j == 0:
                        return e.tensor_tensor(mixT[:, c, :], ps, gates[:, buf, :], ALU.mult)
                    seq(e.tensor_tensor(self.scratch[:], ps, gates[:, buf, :], ALU.mult))
                    return e.tensor_tensor(mixT[:, c, :], mixT[:, c, :], self.scratch[:], ALU.add)
                tiles.append(dict(by="dve", needs=[g] + ([b - 2] if j else []), empty=add,
                                  frees=int(frees), **branch))
                readers.append(b)
        self.split_products(name, tiles, inputs, norm)
        self.top -= 2 * T

    def merge(self):
        mixT = self.take(ND, T)
        ysT = self.ysT
        y = self.split_u

        def plan(c):
            branches = []
            for i in range(4):
                key, j = ("merge", c, i // 2), i % 2
                branches.append((key if j == 0 else None, j == 1,
                                 lambda ch, key=key, j=j: ch[key][:, j * ND:(j + 1) * ND, :],
                                 dict(weights=lambda ch, key=key, j=j: ch[key][:, 2 * ND + 2 * j:2 * ND + 2 * j + 2, :],
                                      K=2, x=[part[:, 2 * i:2 * i + 2, :] for part in y]), 0.0))
            return branches
        inputs = {0: self.by_k(self.hT, self.split_h)}
        for i in range(4):
            inputs[2 * i + 1] = self.by_k(ysT, y)[2 * i:2 * i + 2]
        self.gated_sum("merge", mixT, plan, inputs, self.norm)
        self.add_products("out", lambda c: ("out", c), mixT, None)

    def add_products(self, name, key, srcT, scale):
        tiles = []
        for c in range(ND):
            k_ = key(c // 4)

            def add(e, seq, ps, c=c):
                x = self.xT[:, c, :]
                if scale is None:
                    return e.tensor_tensor(x, ps, x, ALU.add)
                return e.scalar_tensor_tensor(x, ps, scale(c), x, ALU.mult, ALU.add)
            tiles.append(dict(by="dve", empty=add, K=ND, x=self.split_u,
                              weights=lambda ch, c=c, k_=k_: ch[k_][:, :, c % 4 * P:c % 4 * P + P]))
            if c % 4 == 0:
                tiles[-1]["takes"] = [(k_, 512)]
            if c % 4 == 3:
                tiles[-1]["frees"] = 1
        self.split_products(name, tiles, {0: self.by_k(srcT, self.split_u)})

    def layer_tables(self):
        nc, a = self.nc, self.a
        R = E // 4 // 2
        self.cos, self.sin = self.take(NT, R), self.take(NT, R)
        self.cond = self.take(ND)
        self.mod = self.take(48)
        self.gain_m, self.gain_f = self.take(ND), self.take(ND)
        self.gain_a, self.gain_b = self.take(2, 2, E), self.take(2, 2, E)
        self.subln = self.take(2, P)
        self.neg_lam = self.take(2)
        self.near = self.take(3 * P)
        self.mid = self.take(7 * P)
        self.far = self.take(4 * P)
        keep = self.top
        pos_i = self.nc_pos
        pos, ang, n = self.take(NT), self.take(NT, R), self.take(NT, R)
        lam = self.take(2, 2, 2, E)
        lsum = self.take(4)
        dist = self.take(7 * P)
        dist_i = self.nc_dist
        landed = self.params_landed
        freq = [float(np.float32(500000.0) ** np.float32(-2.0 * j / (2 * R))) for j in range(R)]
        MAGIC = 1.5 * 2 ** 23
        C1 = 6.28125
        C2 = float(np.float32(2 * math.pi - C1))
        PI = float(np.nextafter(np.float32(math.pi), np.float32(0)))
        LAM = [0.8 - 0.6 * math.exp(-0.3 * l) for l in range(2)]
        self.pool_ready.order_of(["dist", "masks"])
        self.dve_ready.order_of(["angles", "lam_sums", "near", "mods"])
        self.act_ready.order_of(["sin", "lam", "cond"])
        with nc.Block() as block:
            @block.scalar
            def _(act):
                act.dma_start(pos_i[:], a["positions_2"].rearrange("b (i p) -> p (b i)", p=P),
                              allow_slow_non_contiguous=True).then_inc(*landed.dma())
                for l in range(2):
                    for dst, name in ((self.gain_a, "qk_gain_a_2"), (self.gain_b, "qk_gain_b_2")):
                        act.dma_start(dst[:, l], a[name][l:l + 1].rearrange("l a e -> l (a e)")
                                      .broadcast_to([P, 2 * E])).then_inc(*landed.dma())
                    act.dma_start(self.subln[:, l, :], a["subln_g_a_2"][l:l + 1].broadcast_to([P, P]))\
                       .then_inc(*landed.dma())
                    act.dma_start(lam[:, l], a["lambda_a_2"][l:l + 1].rearrange("l a e -> l (a e)")
                                  .broadcast_to([P, 4 * E])).then_inc(*landed.dma())
                act.wait_ge(*self.dve_ready.after("angles"))
                act.activation(self.sin, ang, ACT.Sin).then_inc(*self.act_order.one())
                act.activation(self.cos, n, ACT.Sin).then_inc(*self.act_ready.step("sin"))
                act.wait_ge(*self.dve_ready.after("lam_sums"))
                act.activation(lsum, lsum, ACT.Exp).then_inc(*self.act_ready.step("lam"))
                act.activation(self.cond, self.par[:, PAR["c_2"]:PAR["c_2"] + ND], ACT.Silu)\
                   .then_inc(*self.act_ready.step("cond"))

            @block.gpsimd
            def _(pool):
                pool.iota(dist_i[:], [[-1, 7 * P]], base=3 * P + 7 * P, channel_multiplier=1)\
                    .then_inc(*self.pool_ready.step("dist"))
                pool.wait_ge(*self.dve_ready.after("mods"))
                seq = self.order(pool, self.pool_order)
                for m, first, reach in ((self.near, -P, 64), (self.mid, -3 * P, 256)):
                    w = m.shape[-1]
                    seq(pool.affine_select(out=m, in_=m, compare_op=ALU.is_ge, fill=NEG, base=reach + first,
                                           pattern=[[1, w]], channel_multiplier=-1))
                    seq(pool.affine_select(out=m, in_=m, compare_op=ALU.is_ge, fill=NEG, base=reach - first,
                                           pattern=[[-1, w]], channel_multiplier=1))
                pool.memset(self.scratch[0:1, 0:1], 0.0).then_inc(*self.pool_ready.step("masks"))

            @block.vector
            def _(dve):
                seq = self.order(dve, self.dve_order)
                ts_, stt = dve.tensor_scalar, dve.scalar_tensor_tensor
                dve.wait_ge(*landed.all_of_stage(16 * 9))
                seq(dve.tensor_copy(pos, pos_i[:]))
                for j in range(R):
                    ts_(ang[:, :, j], pos, freq[j], None, ALU.mult).then_inc(*self.dve_order.one())
                dve.wait_ge(*self.dve_order.all())
                seq(ts_(n, ang, 1.0 / (2 * math.pi), MAGIC, ALU.mult, ALU.add))
                seq(ts_(n, n, MAGIC, None, ALU.subtract))
                seq(stt(ang, n, -C1, ang, ALU.mult, ALU.add))
                seq(stt(ang, n, -C2, ang, ALU.mult, ALU.add))
                seq(ts_(ang, ang, PI, -PI, ALU.min, ALU.max))
                seq(stt(n, ang, -1.0, ang, ALU.mult, ALU.max))
                ts_(n, n, -1.0, math.pi / 2, ALU.mult, ALU.add).then_inc(*self.dve_ready.step("angles"))
                for l in range(2):
                    seq(dve.tensor_tensor(lam[:, l, :, 0, :], lam[:, l, :, 0, :], lam[:, l, :, 1, :], ALU.mult))
                    ins = dve.tensor_reduce(lsum[:, 2 * l:2 * l + 2], lam[:, l, :, 0, :], AX_X, ALU.add)
                    if l == 0:
                        seq(ins)
                ins.then_inc(*self.dve_ready.step("lam_sums"))
                dve.wait_ge(*self.act_ready.after("lam"))
                for l in range(2):
                    seq(dve.tensor_tensor(self.neg_lam[:, l:l + 1], lsum[:, 2 * l + 1:2 * l + 2],
                                          lsum[:, 2 * l:2 * l + 1], ALU.subtract))
                    seq(ts_(self.neg_lam[:, l:l + 1], self.neg_lam[:, l:l + 1], -LAM[l], None, ALU.add))
                    seq(ts_(self.gain_a[:, l, 0, :], self.gain_a[:, l, 0, :], E ** -0.5, None, ALU.mult))
                    seq(ts_(self.subln[:, l, :], self.subln[:, l, :], 1.0 - LAM[l], None, ALU.mult))
                seq(dve.memset(self.near, 0.0))
                dve.wait_ge(*self.pool_ready.after("dist"))
                for m, d, w in ((self.mid, 4, 7 * P), (self.far, 16, 4 * P)):
                    bits = self.nc_bits[:, 0:w]
                    seq(ts_(bits, dist_i[:, 0:w], d - 1, None, ALU.bitwise_and))
                    seq(dve.tensor_copy(m, bits))
                    ins = ts_(m, m, 0.5, NEG, ALU.is_ge, ALU.mult)
                    if d == 4:
                        ins.then_inc(*self.dve_ready.step("near"))
                        dve.wait_ge(*self.dve_ready.after("near"))
                ins.then_inc(*self.dve_ready.step("mods"))

            @block.sync
            def _(sp):
                self.w.feed(sp)
        self.top = keep
        self.end_stage("tables")

    def modulation(self, l):
        nc = self.nc
        keep = self.top
        acc, row = self.take(2, 512), self.take(2, 512)
        N = 6 * D // 512
        cols = self.bank[7]
        ON_DVE = 5
        chunk = {}
        with nc.Block() as block:
            @block.vector
            def _(dve):
                seq = self.order(dve, self.dve_order)

                def copy(c):
                    dve.wait_ge(*self.mm_done.at(c + 1))
                    if c >= 2:
                        dve.wait_ge(*self.pe_ready.at(c - 1))
                    dve.tensor_copy(row[0:1, c % 2, :], self.bank[c % 2][0:1, :]).then_inc(*self.evac_dve.one())
                for c in range(N):
                    w = chunk[c] = self.w.take(dve, ("ada", l, c), 512)
                    if c >= 2:
                        dve.wait_ge(*self.mm_done.at(c - 1))
                    seq(dve.tensor_scalar(acc[:, c % 2, :], w[:, 0, :], self.cond[:, 0:1], None, ALU.mult))
                    for k in range(1, ON_DVE):
                        ins = dve.scalar_tensor_tensor(acc[:, c % 2, :], w[:, k, :], self.cond[:, k:k + 1],
                                                       acc[:, c % 2, :], ALU.mult, ALU.add)
                        if k < ON_DVE - 1:
                            seq(ins)
                    ins.then_inc(*self.dve_ready.one())
                    if c:
                        copy(c - 1)
                copy(N - 1)
                dve.wait_ge(*self.pe_ready.at(N))
                b = PAR["ada_b_2"] + 48 * l
                seq(dve.tensor_tensor(self.mod, cols[:, 0:48], self.par[:, b:b + 48], ALU.add))
                for dst, at, name in ((self.gain_m, 8, "norm_mix_g_2"), (self.gain_f, 32, "norm_mlp_g_2")):
                    g = self.par[:, PAR[name] + 8 * l:PAR[name] + 8 * l + 8]
                    seq(dve.scalar_tensor_tensor(dst, self.mod[:, at:at + 8], 1.0, g, ALU.add, ALU.mult))

            @block.tensor
            def _(pe):
                def columns_of(c):
                    pe.wait_ge(*self.evac_dve.at(c + 1))
                    for j in range(4):
                        ins = pe.matmul(cols[:, 4 * c + j:4 * c + j + 1], row[0:1, c % 2, j * P:(j + 1) * P],
                                        self.ones[0:1, 0:1], start=True, stop=True)
                    ins.then_inc(*self.pe_ready.one())
                for c in range(N):
                    pe.wait_ge(*self.dve_ready.at(c + 1))
                    if c >= 2:
                        pe.wait_ge(*self.evac_dve.at(c - 1))
                    bank = self.bank[c % 2][0:1, :]
                    pe.matmul(bank, self.ones[:, 0:1], acc[:, c % 2, :], start=True, stop=False)
                    for k in range(ON_DVE, ND):
                        ins = pe.matmul(bank, self.cond[:, k:k + 1], chunk[c][:, k, :], start=False, stop=k == ND - 1)
                    ins.then_inc(*self.mm_done.one())
                    self.w.release(self.mm_done)
                    if c:
                        columns_of(c - 1)
                columns_of(N - 1)

            @block.sync
            def _(sp):
                self.w.feed(sp)
        self.top = keep
        self.end_stage(f"mod{l}")

    def queries_keys(self, name, chunks, width, gain, norm=None):
        nc = self.nc
        keep = self.top
        G, NC_ = width // E, width // P
        R = E // 4 // 2
        raw, sq = self.take(3, width), self.take(2, width)
        ss = self.take(3, G)
        t1, t2, t3, t4 = (self.take(G, R) for _ in range(4))
        units = [(c, i) for c in range(len(chunks)) for i in range(NT)]
        N = len(units)
        grp = lambda x: x.rearrange("p (g e) -> p g e", e=E)
        pe_done, turned = self.mm_done, self.pe_ready
        squared, summed, rooted, normed, emptied = (self.act_ready, self.dve_ready, self.act_order, self.evac_dve,
                                                    self.evac_act)

        def steps(*stages):
            for step in range(N + max(lag for lag, _ in stages)):
                for lag, run in stages:
                    if 0 <= step - lag < N:
                        run(step - lag, *units[step - lag])

        with nc.Block() as block:
            @block.tensor
            def _(pe):
                w = {}

                def project(n, c, i):
                    if i == 0:
                        w[0] = self.w.take(pe, chunks[c][0], width)
                    if n >= 3:
                        pe.wait_ge(*squared.at(n - 2))
                    for k in range(ND):
                        if norm is not None and n == 0:
                            pe.wait_ge(*norm.ready(k))
                        ins = pe.matmul(self.bank[n % 3][:, 0:width], self.hT[:, k, i * P:(i + 1) * P], w[0][:, k, :],
                                        start=k == 0, stop=k == ND - 1)
                    ins.then_inc(*pe_done.one())
                    if i == NT - 1:
                        self.w.release(pe_done)

                def turn(n, c, i):
                    pe.wait_ge(*normed.at(n + 1))
                    if n >= 2:
                        pe.wait_ge(*emptied.at(n - 1))
                    for j in range(NC_):
                        ins = pe.transpose(self.bank[4 + n % 2][:, j * P:(j + 1) * P],
                                           raw[:, n % 3, j * P:(j + 1) * P], self.ident[:])
                    ins.then_inc(*turned.one())
                steps((0, project), (2, turn))

            @block.scalar
            def _(act):
                def copy(n, c, i):
                    act.wait_ge(*pe_done.at(n + 1))
                    if n >= 3:
                        act.wait_ge(*turned.at(n - 2))
                    if n >= 2:
                        act.wait_ge(*summed.at(n - 1))
                    act.activation(raw[:, n % 3, :], self.bank[n % 3][:, 0:width], ACT.Copy)\
                       .then_inc(*self.x_landed.one())
                    act.activation(sq[:, n % 2, :], self.bank[n % 3][:, 0:width], ACT.Square)\
                       .then_inc(*squared.one())

                def root(n, c, i):
                    act.wait_ge(*summed.at(n + 1))
                    act.activation(ss[:, n % 3, :], ss[:, n % 3, :], ACT.Ln).then_inc(*self.x_landed.one())
                    act.wait_ge(*self.x_landed.all())
                    act.activation(ss[:, n % 3, :], ss[:, n % 3, :], ACT.Exp, scale=-0.5).then_inc(*rooted.one())

                def empty(n, c, i):
                    act.wait_ge(*turned.at(n + 1))
                    _, _, dst, f = chunks[c]
                    out = dst[:, f:f + NC_, i * P:(i + 1) * P]
                    act.activation(out, self.bank[4 + n % 2][:, 0:width].rearrange("p (j t) -> p j t", j=NC_),
                                   ACT.Copy).then_inc(*emptied.one())
                if norm is not None:
                    norm.scalar(act)
                steps((0, copy), (1, root), (3, empty))

            @block.vector
            def _(dve):
                seq = self.order(dve, self.dve_order)
                tt = dve.tensor_tensor

                def sums(n, c, i):
                    dve.wait_ge(*squared.at(n + 1))
                    seq(dve.tensor_reduce(ss[:, n % 3, :], grp(sq[:, n % 2, :]), AX_X, ALU.add))
                    dve.tensor_scalar(ss[:, n % 3, :], ss[:, n % 3, :], 1.0 / E, EPS, ALU.mult, ALU.add)\
                       .then_inc(*summed.one())

                def scale(n, c, i):
                    x = grp(raw[:, n % 3, :])
                    dve.wait_ge(*rooted.at(n + 1))
                    seq(tt(x, x, ss[:, n % 3, :].unsqueeze(2).broadcast_to([P, G, E]), ALU.mult))
                    seq(tt(x, x, gain[:, chunks[c][1], :].unsqueeze(1).broadcast_to([P, G, E]), ALU.mult))
                    cos = self.cos[:, i, :].unsqueeze(1).broadcast_to([P, G, R])
                    sin = self.sin[:, i, :].unsqueeze(1).broadcast_to([P, G, R])
                    x1, x2 = x[:, :, 0:R], x[:, :, R:2 * R]
                    for t, u, v in ((t1, x1, cos), (t2, x2, sin), (t3, x2, cos), (t4, x1, sin)):
                        tt(t, u, v, ALU.mult).then_inc(*self.dve_order.one())
                    dve.wait_ge(*self.dve_order.all())
                    tt(x1, t1, t2, ALU.subtract).then_inc(*self.dve_order.one())
                    dve.wait_ge(*self.dve_order.all())
                    tt(x2, t3, t4, ALU.add).then_inc(*normed.one())
                if norm is not None:
                    norm.vector(dve)
                steps((0, sums), (1, scale))

            @block.sync
            def _(sp):
                self.w.feed(sp)
        self.top = keep
        self.end_stage(name)

    def values(self, name, chunks, width, dst):
        tiles = []
        for c, key in enumerate(chunks):
            for i in range(NT):
                def copy(e, seq, ps, c=c, i=i):
                    out = dst[:, i, c * width:(c + 1) * width]
                    return e.activation(out, ps, ACT.Copy) if i % 2 else e.tensor_copy(out, ps)
                tiles.append(dict(by="act" if i % 2 else "dve", shape=(P, width), empty=copy,
                                  pairs=lambda ch, key=key, i=i: [
                                      (self.hT[:, k, i * P:(i + 1) * P], ch[key][:, k, :]) for k in range(ND)]))
            tiles[-NT]["takes"] = [(key, width)]
            tiles[-1]["frees"] = 1
        self.products(name, tiles)

    def differential(self, l):
        oaT = self.oaT
        keep = self.top
        qT, kT, v, o = self.take(ND, T), self.take(ND, T), self.take(NT, D), self.take(NT, D)
        self.queries_keys(f"qk_a{l}", [(("a", l, 0), 0, qT, 0), (("a", l, 1), 0, qT, 4), (("a", l, 2), 1, kT, 0),
                                       (("a", l, 3), 1, kT, 4)], 512, self.gain_a[:, l], self.norm)
        self.values(f"v_a{l}", [("a", l, 4), ("a", l, 5)], 512, v)
        units, groups = [], []
        coef = self.take(4)
        inv = self.take(4)
        for i in range(NT):
            for half in range(2):
                g = len(groups)
                for h in range(4 * half, 4 * half + 4):
                    parts = [dict(scores=(qT[c * E:(c + 1) * E, h, i * P:(i + 1) * P], kT[c * E:(c + 1) * E, h, :]),
                                  n=T) for c in range(2)]

                    def mix(dve, seq, q, rows):
                        l0, l1 = self.row_sum[:, q:q + 1], self.row_sum[:, q + 1:q + 2]
                        by = coef[:, q // 2 % 4:q // 2 % 4 + 1]
                        seq(dve.reciprocal(by, l1))
                        seq(dve.scalar_tensor_tensor(by, l0, self.neg_lam[:, l:l + 1], by, ALU.mult, ALU.mult))
                        return dve.scalar_tensor_tensor(rows[0], rows[1], by, rows[0], ALU.mult, ALU.add)
                    units.append(dict(parts=parts, mix=mix, group=g, cols=((h - 4 * half) * P, (h - 4 * half + 1) * P),
                                      values=[v[:, b, h * P:(h + 1) * P] for b in range(NT)]))

                def take_out(dve, seq, bank, i=i, half=half, g=g):
                    sums = self.row_sum[:, 8 * g:8 * g + 8].rearrange("p (h c) -> p h c", c=2)[:, :, 0]
                    seq(dve.reciprocal(inv, sums))
                    return dve.tensor_tensor(
                        o[:, i, half * 512:(half + 1) * 512].rearrange("p (h e) -> p h e", h=4),
                        bank[:].rearrange("p (h e) -> p h e", h=4), inv.unsqueeze(2).broadcast_to([P, 4, P]), ALU.mult)
                groups.append(take_out)
        self.attention(f"diff{l}", units, groups, parts=2)
        nc = self.nc
        sq = self.take(2, D)
        ms = self.take(NT, 8)
        with nc.Block() as block:
            @block.scalar
            def _(act):
                seq = self.order(act, self.act_order)
                for i in range(NT):
                    if i >= 2:
                        act.wait_ge(*self.dve_ready.at(i - 1))
                    act.activation(sq[:, i % 2, :], o[:, i, :], ACT.Square).then_inc(*self.act_ready.one())
                for i in range(NT):
                    act.wait_ge(*self.dve_ready.at(i + 1))
                act.activation(ms, ms, ACT.Ln).then_inc(*self.act_order.one())
                act.wait_ge(*self.act_order.all())
                act.activation(ms, ms, ACT.Exp, scale=-0.5).then_inc(*self.act_ready.one())
                for h in range(0, ND, 2):
                    act.wait_ge(*self.mm_done.at(h + 1))
                    act.activation(oaT[:, h, :], self.bank[h][:], ACT.Copy).then_inc(*self.evac_act.one())

            @block.vector
            def _(dve):
                seq = self.order(dve, self.dve_order)
                for i in range(NT):
                    dve.wait_ge(*self.act_ready.at(i + 1))
                    seq(dve.tensor_reduce(ms[:, i, :], sq[:, i % 2, :].rearrange("p (h e) -> p h e", h=8), AX_X,
                                          ALU.add))
                    dve.tensor_scalar(ms[:, i, :], ms[:, i, :], 1.0 / P, EPS, ALU.mult, ALU.add)\
                       .then_inc(*self.dve_ready.one())
                dve.wait_ge(*self.act_ready.at(NT + 1))
                for i in range(NT):
                    x = o[:, i, :].rearrange("p (h e) -> p h e", h=8)
                    seq(dve.tensor_tensor(x, x, ms[:, i, :].unsqueeze(2).broadcast_to([P, 8, P]), ALU.mult))
                    dve.tensor_tensor(x, x, self.subln[:, l, :].unsqueeze(1).broadcast_to([P, 8, P]), ALU.mult)\
                       .then_inc(*self.dve_ready.one())
                for h in range(1, ND, 2):
                    dve.wait_ge(*self.mm_done.at(h + 1))
                    dve.tensor_copy(oaT[:, h, :], self.bank[h][:]).then_inc(*self.evac_dve.one())

            @block.tensor
            def _(pe):
                for i in range(NT):
                    pe.wait_ge(*self.dve_ready.at(NT + i + 1))
                    for h in range(ND):
                        ins = pe.transpose(self.bank[h][:, i * P:(i + 1) * P], o[:, i, h * P:(h + 1) * P],
                                           self.ident[:])
                        if i == NT - 1:
                            ins.then_inc(*self.mm_done.one())

            @block.sync
            def _(sp):
                self.w.feed(sp)
        self.top = keep
        self.end_stage(f"oa{l}")

    def dilated(self, l):
        obT = self.obT
        keep = self.top
        qT, kT, v, o = self.take(6, T), self.take(6, T), self.take(NT, 768), self.take(NT, MIX)
        self.queries_keys(f"qk_b{l}", [(("b", l, 0), 0, qT, 0), (("b", l, 1), 0, qT, 3), (("b", l, 2), 1, kT, 0),
                                       (("b", l, 3), 1, kT, 3)], 384, self.gain_b[:, l])
        self.values(f"v_b{l}", [("b", l, 4), ("b", l, 5)], 384, v)
        units, groups = [], []
        inv = self.take(4)
        for i in range(NT):
            windows = [(max(0, i - 1), min(NT, i + 2), self.near, i - 1),
                       (max(0, i - 2) if i == 3 else 0, NT if i else 3, self.mid, i - 3),
                       (0, NT, self.far, 0)]
            for h in range(H):
                for w, (b0, b1, table, origin) in enumerate(windows):
                    f, lo = (w * H + h) // 2, (w * H + h) % 2 * E
                    part = dict(scores=(qT[lo:lo + E, f, i * P:(i + 1) * P], kT[lo:lo + E, f, b0 * P:b1 * P]),
                                n=(b1 - b0) * P, table=table[:, (b0 - origin) * P:(b1 - origin) * P])
                    units.append(dict(parts=[part], group=i, cols=(h * E, (h + 1) * E),
                                      values=[v[:, b, (w * H + h) * E:(w * H + h + 1) * E] for b in range(b0, b1)]))

            def take_out(dve, seq, bank, i=i):
                sums = self.row_sum[:, 12 * i:12 * i + 12].rearrange("p (h w) -> p h w", w=3)
                seq(dve.tensor_reduce(inv, sums, AX_X, ALU.add))
                seq(dve.reciprocal(inv, inv))
                return dve.tensor_tensor(o[:, i, :].rearrange("p (h e) -> p h e", h=H),
                                         bank[:, 0:MIX].rearrange("p (h e) -> p h e", h=H),
                                         inv.unsqueeze(2).broadcast_to([P, H, E]), ALU.mult)
            groups.append(take_out)
        self.attention(f"dil{l}", units, groups, joint=3)
        nc = self.nc
        with nc.Block() as block:
            @block.tensor
            def _(pe):
                for c in range(2):
                    for i in range(NT):
                        ins = pe.transpose(self.bank[c][:, i * P:(i + 1) * P], o[:, i, c * P:(c + 1) * P],
                                           self.ident[:])
                    ins.then_inc(*self.mm_done.one())

            @block.vector
            def _(dve):
                for c in range(2):
                    dve.wait_ge(*self.mm_done.at(c + 1))
                    dve.tensor_copy(obT[:, c, :], self.bank[c][:]).then_inc(*self.evac_dve.one())

            @block.sync
            def _(sp):
                self.w.feed(sp)
        self.top = keep
        self.end_stage(f"ob{l}")

    def layer(self, l):
        mod = lambda part: (lambda k: self.mod[:, 8 * part + k:8 * part + k + 1])
        keep = self.top
        self.modulation(l)
        self.rms(f"rms_mix{l}", lambda k: self.gain_m[:, k:k + 1], mod(0))
        self.oaT, self.obT = self.take(ND, T), self.take(2, T)
        self.differential(l)
        self.dilated(l)
        mixT = self.oaT

        def plan(c):
            key = ("branches", l, c)
            bias = [self.par[:, PAR["gate_bias_2"] + 16 * l + 8 * i + c:][:, 0:1] for i in range(2)]
            gate = lambda i: (lambda ch: ch[key][:, i * ND:(i + 1) * ND, :])
            a_branch = dict(weights=lambda ch: ch[key][:, 2 * ND:3 * ND, :], K=ND, x=self.split_u)
            b_branch = dict(direct=lambda ch: [(ch[key][:, 3 * ND + k, :], self.obT[:, k, :]) for k in range(2)])
            return [(key, False, gate(0), a_branch, bias[0]), (None, True, gate(1), b_branch, bias[1])]
        self.gated_sum(f"gates{l}", mixT, plan, {0: self.by_k(self.hT, self.split_h),
                                                 1: self.by_k(self.oaT, self.split_u)})
        self.add_products(f"out{l}", lambda c: ("out", l, c), mixT, mod(2))
        self.top = keep
        self.rms(f"rms_mlp{l}", lambda k: self.gain_f[:, k:k + 1], mod(3))
        self.mlp(l, mod(5))
        self.top = keep

    def mlp(self, l, gate):
        nc = self.nc
        relu = self.take(2, T)
        square = self.take(2, T)
        assert self.top <= SPLIT_AT
        hs, us, ws = self.split_h, self.split_u, self.split_w
        hT = self.hT
        tiles = [(r, way, c) for r in range(4) for way in ("up", "down") for c in range(ND)]
        N = len(tiles)
        NB = 8
        src = {}
        hi_done, lo_done = self.act_ready, self.dve_ready
        pe_done, relu_done, out = self.mm_done, self.evac_act, self.evac_dve
        relus = [sum(way == "up" for _, way, _ in tiles[:t + 1]) for t in range(N)]
        with nc.Block() as block:
            @block.scalar
            def _(act):
                def split(t):
                    r, way, c = tiles[t]
                    if c % 4 == 0:
                        key = ("up", l, 2 * r + c // 4) if way == "up" else ("down", l, r, c // 4)
                        src[t // 4] = self.w.take(act, key, 512)
                    if t >= 2:
                        act.wait_ge(*pe_done.at(t - 1))
                    act.activation(ws[0][:, t % 2], src[t // 4][:, :, c % 4 * P:c % 4 * P + P], ACT.Copy)\
                       .then_inc(*hi_done.one())
                self.norm.scalar(act)
                split(0)
                for k in range(ND):
                    act.wait_ge(*self.norm.ready(k))
                    act.activation(hs[0][:, k, :], hT[:, k, :], ACT.Copy).then_inc(*hi_done.one())
                for t, (r, way, c) in enumerate(tiles):
                    if t + 1 < N:
                        split(t + 1)
                    if way == "up":
                        act.wait_ge(*pe_done.at(t + 1))
                        if relus[t] > 2:
                            act.wait_ge(*out.at(tiles.index((r, way, c)) - 1 if c >= 2 else tiles.index(
                                (r - 1, "up", ND - 2 + c)) + 1))
                        act.activation(relu[:, c % 2, :], self.bank[t % NB][:], ACT.Relu).then_inc(*relu_done.one())

            @block.vector
            def _(dve):
                seq = self.order(dve, self.dve_order)
                def split(t):
                    c = tiles[t][2]
                    dve.wait_ge(*hi_done.at(ND + t + 1 if t else 1))
                    if t >= 2:
                        dve.wait_ge(*pe_done.at(t - 1))
                    dve.tensor_tensor(ws[1][:, t % 2], src[t // 4][:, :, c % 4 * P:c % 4 * P + P],
                                      ws[0][:, t % 2].bitcast(F32), ALU.subtract).then_inc(*lo_done.one())
                    if c % 4 == 3:
                        self.w.release(lo_done)
                self.norm.vector(dve)
                split(0)
                for k in range(ND):
                    dve.wait_ge(*hi_done.at(k + 2))
                    dve.tensor_tensor(hs[1][:, k, :], hT[:, k, :], hs[0][:, k, :].bitcast(F32), ALU.subtract)\
                       .then_inc(*lo_done.one())
                for t, (r, way, c) in enumerate(tiles):
                    if t + 1 < N:
                        split(t + 1)
                    if way == "up":
                        dve.wait_ge(*relu_done.at(relus[t]))
                        s = square[:, c % 2, :]
                        seq(dve.tensor_tensor(s, relu[:, c % 2, :], relu[:, c % 2, :], ALU.mult))
                        seq(dve.tensor_copy(us[0][:, c, :], s))
                        dve.tensor_tensor(us[1][:, c, :], s, us[0][:, c, :].bitcast(F32), ALU.subtract)\
                           .then_inc(*out.one())
                    else:
                        dve.wait_ge(*pe_done.at(t + 1))
                        if r:
                            dve.wait_ge(*out.at(t - 2 * ND + 1))
                        dve.scalar_tensor_tensor(self.xT[:, c, :], self.bank[t % NB][:], gate(c), self.xT[:, c, :],
                                                 ALU.mult, ALU.add).then_inc(*out.one())

            @block.tensor
            def _(pe):
                for t, (r, way, c) in enumerate(tiles):
                    x = hs if way == "up" else us
                    if t >= NB:
                        pe.wait_ge(*out.at(t - NB + 1))
                    pe.wait_ge(*lo_done.at(ND + t + 1 if t else 1))
                    for k in range(ND):
                        if t == 0:
                            pe.wait_ge(*lo_done.at(k + 2))
                        elif way == "down" and c == 0:
                            pe.wait_ge(*out.at(t - ND + k + 1))
                        for a_, b_ in ((0, 0), (0, 1), (1, 0)):
                            ins = pe.matmul(self.bank[t % NB][:], ws[a_][:, t % 2, k, :], x[b_][:, k, :],
                                            start=k + a_ + b_ == 0, stop=k == ND - 1 and a_ == 1)
                    ins.then_inc(*pe_done.one())

            @block.sync
            def _(sp):
                self.w.feed(sp)
        self.end_stage(f"down{l}")

    def store(self):
        nc = self.nc
        y = self.take(NT, D)
        with nc.Block() as block:
            @block.tensor
            def _(pe):
                for n in range(8):
                    i, half = n // 2, n % 2
                    for k in range(4):
                        ins = pe.transpose(self.bank[n][:, k * P:(k + 1) * P],
                                           self.xT[:, 4 * half + k, i * P:(i + 1) * P], self.ident[:])
                    ins.then_inc(*self.mm_done.one())

            @block.vector
            def _(dve):
                for n in range(8):
                    dve.wait_ge(*self.mm_done.at(n + 1))
                    dve.tensor_copy(y[:, n // 2, n % 2 * 512:n % 2 * 512 + 512], self.bank[n][:])\
                       .then_inc(*self.evac_dve.one())

            @block.sync
            def _(sp):
                for i in range(NT):
                    sp.wait_ge(*self.evac_dve.at(2 * i + 2))
                    sp.dma_start(self.out[0, i * P:(i + 1) * P, :], y[:, i, :]).then_inc(*self.stored.dma())
                sp.wait_ge(*self.stored.all())
        self.end_stage("store")

    def build(self):
        self.load()
        col = lambda name: (lambda k: self.par[:, PAR[name] + k:PAR[name] + k + 1])
        self.rms("rms1", col("norm_gain"))
        self.first_projection()
        self.sparse_attention()
        self.spatial_gating()
        self.mixer_preparation()
        self.recurrences()
        self.w.limit = None
        self.rms("rms1_again", col("norm_gain"))
        self.top = self.after_ys
        self.merge()
        self.top = 0
        self.rms("final", col("final_gain"), dst=self.xT)
        self.layer_tables()
        for l in range(2):
            self.layer(l)
        self.store()


def hybrid_then_conditioned_layers(nc, arrays, out):
    k = Kernel(nc, arrays, out)
    try:
        k.build()
    except Stop:
        pass
    return k


_INS = ['x', 'norm_gain', 'w_in', 'gdn_conv', 'gdn_a_log', 'gdn_dt_bias', 'gdn_norm', 'sg_ln_gain', 'sg_ln_bias',
        'sg_w_s', 'sg_b_s', 'rw_mu', 'rw_w_up', 'rw_w0', 'rw_a_up', 'rw_a0', 'rw_k_k', 'rw_k_a', 'rw_r_k',
        'rw_gn_gain', 'rw_gn_bias', 'nsa_cmp_pos', 'nsa_cmp_w1', 'nsa_cmp_w2', 'w_branch', 'w_out', 'final_gain',
        'c_2', 'positions_2', 'ada_w_2', 'ada_b_2', 'norm_mix_g_2', 'norm_mlp_g_2', 'w_in_2', 'qk_gain_a_2',
        'lambda_a_2', 'subln_g_a_2', 'qk_gain_b_2', 'w_branch_a_2', 'w_branch_b_2', 'gate_bias_2', 'w_out_2',
        'w_mlp_up_2', 'w_mlp_down_2']


def kernel(**inputs):
    import concourse.bacc as bacc
    from concourse.bass_utils import run_bass_kernel_spmd

    nc = bacc.Bacc("TRN2", target_bir_lowering=False, num_devices=1)
    arrays, views = {}, {}
    for name in _INS:
        v = np.ascontiguousarray(inputs[name])
        arrays[f"in_{name}"] = v
        views[name] = nc.dram_tensor(f"in_{name}", v.shape, mybir.dt.from_np(v.dtype), kind="ExternalInput").ap()
    out = nc.dram_tensor("out_0", (1, T, D), F32, kind="ExternalOutput").ap()
    hybrid_then_conditioned_layers(nc, views, out)
    r = run_bass_kernel_spmd(nc, [arrays], core_ids=[0])
    return r.results[0]["out_0"]
```
